# Optimizing a Trainium2 kernel written in Bass

```python
import jax
import jax.numpy as jnp
from jax import lax
import numpy as np

D_MODEL = 1024
BATCH = 1
SEQ = 256
DEPTH = 2

GRID_W = 64
CTX_LEN = 256
N_MIXERS = 2
EPS = 1e-6
N_MOD = 6

M_HEADS = 8
M_DK = 64
M_DV = 128
M_CHUNK = 64
M_CONV = 3
M_F_BIAS = 3.5

H_HEADS = 8
H_DK = 128
H_DV = 128
H_CHUNK = 32

FFN_HIDDEN = 2816
N_EXPERTS = 8
TOP_K = 2
EXPERT_HIDDEN = 2816

F32 = jnp.float32

kernel_name = 'hybrid_mlstm_hgrn2_moe_dit'

def rmsnorm(x, g):
    xf = x.astype(F32)
    y = xf * lax.rsqrt(jnp.mean(xf * xf, axis=-1, keepdims=True) + EPS)
    return (y * g.astype(F32)).astype(x.dtype)

def short_conv(x, w):
    K, C = w.shape
    left = (K - 1) // 2
    return lax.conv_general_dilated(x, w[:, None, :].astype(x.dtype), window_strides=(1,),
                                    padding=[(left, K - 1 - left)],
                                    dimension_numbers=('NWC', 'WIO', 'NWC'),
                                    feature_group_count=C)

def to_heads(a, n_heads):
    B, T, C = a.shape
    return a.reshape(B, T, n_heads, C // n_heads).transpose(0, 2, 1, 3).astype(F32)

def to_chunks(a, L):
    B, H, T = a.shape[:3]
    return jnp.moveaxis(a.reshape(B, H, T // L, L, *a.shape[3:]), 2, 0)

def from_chunks(a):
    N, B, H, L = a.shape[:4]
    return jnp.moveaxis(a, 0, 2).reshape(B, H, N * L, *a.shape[4:])

def to_column_major(a, rows):
    B, T, C = a.shape
    return a.reshape(B, rows, GRID_W, C).transpose(0, 2, 1, 3).reshape(B, T, C)

def from_column_major(a, rows):
    B, T, C = a.shape
    return a.reshape(B, GRID_W, rows, C).transpose(0, 2, 1, 3).reshape(B, T, C)

def mlstm_scan(q, k, v, ig, lf, state):
    L = M_CHUNK
    causal = jnp.tril(jnp.ones((L, L), dtype=bool))

    def step(carry, xs):
        C, n, m = carry
        qc, kc, vc, ic, fc = xs
        b = jnp.cumsum(fc, axis=-1)
        d = jnp.where(causal, b[..., :, None] - b[..., None, :] + ic[..., None, :], -jnp.inf)
        inter = b + m[..., None]
        m_t = jnp.maximum(inter, jnp.max(d, axis=-1))
        s = jnp.einsum('bhtd,bhsd->bhts', qc, kc) * jnp.exp(d - m_t[..., None])
        w_inter = jnp.exp(inter - m_t)
        num = jnp.einsum('bhts,bhsv->bhtv', s, vc) + w_inter[..., None] * jnp.einsum('bhtd,bhdv->bhtv', qc, C)
        den = jnp.sum(s, axis=-1) + w_inter * jnp.einsum('bhtd,bhd->bht', qc, n)
        h = num / jnp.maximum(jnp.abs(den), jnp.exp(-m_t))[..., None]
        b_last = b[..., -1]
        g = b_last[..., None] - b + ic
        m_new = jnp.maximum(b_last + m, jnp.max(g, axis=-1))
        w_k = jnp.exp(g - m_new[..., None])
        decay = jnp.exp(b_last + m - m_new)
        C = decay[..., None, None] * C + jnp.einsum('bhs,bhsd,bhsv->bhdv', w_k, kc, vc)
        n = decay[..., None] * n + jnp.einsum('bhs,bhsd->bhd', w_k, kc)
        return (C, n, m_new), h

    state, h = lax.scan(step, state, tuple(to_chunks(a, L) for a in (q, k, v, ig, lf)))
    return from_chunks(h), state

def hgrn2_scan(q, k, v, lf, S):
    L = H_CHUNK
    causal = jnp.tril(jnp.ones((L, L), dtype=bool))[:, :, None]

    def step(S, xs):
        qc, kc, vc, fc = xs
        a = jnp.cumsum(fc, axis=-2)
        decay = jnp.exp(jnp.where(causal, a[..., :, None, :] - a[..., None, :, :], -jnp.inf))
        s = jnp.einsum('bhtd,bhsd,bhtsd->bhts', qc, kc, decay)
        o = jnp.einsum('bhts,bhsv->bhtv', s, vc) + jnp.einsum('bhtd,bhdv->bhtv', qc * jnp.exp(a), S)
        a_last = a[..., -1:, :]
        S = jnp.exp(a_last[..., 0, :])[..., None] * S + jnp.einsum('bhsd,bhsv->bhdv', kc * jnp.exp(a_last - a), vc)
        return S, o

    S, o = lax.scan(step, S, tuple(to_chunks(a, L) for a in (q, k, v, lf)))
    return from_chunks(o), S

def _flip_t(a):
    return jnp.flip(a, axis=2)

def bidirectional_scan(scan_fn, ctx_fwd, ctx_bwd, lat_fwd, lat_bwd, state0):
    hc_f, st_f = scan_fn(*ctx_fwd, state0)
    hc_b, st_b = scan_fn(*[_flip_t(a) for a in ctx_bwd], state0)
    hl_f, _ = scan_fn(*lat_fwd, st_f)
    hl_b, _ = scan_fn(*[_flip_t(a) for a in lat_bwd], st_b)
    return hc_f + _flip_t(hc_b), hl_f + _flip_t(hl_b)

def head_out(h, gate, g_head, w_out, dtype):
    B, H, T, dv = h.shape
    h = h.transpose(0, 2, 1, 3)
    h = h * lax.rsqrt(jnp.mean(h * h, axis=-1, keepdims=True) + EPS)
    h = h.reshape(B, T, H * dv) * g_head.astype(F32) * gate
    return h.astype(dtype) @ w_out

def mlstm_mixer(u_ctx, u_lat, w_in, b_gate, w_conv, g_head, w_out, with_ctx_out):
    qk_w = 2 * M_HEADS * M_DK
    v_w = M_HEADS * M_DV

    def streams(u):
        B, T, _ = u.shape
        qk, v, o, gates = jnp.split(u @ w_in, [qk_w, qk_w + v_w, qk_w + 2 * v_w], axis=-1)
        qk = jax.nn.silu(short_conv(qk, w_conv))
        q, k = jnp.split(qk, 2, axis=-1)
        q = to_heads(q, M_HEADS)
        k = to_heads(k, M_HEADS) * (M_DK ** -0.5)
        v = to_heads(v, M_HEADS)
        g = (gates + b_gate.reshape(-1)).astype(F32).reshape(B, T, 4, M_HEADS).transpose(2, 0, 3, 1)
        fwd = (q, k, v, g[0], jax.nn.log_sigmoid(g[1]))
        bwd = (q, k, v, g[2], jax.nn.log_sigmoid(g[3]))
        return fwd, bwd, jax.nn.sigmoid(o.astype(F32))

    c_fwd, c_bwd, c_gate = streams(u_ctx)
    l_fwd, l_bwd, l_gate = streams(u_lat)
    B = u_lat.shape[0]
    state0 = (jnp.zeros((B, M_HEADS, M_DK, M_DV), F32),
              jnp.zeros((B, M_HEADS, M_DK), F32),
              jnp.zeros((B, M_HEADS), F32))
    h_ctx, h_lat = bidirectional_scan(mlstm_scan, c_fwd, c_bwd, l_fwd, l_bwd, state0)
    y_lat = head_out(h_lat, l_gate, g_head, w_out, u_lat.dtype)
    y_ctx = head_out(h_ctx, c_gate, g_head, w_out, u_ctx.dtype) if with_ctx_out else None
    return y_ctx, y_lat

def hgrn2_mixer(u_ctx, u_lat, w_in, b_f, lb, g_head, w_out, rows, with_ctx_out):
    kw = H_HEADS * H_DK
    vw = H_HEADS * H_DV

    def streams(u):
        q, v, f_f, f_b, g = jnp.split(u @ w_in, [kw, kw + vw, 2 * kw + vw, 3 * kw + vw], axis=-1)

        def direction(f_pre, bias, lbd):
            f = lbd + (1.0 - lbd) * jax.nn.sigmoid(f_pre.astype(F32) + bias.astype(F32))
            return to_heads(1.0 - f, H_HEADS), to_heads(jnp.log(f), H_HEADS)

        k_f, lf_f = direction(f_f, b_f[0], lb[0])
        k_b, lf_b = direction(f_b, b_f[1], lb[1])
        q = to_heads(q, H_HEADS)
        v = to_heads(v, H_HEADS)
        return (q, k_f, v, lf_f), (q, k_b, v, lf_b), jax.nn.sigmoid(g.astype(F32))

    c_fwd, c_bwd, c_gate = streams(u_ctx)
    l_fwd, l_bwd, l_gate = streams(to_column_major(u_lat, rows))
    B = u_lat.shape[0]
    state0 = jnp.zeros((B, H_HEADS, H_DK, H_DV), F32)
    h_ctx, h_lat = bidirectional_scan(hgrn2_scan, c_fwd, c_bwd, l_fwd, l_bwd, state0)
    y_lat = from_column_major(head_out(h_lat, l_gate, g_head, w_out, u_lat.dtype), rows)
    y_ctx = head_out(h_ctx, c_gate, g_head, w_out, u_ctx.dtype) if with_ctx_out else None
    return y_ctx, y_lat

def swiglu(u, w_gu, w_down):
    g, up = jnp.split(u @ w_gu, 2, axis=-1)
    return (jax.nn.silu(g) * up) @ w_down

def moe_swiglu(u, w_router, b_router, w_gu, w_down):
    logits = (u @ w_router).astype(F32) + b_router.astype(F32)
    top_val, top_idx = lax.top_k(logits, TOP_K)
    weights = jax.nn.softmax(top_val, axis=-1)
    combine = jnp.einsum('...k,...ke->...e', weights, jax.nn.one_hot(top_idx, N_EXPERTS, dtype=F32))
    out = jnp.zeros(u.shape[:-1] + (w_down.shape[-1],), F32)
    for e in range(N_EXPERTS):
        out = out + combine[..., e:e + 1] * swiglu(u, w_gu[e], w_down[e]).astype(F32)
    return out.astype(u.dtype)

def setup_inputs(seed: int = 0) -> dict:
    key = jax.random.key(seed)
    keys = jax.random.split(key, 24)
    D = D_MODEL
    n_even = (DEPTH + 1) // 2
    n_odd = DEPTH // 2
    m_in = 2 * M_HEADS * M_DK + 2 * M_HEADS * M_DV + 4 * M_HEADS
    h_in = 3 * H_HEADS * H_DK + 2 * H_HEADS * H_DV

    def nrm(k, shape, scale):
        return jax.random.normal(k, shape, jnp.float32) * scale

    gate_offset = jnp.tile(jnp.array([0.0, M_F_BIAS, 0.0, M_F_BIAS], jnp.float32)[:, None], (1, M_HEADS))
    return {
        'x': nrm(keys[0], (BATCH, SEQ, D), 1.0),
        'c': nrm(keys[1], (BATCH, D), 1.0),
        'ctx': nrm(keys[2], (BATCH, CTX_LEN, D), 1.0),
        'c_ctx': nrm(keys[3], (D,), 1.0),
        'mod_w': nrm(keys[4], (DEPTH, D, N_MOD * D), 0.5 * D ** -0.5),
        'mod_b': nrm(keys[5], (DEPTH, N_MOD * D), 0.02),
        'norm_g': 1.0 + nrm(keys[6], (DEPTH, 4, D), 0.1),
        'm_w_in': nrm(keys[7], (n_even, D, m_in), D ** -0.5),
        'm_b_gate': gate_offset + nrm(keys[8], (n_even, 4, M_HEADS), 0.5),
        'm_w_conv': nrm(keys[9], (n_even, M_CONV, 2 * M_HEADS * M_DK), M_CONV ** -0.5),
        'm_g_head': 1.0 + nrm(keys[10], (n_even, M_HEADS * M_DV), 0.1),
        'm_w_out': nrm(keys[11], (n_even, M_HEADS * M_DV, D), (M_HEADS * M_DV) ** -0.5),
        'h_w_in': nrm(keys[12], (n_odd, D, h_in), D ** -0.5),
        'h_b_f': nrm(keys[13], (n_odd, 2, H_HEADS * H_DK), 0.1),
        'h_lb_raw': nrm(keys[14], (n_odd, 2, H_HEADS * H_DK), 1.0),
        'h_g_head': 1.0 + nrm(keys[15], (n_odd, H_HEADS * H_DV), 0.1),
        'h_w_out': nrm(keys[16], (n_odd, H_HEADS * H_DV, D), (H_HEADS * H_DV) ** -0.5),
        'f_w_gu': nrm(keys[17], (n_even, D, 2 * FFN_HIDDEN), D ** -0.5),
        'f_w_down': nrm(keys[18], (n_even, FFN_HIDDEN, D), FFN_HIDDEN ** -0.5),
        'e_w_router': nrm(keys[19], (n_odd, D, N_EXPERTS), D ** -0.5),
        'e_b_router': nrm(keys[20], (n_odd, N_EXPERTS), 0.01),
        'e_w_gu': nrm(keys[21], (n_odd, N_EXPERTS, D, 2 * EXPERT_HIDDEN), D ** -0.5),
        'e_w_down': nrm(keys[22], (n_odd, N_EXPERTS, EXPERT_HIDDEN, D), EXPERT_HIDDEN ** -0.5),
    }

def reference(x, c, ctx, c_ctx, mod_w, mod_b, norm_g, m_w_in, m_b_gate, m_w_conv, m_g_head, m_w_out,
              h_w_in, h_b_f, h_lb_raw, h_g_head, h_w_out, f_w_gu, f_w_down,
              e_w_router, e_b_router, e_w_gu, e_w_down):
    B = x.shape[0]
    rows = x.shape[1] // GRID_W
    silu_c = jax.nn.silu(c)
    silu_cc = jax.nn.silu(c_ctx)
    lb_all = jax.nn.softmax(h_lb_raw.astype(F32), axis=0)
    lb_all = jnp.cumsum(lb_all, axis=0) - lb_all[0]
    lat, cx = x, ctx
    for i in range(DEPTH):
        j = i // 2
        with_ctx = i < DEPTH - 1
        mod_l = (silu_c @ mod_w[i] + mod_b[i]).reshape(B, 1, N_MOD, D_MODEL)
        mod_c = (silu_cc @ mod_w[i] + mod_b[i]).reshape(1, N_MOD, D_MODEL)
        sh1, sc1, gt1, sh2, sc2, gt2 = [mod_l[:, :, s] for s in range(N_MOD)]
        csh1, csc1, cgt1, csh2, csc2, cgt2 = [mod_c[:, s] for s in range(N_MOD)]

        u_l = rmsnorm(lat, norm_g[i, 0]) * (1 + sc1) + sh1
        u_c = rmsnorm(cx, norm_g[i, 0]) * (1 + csc1) + csh1
        if i % N_MIXERS == 0:
            y_c, y_l = mlstm_mixer(u_c, u_l, m_w_in[j], m_b_gate[j], m_w_conv[j], m_g_head[j], m_w_out[j], with_ctx)
        else:
            y_c, y_l = hgrn2_mixer(u_c, u_l, h_w_in[j], h_b_f[j], lb_all[j], h_g_head[j], h_w_out[j], rows, with_ctx)
        lat = lat + gt1 * rmsnorm(y_l, norm_g[i, 1])

        if i % 2 == 0:
            ffn = lambda u: swiglu(u, f_w_gu[j], f_w_down[j])
        else:
            ffn = lambda u: moe_swiglu(u, e_w_router[j], e_b_router[j], e_w_gu[j], e_w_down[j])
        u_l = rmsnorm(lat, norm_g[i, 2]) * (1 + sc2) + sh2
        lat = lat + gt2 * rmsnorm(ffn(u_l), norm_g[i, 3])

        if with_ctx:
            cx = cx + cgt1 * rmsnorm(y_c, norm_g[i, 1])
            u_c = rmsnorm(cx, norm_g[i, 2]) * (1 + csc2) + csh2
            cx = cx + cgt2 * rmsnorm(ffn(u_c), norm_g[i, 3])
    return lat


_drawn_inputs = setup_inputs


def setup_inputs(seed=0):
    import zlib

    import numpy as np

    out = dict(_drawn_inputs(seed))
    spreads = {}
    factors = {'h_b_f': 2.876, 'e_b_router': 8.0}
    for name, (base, spread) in spreads.items():
        noise = np.random.default_rng([zlib.crc32(name.encode()), seed]).standard_normal(out[name].shape)
        drawn = base * np.exp(spread * noise) if base else spread * noise
        out[name] = jnp.asarray(drawn.astype(out[name].dtype))
    for name, factor in factors.items():
        out[name] = (out[name] * factor).astype(out[name].dtype)
    return out
```

```python
from contextlib import ExitStack

import concourse.bass as bass
from concourse import mybir
from concourse.alu_op_type import AluOpType as ALU

F32 = mybir.dt.float32
I32 = mybir.dt.int32
U8 = mybir.dt.uint8
ACT = mybir.ActivationFunctionType
AX = mybir.AxisListType

P = 128
D = 1024
KD = D // P
CTX, LAT = 256, 256
T = CTX + LAT
NT = T // P
HALF = 512
EPS = 1e-6
N_MOD = 6
HEADS = 8
DV = 128
M_DK = 64
M_QK = 2 * HEADS * M_DK
M_V = HEADS * DV
VST = DV + 2
FFN = 2816
FC = FFN // P
GRID_W = 64
GRID_H = LAT // GRID_W
EXPERTS = 8
SHIFT = 0.125

RING = 4
SLOT = KD * HALF
E_RING = 6
E_N = 352
E_TILES = FFN // E_N
E_KH = FC // 2
E_Q = 256
E_SLOT = KD * E_N
E_UNITS = 2 * E_TILES + 2 * (D // E_Q)
LEVELS = 7


class Names:
    pass


class Chain:

    def __init__(self, engine, sem):
        self.engine, self.sem, self.n = engine, sem, 0

    def link(self, instruction):
        instruction.then_inc(self.sem, 1)
        self.n += 1
        self.engine.wait_ge(self.sem, self.n)


class WeightStream:

    def __init__(self, ring, rows, loaded):
        self.ring, self.rows, self.loaded = ring, rows, loaded
        self.parts, self.value, self.sent = [], [], 0
        self.count = [0] * RING
        self.release = {}

    def slot(self, n):
        s = n % RING
        return self.ring[:, s * SLOT:(s + 1) * SLOT]

    def aux(self, n, partition):
        s = n % RING
        return self.rows[partition:partition + 1, s * HALF:(s + 1) * HALF]

    def add(self, *parts):
        n = len(self.parts)
        self.parts.append(parts)
        self.count[n % RING] += 16 * len(parts)
        self.value.append(self.count[n % RING])

    def send(self, sp, end):
        for n in range(self.sent, min(end, len(self.parts))):
            if n - RING in self.release:
                sp.wait_ge(*self.release[n - RING])
            for place, source in self.parts[n]:
                sp.dma_start(self.aux(n, place) if isinstance(place, int) else place(self.slot(n)), source).then_inc(self.loaded[n % RING], 16)
        self.sent = max(self.sent, min(end, len(self.parts)))

    def arrived(self, engine, n):
        engine.wait_ge(self.loaded[n % RING], self.value[n])


def rows_of(width):
    return lambda slot: slot[:, 0:KD * width].rearrange("p (k n) -> p k n", k=KD)


def columns(w, first, width):
    return w[:, first:first + width].rearrange("(k p) n -> p k n", p=P)


def row(v, first):
    return v[first:first + HALF].rearrange("(o n) -> o n", o=1)


def plan_stream(k):
    a, s = k.a, k.stream
    wide = rows_of(HALF)
    plan = {}

    def start(name):
        plan[name] = len(s.parts)

    def add_mod(layer):
        start(f"mod{layer}")
        for n in range(2 * N_MOD):
            parts = [(wide, columns(a["mod_w"][layer], n * HALF, HALF)),
                     (0, row(a["mod_b"][layer], n * HALF))]
            if n // 2 in (2, 5):
                gain = a["norm_g"][layer, 1 if n // 2 == 2 else 3]
                parts.append((32, row(gain, (n % 2) * HALF)))
            s.add(*parts)

    add_mod(0)
    w = a["m_w_in"][0]
    start("m_in")
    s.add((rows_of(4 * HEADS), columns(w, M_QK + 2 * M_V, 4 * HEADS)))
    for n in range(0, M_QK + 2 * M_V, HALF):
        s.add((wide, columns(w, n, HALF)))
    start("m_out")
    for n in range(0, D, HALF):
        s.add((wide, columns(a["m_w_out"][0], n, HALF)))
    w = a["f_w_gu"][0]
    start("f_up")
    for f in range(0, FC, 2):
        def place(side):
            return lambda slot: slot[:, 0:SLOT].rearrange("p (k s n) -> p k s n", k=KD, s=2)[:, :, side, :]
        s.add((place(0), columns(w, f * P, 2 * P)), (place(1), columns(w, FFN + f * P, 2 * P)))
    start("f_down")
    w = a["f_w_down"][0].rearrange("(f p) n -> p f n", p=P)
    for f in range(0, FC, 4):
        m = min(4, FC - f)
        s.add((lambda slot, m=m: slot[:, 0:m * D].rearrange("p (f n) -> p f n", f=m), w[:, f:f + m, :]))
    add_mod(1)
    w = a["h_w_in"][0]
    start("h_in")
    for direction in range(2):
        for half in range(2):
            s.add((wide, columns(w, (2 + direction) * D + half * HALF, HALF)))
    for first in (D, 0, 4 * D):
        for half in range(2):
            s.add((wide, columns(w, first + half * HALF, HALF)))
    start("h_out")
    for n in range(0, D, HALF):
        s.add((wide, columns(a["h_w_out"][0], n, HALF)))
    k.plan = plan



def setup(k):
    nc, a = k.nc, k.a
    rows_in, x_in, made, same_made = k.sem("rows_in"), k.sem("x_in"), k.sem("ones_made"), k.sem("same_made")
    small_in, silu_done, turned = k.sem("small_in"), k.sem("silu_done"), k.sem("rows_turned")
    own, iota_made = k.sem("setup_chain"), k.sem("iota_made")
    same = k.ex[:, 0:1024].rearrange("p (l n) -> p l n", l=8)
    iota_i = k.ex[:, 1024:1024 + 272].bitcast(I32)

    with nc.Block() as block:

        @block.sync
        def _(sp):
            sp.dma_start(k.crows[0:8, :], a["c_ctx"].rearrange("(k p) -> k p", p=P)).then_inc(rows_in, 16)
            sp.dma_start(k.crows[8:16, :], a["c"][0].rearrange("(k p) -> k p", p=P)).then_inc(rows_in, 16)
            sp.dma_start(k.crows[16:32, :], a["h_lb_raw"][0].rearrange("a (k p) -> (a k) p", p=P)).then_inc(rows_in, 16)
            sp.dma_start(k.vrows[0:64, :], a["norm_g"].rearrange("l n (k p) -> (l n k) p", p=P)).then_inc(rows_in, 16)
            sp.dma_start(k.vrows[64:88, :], a["m_w_conv"][0].rearrange("t (k p) -> (t k) p", p=P)).then_inc(rows_in, 16)
            sp.dma_start(k.vrows[88:96, :], a["m_g_head"][0].rearrange("(k p) -> k p", p=P)).then_inc(rows_in, 16)
            sp.dma_start(k.vrows[96:104, :], a["h_g_head"][0].rearrange("(k p) -> k p", p=P)).then_inc(rows_in, 16)
            sp.dma_start(k.vrows[104:120, :], a["h_b_f"][0].rearrange("a (k p) -> (a k) p", p=P)).then_inc(rows_in, 16)
            k.stream.send(sp, RING)
            sp.dma_start(k.resid[:, 0:2, :], a["ctx"][0].rearrange("(t p) d -> p t d", p=P)).then_inc(x_in, 16)
            sp.dma_start(k.resid[:, 2:4, :], a["x"][0].rearrange("(t p) d -> p t d", p=P)).then_inc(x_in, 16)
            for g in range(4):
                sp.dma_start(k.gate_bias[(g // 2) * 8:(g // 2) * 8 + 8, g % 2:g % 2 + 1],
                             a["m_b_gate"][0, g].rearrange("(h o) -> h o", o=1)).then_inc(small_in, 16)
            sp.dma_start(k.w_router[:, :, :], a["e_w_router"][0].rearrange("(k p) e -> p k e", p=P)).then_inc(small_in, 16)
            sp.dma_start(k.b_router[0:1, :], a["e_b_router"][0:1, :]).then_inc(small_in, 16)
            sp.wait_ge(x_in, 32)
            sp.wait_ge(small_in, 96)

        @block.gpsimd
        def _(pool):
            pool.memset(k.ones[:, :], 1.0).then_inc(made, 1)
            pool.wait_ge(made, 1)
            pool.affine_select(out=k.ident[:, :], in_=k.ones[:, :], compare_op=ALU.is_equal, fill=0.0, base=0,
                               pattern=[[-1, P]], channel_multiplier=1).then_inc(made, 1)
            pool.affine_select(out=k.before[:, :], in_=k.ones[:, :], compare_op=ALU.is_gt, fill=0.0, base=0,
                               pattern=[[1, P]], channel_multiplier=-1).then_inc(made, 1)
            pool.affine_select(out=k.after[:, :], in_=k.ones[:, :], compare_op=ALU.is_gt, fill=0.0, base=0,
                               pattern=[[-1, P]], channel_multiplier=1).then_inc(made, 1)
            pool.iota(iota_i[:, 0:256], pattern=[[1, 256]], base=0, channel_multiplier=0).then_inc(iota_made, 1)
            pool.iota(iota_i[:, 256:272], pattern=[[0, 2], [1, 8]], base=8, channel_multiplier=0).then_inc(iota_made, 1)
            for i in range(8):
                size, n = 2 ** i, P // 2 ** i
                view = same[:, i, :].rearrange("p (b l) -> p b l", l=size)
                pool.affine_select(out=view, in_=k.ones[:, :].rearrange("p (b l) -> p b l", l=size),
                                   compare_op=ALU.is_ge, fill=0.0, base=0, pattern=[[-size, n], [0, size]],
                                   channel_multiplier=1).then_inc(same_made, 1)
                pool.wait_ge(same_made, 2 * i + 1)
                pool.affine_select(out=view, in_=view, compare_op=ALU.is_ge, fill=0.0, base=size - 1,
                                   pattern=[[size, n], [0, size]], channel_multiplier=-1).then_inc(same_made, 1)

        @block.scalar
        def _(act):
            act.wait_ge(rows_in, 128)
            nc.scalar.activation(k.crows[0:16, :], k.crows[0:16, :], ACT.Silu).then_inc(silu_done, 1)
            act.wait_ge(own, 2)
            nc.scalar.activation(k.lb_exp[:, :], k.lb_exp[:, :], ACT.Exp).then_inc(silu_done, 1)

        @block.tensor
        def _(pe):
            pe.wait_ge(made, 2)
            pe.wait_ge(rows_in, 128)
            nc.tensor.transpose(k.ps[:, 0, 0:120], k.vrows[0:120, :], k.ident[0:120, 0:120]).then_inc(turned, 1)
            pe.wait_ge(silu_done, 1)
            nc.tensor.transpose(k.ps[:, 1, 0:32], k.crows[0:32, :], k.ident[0:32, 0:32]).then_inc(turned, 1)

        @block.vector
        def _(dve):
            chain = Chain(dve, own)
            dve.wait_ge(turned, 2)
            chain.link(nc.vector.tensor_copy(k.lb_raw[:, :], k.ps[:, 1, 16:32]))
            chain.link(nc.vector.tensor_tensor(k.lb_exp[:, :], k.lb_raw[:, :], k.lb_raw[:, :], ALU.subtract))
            nc.vector.tensor_copy(k.vcol[:, :], k.ps[:, 0, 0:120])
            nc.vector.tensor_copy(k.c_cols[:, :, :], k.ps[:, 1, 0:16].rearrange("p (j k) -> p k j", j=2))
            nc.vector.memset(k.eps[:, :], EPS)
            nc.vector.memset(k.vaug[:, :, :, DV:DV + 1], 1.0)
            nc.vector.memset(k.gate_sel[:, :, :], 0.0).then_inc(own, 1)
            chain.n += 1
            dve.wait_ge(made, 4)
            dve.wait_ge(own, chain.n)
            for g, (src, dst) in enumerate(((0, 0), (16, 8), (8, 0), (24, 8))):
                nc.vector.tensor_copy(k.gate_sel[0:32, g, dst:dst + 8], k.ident[0:32, src:src + 8])
            dve.wait_ge(iota_made, 2)
            nc.vector.tensor_copy(k.slot_no[:, :], iota_i[:, 0:256])
            nc.vector.tensor_copy(k.expert_no[:, :, :], iota_i[:, 256:272].rearrange("p (i e) -> p i e", i=2))
            dve.wait_ge(same_made, 16)
            nc.vector.tensor_tensor(k.level_mask[:, :, :], same[:, 1:8, :], same[:, 0:7, :], ALU.subtract)
            dve.wait_ge(silu_done, 2)
            chain.link(nc.vector.reciprocal(k.lb_raw[:, :], k.lb_exp[:, :]))
            chain.link(nc.vector.tensor_tensor(k.lb_exp[:, :], k.lb_exp[:, :], k.lb_raw[:, :], ALU.mult))
            chain.link(nc.vector.tensor_tensor(k.lb_col[:, :], k.lb_exp[:, :], k.lb_exp[:, :], ALU.subtract))
            nc.vector.tensor_scalar(k.lb_rest[:, :], k.lb_col[:, :], -1.0, 1.0, ALU.mult, ALU.add)



def modulation(k, layer):
    nc, s, u0 = k.nc, k.stream, k.plan[f"mod{layer}"]
    row_ready, row_copied = k.sem(f"mod{layer}_row_ready"), k.sem(f"mod{layer}_row_copied")
    cols_ready, cols_copied = k.sem(f"mod{layer}_cols_ready"), k.sem(f"mod{layer}_cols_copied")
    scaled, spread, gate_copied = k.sem(f"mod{layer}_scaled"), k.sem(f"mod{layer}_spread"), k.sem(f"mod{layer}_gate_copied")
    units = 2 * N_MOD
    streams = (0, 1) if layer == 0 else (1,)
    gates = [n for n in range(units) if n // 2 in (2, 5)]
    plain = [n for n in range(units) if n not in gates]
    rows = k.ex[0:2, 0:2 * HALF].rearrange("p (b n) -> p b n", b=2)
    scaled_rows = k.ex[0:2, 2 * HALF:4 * HALF].rearrange("p (b n) -> p b n", b=2)
    s.release = {u0 + n: (row_ready, n + 1) for n in range(units)}

    with nc.Block() as block:

        @block.sync
        def _(sp):
            s.send(sp, u0 + units + RING)

        @block.tensor
        def _(pe):
            def finish(n):
                pe.wait_ge(row_copied, n + 1)
                if n in plain:
                    i = plain.index(n)
                    if i >= 2:
                        pe.wait_ge(cols_copied, i - 1)
                    for c in range(4):
                        last = nc.tensor.transpose(k.ps[:, 4 + i % 2, 2 * c:2 * c + 2],
                                                   rows[0:2, n % 2, c * P:(c + 1) * P], k.ident[0:2, 0:2])
                    last.then_inc(cols_ready, 1)
                else:
                    g = gates.index(n)
                    pe.wait_ge(scaled, g + 1)
                    if g:
                        pe.wait_ge(gate_copied, g * len(streams))
                    for j in streams:
                        nc.tensor.matmul(k.ps[:, 6 + j, :], k.ident[0:2, j:j + 1].to_broadcast([2, P]), scaled_rows[0:2, g % 2, :],
                                         start=True, stop=True).then_inc(spread, 1)

            for n in range(units):
                s.arrived(pe, u0 + n)
                slot = s.slot(u0 + n)
                w = rows_of(HALF)(slot)
                if n >= 2:
                    pe.wait_ge(row_copied, n - 1)
                if n in gates:
                    if gates.index(n):
                        pe.wait_ge(scaled, gates.index(n))
                    nc.tensor.matmul(k.ps[0:2, 2, :], k.ones[32:33, 0:2], s.aux(u0 + n, 32), start=True, stop=True)
                for c in range(KD):
                    nc.tensor.matmul(k.ps[0:2, n % 2, :], k.c_cols[:, c, :], w[:, c, :], start=(c == 0), stop=False)
                nc.tensor.matmul(k.ps[0:2, n % 2, :], k.ones[0:1, 0:2], s.aux(u0 + n, 0), start=False,
                                 stop=True).then_inc(row_ready, 1)
                if n:
                    finish(n - 1)
            finish(units - 1)

        @block.scalar
        def _(act):
            for n in range(units):
                act.wait_ge(row_ready, n + 1)
                if n >= 2:
                    if n - 2 in plain:
                        act.wait_ge(cols_ready, plain.index(n - 2) + 1)
                    else:
                        act.wait_ge(scaled, gates.index(n - 2) + 1)
                nc.scalar.activation(rows[0:2, n % 2, :], k.ps[0:2, n % 2, :], ACT.Copy).then_inc(row_copied, 1)

        @block.vector
        def _(dve):
            for n in range(units):
                if n in plain:
                    i = plain.index(n)
                    dve.wait_ge(cols_ready, i + 1)
                    nc.vector.tensor_copy(k.mod_cols[:, n // 2, 4 * (n % 2):4 * (n % 2) + 4, :],
                                          k.ps[:, 4 + i % 2, 0:8].rearrange("p (c j) -> p c j", j=2)).then_inc(cols_copied, 1)
                    continue
                g = gates.index(n)
                dve.wait_ge(row_copied, n + 1)
                if g >= 2:
                    dve.wait_ge(spread, (g - 1) * len(streams))
                nc.vector.tensor_tensor(scaled_rows[0:2, g % 2, :], rows[0:2, n % 2, :], k.ps[0:2, 2, :],
                                        ALU.mult).then_inc(scaled, 1)
                for i, j in enumerate(streams):
                    dve.wait_ge(spread, g * len(streams) + i + 1)
                    nc.vector.tensor_copy(k.gate[:, g // 2, j, (n % 2) * HALF:(n % 2 + 1) * HALF],
                                          k.ps[:, 6 + j, :]).then_inc(gate_copied, 1)
            dve.wait_ge(cols_copied, len(plain))
            for w in range(2):
                gain = k.vcol[:, (layer * 4 + 2 * w) * KD:(layer * 4 + 2 * w + 1) * KD]
                nc.vector.scalar_tensor_tensor(out=k.mod_scale[:, w, :, :], in0=k.mod_cols[:, 1 + 3 * w, :, :], scalar=1.0,
                                               in1=gain.unsqueeze(2).to_broadcast([P, KD, 2]), op0=ALU.add, op1=ALU.mult)



def norm_in(k, name, which, tiles, column_major=False):
    nc = k.nc
    squared, root, normed = k.sem(name + "_squared"), k.sem(name + "_root"), k.sem(name + "_normed")
    turned, recip = k.sem(name + "_turned"), k.sem(name + "_recip")
    t0, t1 = tiles[0], tiles[-1] + 1
    streams = [j for j in range(2) if 2 * j in tiles]

    def source(c, j):
        return k.ps[:, c, j * 256:(j + 1) * 256]

    def views(c, j):
        src, dst = source(c, j), k.u_cols[:, c, j * 256:(j + 1) * 256]
        if column_major and j == 1:
            return (src.rearrange("p (r w) -> p r w", r=GRID_H), dst.rearrange("p (w r) -> p r w", r=GRID_H))
        return src, dst

    with nc.Block() as block:

        @block.scalar
        def _(act):
            for i in tiles:
                nc.scalar.activation(k.tok[:, i, :], k.resid[:, i, :], ACT.Square,
                                     accum_out=k.ssq[:, i:i + 1]).then_inc(squared, 1)
            act.wait_ge(squared, len(tiles))
            nc.scalar.activation(k.rms[:, t0:t1], k.ssq[:, t0:t1], ACT.Sqrt, bias=k.eps[:, 0:1],
                                 scale=1.0 / D).then_inc(root, 1)
            for c in range(1, KD, 2):
                act.wait_ge(turned, c + 1)
                for j in streams:
                    src, dst = views(c, j)
                    nc.scalar.activation(dst, src, ACT.Identity, bias=k.mod_cols[:, 3 * which, c, j:j + 1],
                                         scale=k.mod_scale[:, which, c, j:j + 1])

        @block.vector
        def _(dve):
            dve.wait_ge(root, 1)
            nc.vector.reciprocal(k.rstd[:, t0:t1], k.rms[:, t0:t1]).then_inc(recip, 1)
            dve.wait_ge(recip, 1)
            for i in tiles:
                nc.vector.tensor_scalar(k.tok[:, i, :], k.resid[:, i, :], k.rstd[:, i:i + 1], None,
                                        ALU.mult).then_inc(normed, 1)
            for c in range(0, KD, 2):
                dve.wait_ge(turned, c + 1)
                for j in streams:
                    src, dst = views(c, j)
                    nc.vector.tensor_scalar(dst, src, k.mod_scale[:, which, c, j:j + 1],
                                            k.mod_cols[:, 3 * which, c, j:j + 1], ALU.mult, ALU.add)

        @block.tensor
        def _(pe):
            for n, i in enumerate(tiles):
                pe.wait_ge(normed, n + 1)
                for c in range(KD):
                    last = nc.tensor.transpose(k.ps[:, c, i * P:(i + 1) * P], k.tok[:, i, c * P:(c + 1) * P], k.ident[:, :])
                    if i == tiles[-1]:
                        last.then_inc(turned, 1)



def residual_scalar(k, act, r, tiles, copies):
    nc = k.nc
    if copies:
        for n, i in enumerate(tiles):
            act.wait_ge(r.ready, r.ready_value(i, 0))
            nc.scalar.activation(k.tok[:, i, 0:HALF], k.ps[:, r.bank(i, 0), :], ACT.Copy).then_inc(r.copied_a, 1)
    for n, i in enumerate(tiles):
        if copies:
            act.wait_ge(r.copied_a, n + 1)
            act.wait_ge(r.copied_b, n + 1)
        nc.scalar.activation(k.junk[:, :], k.tok[:, i, :], ACT.Square, accum_out=k.ssq[:, i:i + 1]).then_inc(r.squared, 1)
        act.wait_ge(r.squared, n + 1)
        nc.scalar.activation(k.rms[:, i:i + 1], k.ssq[:, i:i + 1], ACT.Sqrt, bias=k.eps[:, 0:1],
                             scale=1.0 / D).then_inc(r.root, 1)


def residual_vector(k, dve, r, tiles, which, copies):
    nc = k.nc
    if copies:
        for n, i in enumerate(tiles):
            dve.wait_ge(r.ready, r.ready_value(i, 1))
            nc.vector.tensor_copy(k.tok[:, i, HALF:D], k.ps[:, r.bank(i, 1), :]).then_inc(r.copied_b, 1)
    chain = Chain(dve, r.chain)
    for n, i in enumerate(tiles):
        dve.wait_ge(r.root, n + 1)
        chain.link(nc.vector.reciprocal(k.rstd[:, i:i + 1], k.rms[:, i:i + 1]))
        chain.link(nc.vector.scalar_tensor_tensor(out=k.tok[:, i, :], in0=k.tok[:, i, :], scalar=k.rstd[:, i:i + 1],
                                                  in1=k.gate[:, which, i // 2, :], op0=ALU.mult, op1=ALU.mult))
        nc.vector.tensor_tensor(k.resid[:, i, :], k.resid[:, i, :], k.tok[:, i, :], ALU.add).then_inc(r.added, 1)


def residual_sems(k, name, bank, ready_value):
    r = Names()
    r.bank, r.ready_value = bank, ready_value
    r.ready, r.copied_a, r.copied_b = k.sem(name + "_ready"), k.sem(name + "_copied_a"), k.sem(name + "_copied_b")
    r.squared, r.root, r.chain, r.added = (k.sem(f"{name}_{n}") for n in ("squared", "root", "chain", "added"))
    return r



def mlstm_in(k):
    nc, s, u0 = k.nc, k.stream, k.plan["m_in"]
    gates_ready, gates_copied, picked = k.sem("m_gates_ready"), k.sem("m_gates_copied"), k.sem("m_picked")
    job_ready, conv_done, job_copied = k.sem("m_job_ready"), k.sem("m_conv_done"), k.sem("m_job_copied")
    own, act_own, scan_ready, cols_ready = k.sem("m_chain"), k.sem("m_act_own"), k.sem("m_scan_ready"), k.sem("m_cols_ready")
    conv_own, scan_input, exp_ready = k.sem("m_conv_own"), k.sem("m_scan_input"), k.sem("m_exp_ready")
    units = 7
    s.release = {u0: (gates_ready, 1)}
    for u in range(6):
        s.release[u0 + 1 + u] = (job_ready, 4 * u + 4)
    pre = k.junk

    with nc.Block() as block:

        @block.sync
        def _(sp):
            s.send(sp, u0 + units + RING)

        @block.tensor
        def _(pe):
            s.arrived(pe, u0)
            w = rows_of(4 * HEADS)(s.slot(u0))
            for c in range(KD):
                last = nc.tensor.matmul(k.ps[0:32, 0, :], w[:, c, :], k.u_cols[:, c, :], start=(c == 0), stop=(c == KD - 1))
            last.then_inc(gates_ready, 1)

            def job(r):
                u = u0 + 1 + r // 4
                if r % 4 == 0:
                    s.arrived(pe, u)
                w = rows_of(HALF)(s.slot(u))
                bank = 1 + r % 4
                if r >= 12:
                    pe.wait_ge(job_copied, r - 3)
                elif r >= 4:
                    pe.wait_ge(conv_done, r - 3)
                i = r % 4
                for c in range(KD):
                    if 8 <= r < 16:
                        lhs, rhs = k.u_cols[:, c, i * P:(i + 1) * P], w[:, c, :]
                    else:
                        lhs, rhs = w[:, c, i * P:(i + 1) * P], k.u_cols[:, c, :]
                    last = nc.tensor.matmul(k.ps[:, bank, :], lhs, rhs, start=(c == 0), stop=(c == KD - 1))
                last.then_inc(job_ready, 1)

            for r in range(24):
                job(r)
                if r == 0:
                    pe.wait_ge(gates_copied, 2)
                    for g in range(2):
                        nc.tensor.matmul(k.ps[0:16, 6 + g, :], k.gate_sel[0:32, 2 * g, :], k.gates_f[0:32, :],
                                         start=True, stop=False)
                        last = nc.tensor.matmul(k.ps[0:16, 6 + g, :], k.gate_sel[0:32, 2 * g + 1, :], k.gates_b[0:32, :],
                                                start=False, stop=True)
                    last.then_inc(picked, 1)
                if r == 20:
                    pe.wait_ge(scan_ready, 1)
                    for q, src in enumerate((k.scan_a, k.scan_a_rev, k.scan_e, k.scan_e_rev)):
                        for i in range(NT):
                            n = (q * NT + i) * 16
                            last = nc.tensor.transpose(k.ps[:, 0, n:n + 16], src[0:16, i * P:(i + 1) * P], k.ident[0:16, 0:16])
                    last.then_inc(cols_ready, 1)

        @block.scalar
        def _(act):
            def gates():
                act.wait_ge(picked, 1)
                nc.scalar.activation(k.scan_t[0:16, :], k.ps[0:16, 7, :], ACT.Abs, bias=k.gate_bias[0:16, 1:2]).then_inc(act_own, 1)
                act.wait_ge(act_own, 1)
                nc.scalar.activation(k.scan_t[0:16, :], k.scan_t[0:16, :], ACT.Exp, scale=-1.0).then_inc(act_own, 1)
                act.wait_ge(act_own, 2)
                nc.scalar.activation(k.scan_t[0:16, :], k.scan_t[0:16, :], ACT.Ln, bias=1.0).then_inc(scan_input, 1)

            for r in range(24):
                if r < 8:
                    act.wait_ge(conv_done, r + 1)
                    nc.scalar.activation(k.qk[:, r, :], pre[:, (r % 2) * HALF:(r % 2 + 1) * HALF], ACT.Silu).then_inc(job_copied, 1)
                elif r < 16:
                    i, half = r % 4, (r - 8) // 4
                    act.wait_ge(job_ready, r + 1)
                    nc.scalar.activation(k.vaug[:, i, 4 * half:4 * half + 4, 0:DV],
                                         k.ps[:, 1 + r % 4, :].rearrange("p (h d) -> p h d", h=4), ACT.Copy).then_inc(job_copied, 1)
                else:
                    act.wait_ge(job_ready, r + 1)
                    nc.scalar.activation(k.o_cols[:, r - 16, :], k.ps[:, 1 + r % 4, :], ACT.Sigmoid).then_inc(job_copied, 1)
                if r == 1:
                    gates()
                if r == 15:
                    act.wait_ge(exp_ready, 1)
                    nc.scalar.activation(k.scan_e[0:16, :], k.scan_e[0:16, :], ACT.Exp, scale=-1.0).then_inc(act_own, 1)

        @block.vector
        def _(dve):
            chain = Chain(dve, own)
            chain.link(nc.vector.memset(k.zeros[0:16, :], 0.0))
            dve.wait_ge(gates_ready, 1)
            g = k.ps[0:32, 0, :].rearrange("p (s t) -> p s t", s=2)
            nc.vector.tensor_copy(k.gates_f[0:32, :], k.ps[0:32, 0, :]).then_inc(gates_copied, 1)
            nc.vector.tensor_copy(k.gates_b[0:32, :].rearrange("p (s t) -> p s t", s=2), g[:, :, ::-1]).then_inc(gates_copied, 1)

            def scan():
                z, i_sum, t = k.scan_z[0:16, :], k.scan_a[0:16, :], k.scan_t[0:16, :]
                dve.wait_ge(picked, 1)
                dve.wait_ge(scan_input, 1)
                chain.link(nc.vector.tensor_scalar(z, k.ps[0:16, 7, :], k.gate_bias[0:16, 1:2], None, ALU.add))
                chain.link(nc.vector.scalar_tensor_tensor(out=t, in0=z, scalar=0.0, in1=t, op0=ALU.min, op1=ALU.subtract))
                chain.link(nc.vector.tensor_tensor_scan(z, t, k.zeros[0:16, :], 0.0, ALU.add, ALU.add))
                chain.link(nc.vector.scalar_tensor_tensor(out=i_sum, in0=k.ps[0:16, 6, :], scalar=k.gate_bias[0:16, 0:1],
                                                          in1=z, op0=ALU.add, op1=ALU.subtract))
                chain.link(nc.vector.tensor_tensor_scan(k.scan_m[0:16, :], i_sum, i_sum, 0.0, ALU.max, ALU.max))
                nc.vector.tensor_tensor(k.scan_e[0:16, :], k.scan_m[0:16, :], z, ALU.add).then_inc(exp_ready, 1)

            for r in range(8):
                dve.wait_ge(job_ready, r + 1)
                if r >= 2:
                    dve.wait_ge(job_copied, r - 1)
                x = k.ps[:, 1 + r % 4, :].rearrange("p (s t) -> p s t", s=2)
                y = pre[:, (r % 2) * HALF:(r % 2 + 1) * HALF].rearrange("p (s t) -> p s t", s=2)
                tap = [k.vcol[:, 64 + t * KD + r:65 + t * KD + r] for t in range(3)]
                nc.vector.tensor_scalar(y, x, tap[1], None, ALU.mult).then_inc(conv_own, 1)
                dve.wait_ge(conv_own, 2 * r + 1)
                nc.vector.scalar_tensor_tensor(out=y[:, :, 1:], in0=x[:, :, 0:255], scalar=tap[0], in1=y[:, :, 1:],
                                               op0=ALU.mult, op1=ALU.add).then_inc(conv_own, 1)
                dve.wait_ge(conv_own, 2 * r + 2)
                nc.vector.scalar_tensor_tensor(out=y[:, :, 0:255], in0=x[:, :, 1:], scalar=tap[2], in1=y[:, :, 0:255],
                                               op0=ALU.mult, op1=ALU.add).then_inc(conv_done, 1)
                if r == 3:
                    scan()
            dve.wait_ge(act_own, 3)
            for dst, src in ((k.scan_a_rev, k.scan_a), (k.scan_m_rev, k.scan_m), (k.scan_e_rev, k.scan_e)):
                last = nc.vector.tensor_copy(dst[0:16, :].rearrange("p (s t) -> p s t", s=2),
                                             src[0:16, :].rearrange("p (s t) -> p s t", s=2)[:, :, ::-1])
            last.then_inc(scan_ready, 1)
            dve.wait_ge(cols_ready, 1)
            c = k.ps[:, 0, 0:256].rearrange("p (q r i h) -> p q r i h", q=2, r=2, h=16)
            for d in range(2):
                nc.vector.tensor_copy(k.a_cols[:, :, 8 * d:8 * d + 8], c[:, 0, d, :, 8 * d:8 * d + 8])
                nc.vector.tensor_copy(k.e_cols[:, :, 8 * d:8 * d + 8], c[:, 1, d, :, 8 * d:8 * d + 8])



SEEN = {0: [(0, 4), (1, 4), (2, 4), (3, 4)], 1: [(0, 4), (0, 4), (2, 3), (2, 4)]}
SOURCES = {0: [[0], [0, 1], [0, 1, 2], [0, 1, 2, 3]], 1: [[0, 1], [1], [0, 1, 2, 3], [0, 1, 3]]}


def mlstm_heads(k):
    nc = k.nc
    scored, spread, weighed, probs = k.sem("a_scored"), k.sem("a_spread"), k.sem("a_weighed"), k.sem("a_probs")
    masked, summed, own, added = k.sem("a_masked"), k.sem("a_summed"), k.sem("a_chain"), k.sem("a_added")
    turn_done, squares = k.sem("a_turn_done"), k.sem("a_squares")
    prob = k.u_area.rearrange("p (b s t) -> p b s t", b=2, s=NT)
    decay = k.ex[:, 0:4 * HALF].rearrange("p (s t) -> p s t", s=NT)
    part = k.ex[:, 4 * HALF:6 * HALF].rearrange("p (b t) -> p b t", b=2)
    turns = 2 * HEADS

    def score_cols(j):
        return (j, 0) if j < 2 else (2, (j - 2) * 256 - 256)

    with nc.Block() as block:

        @block.sync
        def _(sp):
            s = k.stream
            s.release = {}
            s.send(sp, s.sent)

        @block.tensor
        def _(pe):
            def scores(h):
                if h:
                    pe.wait_ge(probs, 8 * h)
                base = (h % 2) * 64
                for j in range(NT):
                    bank, col = score_cols(j)
                    t0 = 0 if j < 2 else 256
                    last = nc.tensor.matmul(k.ps[:, bank, col + t0:col + T], k.qk[base:base + 64, 4 + h // 2, j * P:(j + 1) * P],
                                            k.qk[base:base + 64, h // 2, t0:T], start=True, stop=True)
                last.then_inc(scored, 1)

            def spread_m(n):
                h, d = n // 2, n % 2
                if n >= 2:
                    pe.wait_ge(weighed, 4 * (n - 1))
                src = (k.scan_m, k.scan_m_rev)[d]
                nc.tensor.matmul(k.ps[:, 3 + d, :], k.ident[0:16, 8 * d + h:8 * d + h + 1].to_broadcast([16, P]),
                                 src[0:16, :], start=True, stop=True).then_inc(spread, 1)

            def values(n):
                h, d = n // 2, n % 2
                pe.wait_ge(masked, n + 1)
                if n:
                    pe.wait_ge(summed, n)
                for i in range(NT):
                    js = SOURCES[d][i]
                    for m, j in enumerate(js):
                        last = nc.tensor.matmul(k.ps[:, 5 + i // 2, (i % 2) * 256:(i % 2) * 256 + DV + 1],
                                                prob[:, n % 2, j, i * P:(i + 1) * P], k.vaug[:, j, h, 0:DV + 1],
                                                start=(m == 0), stop=(m == len(js) - 1))
                last.then_inc(turn_done, 1)

            scores(0)
            spread_m(0)
            spread_m(1)
            for n in range(turns):
                if n % 2 == 0 and n:
                    scores(n // 2)
                    spread_m(n)
                    spread_m(n + 1)
                if n:
                    values(n - 1)
            values(turns - 1)

        @block.scalar
        def _(act):
            for n in range(turns):
                h, d = n // 2, n % 2
                act.wait_ge(spread, n + 1)
                for j in range(NT):
                    t0, t1 = (x * P for x in SEEN[d][j])
                    if n:
                        act.wait_ge(probs, 4 * (n - 1) + j + 1)
                    nc.scalar.activation(decay[:, j, t0:t1], k.ps[:, 3 + d, t0:t1], ACT.Exp, scale=-1.0,
                                         bias=k.a_cols[:, j, 8 * d + h:8 * d + h + 1]).then_inc(weighed, 1)

        @block.vector
        def _(dve):
            chain = Chain(dve, own)

            def weigh(n):
                h, d = n // 2, n % 2
                dve.wait_ge(scored, h + 1)
                if n >= 2:
                    dve.wait_ge(turn_done, n - 1)
                for j in range(NT):
                    t0, t1 = (x * P for x in SEEN[d][j])
                    bank, col = score_cols(j)
                    dve.wait_ge(weighed, 4 * n + j + 1)
                    nc.vector.scalar_tensor_tensor(out=prob[:, n % 2, j, t0:t1], in0=k.ps[:, bank, col + t0:col + t1],
                                                   scalar=SHIFT, in1=decay[:, j, t0:t1], op0=ALU.mult,
                                                   op1=ALU.mult).then_inc(probs, 1)

            def finish(n):
                h, d = n // 2, n % 2
                dve.wait_ge(turn_done, n + 1)
                out = k.ps[:, 5:7, :].rearrange("p b (i c) -> p (b i) c", i=2)
                den = k.den[:, n % 2, :]
                chain.link(nc.vector.tensor_tensor(den, out[:, :, DV], k.e_cols[:, :, 8 * d + h], ALU.max))
                chain.link(nc.vector.scalar_tensor_tensor(out=den, in0=out[:, :, DV], scalar=-1.0, in1=den,
                                                          op0=ALU.mult, op1=ALU.max))
                chain.link(nc.vector.reciprocal(den, den))
                if n >= 2:
                    dve.wait_ge(added, n // 2)
                nc.vector.tensor_tensor(part[:, d, :].rearrange("p (i c) -> p i c", i=NT), out[:, :, 0:DV],
                                        den.unsqueeze(2).to_broadcast([P, NT, DV]), ALU.mult).then_inc(summed, 1)

            for n in range(turns):
                weigh(n)
                if n:
                    finish(n - 1)
            finish(turns - 1)

        @block.gpsimd
        def _(pool):
            def add(h):
                pool.wait_ge(summed, 2 * h + 2)
                hv = k.tok[:, :, h * DV:(h + 1) * DV]
                pool.tensor_tensor(hv, part[:, 0, :].rearrange("p (i c) -> p i c", i=NT),
                                   part[:, 1, :].rearrange("p (i c) -> p i c", i=NT), ALU.add).then_inc(added, 1)

            for n in range(turns):
                d = n % 2
                pool.wait_ge(probs, 4 * n + 4)
                flat = k.u_area[:, d * NT * T:(d + 1) * NT * T]
                diag = bass.AP(flat.tensor, flat.offset, [list(flat.ap[0]), [T + P, NT], [1, P]])
                sign = 1 if d == 0 else -1
                pool.affine_select(out=diag, in_=diag, compare_op=ALU.is_ge, fill=0.0, base=0,
                                   pattern=[[0, NT], [sign, P]], channel_multiplier=-sign).then_inc(masked, 1)
                if d == 1 and n > 1:
                    add(n // 2 - 1)
            add(HEADS - 1)



def mixer_out(k, name, unit, tiles, gain0, gate_of, column_major):
    nc, s, u0 = k.nc, k.stream, k.plan[unit]
    n_t = len(tiles)
    t0 = tiles[0]
    squared, rooted, normed = k.sem(name + "_hsq"), k.sem(name + "_hroot"), k.sem(name + "_hnormed")
    turned, cols_copied, own = k.sem(name + "_hturned"), k.sem(name + "_hcols"), k.sem(name + "_hown")
    r = residual_sems(k, name + "_res", lambda i, half: 4 * half + i,
                      lambda i, half: (n_t if half == 0 else n_t + 1 + i - t0))
    s.release = {u0: (r.ready, n_t), u0 + 1: (r.ready, 2 * n_t)}
    width = n_t * P
    col0 = t0 * P
    sums = k.head_sum[:, 0:n_t * HEADS]
    h_cols = k.u_area.rearrange("p (c t) -> p c t", c=KD)

    with nc.Block() as block:

        @block.sync
        def _(sp):
            s.send(sp, u0 + 2 + RING)

        @block.scalar
        def _(act):
            for n, i in enumerate(tiles):
                nc.scalar.activation(k.sq[:, n, :], k.tok[:, i, :], ACT.Square).then_inc(squared, 1)
            act.wait_ge(own, 1)
            nc.scalar.activation(sums, sums, ACT.Sqrt, bias=k.eps[:, 0:1], scale=1.0 / DV).then_inc(rooted, 1)
            residual_scalar(k, act, r, tiles, True)

        @block.vector
        def _(dve):
            dve.wait_ge(squared, n_t)
            nc.vector.tensor_reduce(out=sums, in_=k.sq[:, 0:n_t, :].rearrange("p i (h c) -> p (i h) c", h=HEADS),
                                    op=ALU.add, axis=AX.X).then_inc(own, 1)
            dve.wait_ge(rooted, 1)
            nc.vector.reciprocal(sums, sums).then_inc(own, 1)
            dve.wait_ge(own, 2)
            for n, i in enumerate(tiles):
                nc.vector.tensor_tensor(k.tok[:, i, :].rearrange("p (h c) -> p h c", h=HEADS),
                                        k.tok[:, i, :].rearrange("p (h c) -> p h c", h=HEADS),
                                        sums[:, n * HEADS:(n + 1) * HEADS].unsqueeze(2).to_broadcast([P, HEADS, DV]),
                                        ALU.mult).then_inc(normed, 1)
            for h in range(HEADS):
                dve.wait_ge(turned, h + 1)
                src, gate, dst = k.ps[:, 4 + h % 4, 0:width], gate_of(h), h_cols[:, h, col0:col0 + width]
                if column_major:
                    src = src.rearrange("p (w r) -> p r w", r=GRID_H)
                    gate = gate.rearrange("p (w r) -> p r w", r=GRID_H)
                    dst = dst.rearrange("p (r w) -> p r w", r=GRID_H)
                nc.vector.scalar_tensor_tensor(out=dst, in0=src, scalar=k.vcol[:, gain0 + h:gain0 + h + 1], in1=gate,
                                               op0=ALU.mult, op1=ALU.mult).then_inc(cols_copied, 1)
            residual_vector(k, dve, r, tiles, 0, True)

        @block.tensor
        def _(pe):
            def turn(h):
                if h >= 4:
                    pe.wait_ge(cols_copied, h - 3)
                for n, i in enumerate(tiles):
                    last = nc.tensor.transpose(k.ps[:, 4 + h % 4, n * P:(n + 1) * P], k.tok[:, i, h * DV:(h + 1) * DV],
                                               k.ident[:, :])
                last.then_inc(turned, 1)

            pe.wait_ge(normed, n_t)
            for h in range(3):
                turn(h)
            s.arrived(pe, u0)
            w = rows_of(HALF)(s.slot(u0))
            for h in range(HEADS):
                if h + 3 < HEADS:
                    turn(h + 3)
                pe.wait_ge(cols_copied, h + 1)
                for i in tiles:
                    last = nc.tensor.matmul(k.ps[:, i, :], h_cols[:, h, i * P:(i + 1) * P], w[:, h, :],
                                            start=(h == 0), stop=(h == HEADS - 1))
                    if h == HEADS - 1:
                        last.then_inc(r.ready, 1)
            s.arrived(pe, u0 + 1)
            w = rows_of(HALF)(s.slot(u0 + 1))
            for i in tiles:
                for h in range(HEADS):
                    last = nc.tensor.matmul(k.ps[:, 4 + i, :], h_cols[:, h, i * P:(i + 1) * P], w[:, h, :],
                                            start=(h == 0), stop=(h == HEADS - 1))
                last.then_inc(r.ready, 1)



def feed_forward(k):
    nc, s, u0, v0 = k.nc, k.stream, k.plan["f_up"], k.plan["f_down"]
    PAIRS = 4
    gate_ready, up_ready, silu_ready, pair_free = (k.sem("f_" + n) for n in ("gate_ready", "up_ready", "silu_ready", "pair_free"))
    down_used = k.sem("f_down_used")
    r = residual_sems(k, "f_res", lambda i, half: 2 * i + half, lambda i, half: 2 * i + half + 1)
    silu = k.ex[:, 0:PAIRS * HALF].rearrange("p (b t) -> p b t", b=PAIRS)
    up_units = v0 - u0
    loops = up_units // RING
    per = 2 * RING
    down_units = -(-FC // 4)
    s.release = {u0 + n: (up_ready, 2 * n + 2) for n in range(up_units)}
    s.release.update({v0 + n: (down_used, n + 1) for n in range(down_units - 1)})
    s.release[v0 + down_units - 1] = (r.ready, 2 * NT)

    with nc.Block() as block:

        @block.sync
        def _(sp):
            s.send(sp, v0 + down_units + RING)

        @block.tensor
        def _(pe):
            def up_unit(n, turn, first):
                pe.wait_ge(s.loaded[n % RING], s.value[n] + 32 * turn)
                w = s.slot(n)[:, 0:SLOT].rearrange("p (k s n) -> p k s n", k=KD, s=2)
                for q in range(2):
                    pair = (2 * (n - u0) + q) % PAIRS
                    pe.wait_ge(pair_free, first + q + 1)
                    for side, ready in ((0, gate_ready), (1, up_ready)):
                        for c in range(KD):
                            last = nc.tensor.matmul(k.ps[:, 2 * pair + side, :], w[:, c, side, q * P:(q + 1) * P],
                                                    k.u_cols[:, c, :], start=(c == 0), stop=(c == KD - 1))
                        last.then_inc(ready, 1)

            with pe.Fori(0, loops) as turn:
                for b in range(RING):
                    up_unit(u0 + b, turn, turn * per + 2 * b)
            for b in range(loops * RING, up_units):
                up_unit(u0 + b, 0, 2 * b)
            pe.wait_ge(pair_free, FC + PAIRS)
            for n in range(down_units):
                s.arrived(pe, v0 + n)
                m = min(4, FC - 4 * n)
                w = s.slot(v0 + n)[:, 0:m * D].rearrange("p (f n) -> p f n", f=m)
                for q in range(m):
                    f = 4 * n + q
                    for i in range(NT):
                        for half in range(2):
                            last = nc.tensor.matmul(k.ps[:, 2 * i + half, :], k.hidden[:, f, i * P:(i + 1) * P],
                                                    w[:, q, half * HALF:(half + 1) * HALF], start=(f == 0), stop=(f == FC - 1))
                            if f == FC - 1:
                                last.then_inc(r.ready, 1)
                if n < down_units - 1:
                    last.then_inc(down_used, 1)

        @block.scalar
        def _(act):
            def chunk(b, f):
                act.wait_ge(gate_ready, f + 1)
                act.wait_ge(pair_free, f + 1)
                nc.scalar.activation(silu[:, b % PAIRS, :], k.ps[:, 2 * (b % PAIRS), :], ACT.Silu).then_inc(silu_ready, 1)

            with act.Fori(0, loops) as turn:
                for b in range(per):
                    chunk(b, turn * per + b)
            for b in range(loops * per, FC):
                chunk(b, b)
            residual_scalar(k, act, r, range(NT), True)

        @block.vector
        def _(dve):
            dve.nop().then_inc(pair_free, PAIRS)

            def chunk(b, f, place):
                dve.wait_ge(up_ready, f + 1)
                dve.wait_ge(silu_ready, f + 1)
                nc.vector.tensor_tensor(place, silu[:, b % PAIRS, :], k.ps[:, 2 * (b % PAIRS) + 1, :],
                                        ALU.mult).then_inc(pair_free, 1)

            flat = k.big[:, 0:FC * T]
            with dve.Fori(0, loops) as turn:
                for b in range(per):
                    chunk(b, turn * per + b, flat[:, bass.ds(turn * (per * T) + b * T, T)])
            for b in range(loops * per, FC):
                chunk(b, b, flat[:, b * T:(b + 1) * T])
            residual_vector(k, dve, r, range(NT), 1, True)



def hgrn_in(k):
    nc, s, u0 = k.nc, k.stream, k.plan["h_in"]
    ready, copied_a, copied_v = k.sem("hi_ready"), k.sem("hi_copied_a"), k.sem("hi_copied_v")
    row_sig, lb_in, lb_row, f_made, act_own, own = (k.sem("hi_" + n) for n in ("row_sig", "lb_in", "lb_row", "f_made", "act_own", "own"))
    raised = k.sem("hi_raised")
    lb = k.tok[:, 2:4, :].rearrange("p a n -> p (a n)")
    bias_row = k.resid[0:1, 0:2, :].rearrange("p a n -> p (a n)")
    units = 10
    jobs = []
    for u in range(4):
        jobs += [(u, "f_row", i) for i in range(2)] + [(u, "f_col", i) for i in range(4)]
    jobs += [(u, "v", i) for u in (4, 5) for i in range(4)]
    jobs += [(u, "q", i) for u in (6, 7) for i in range(4)]
    jobs += [(u, "g", i) for u in (8, 9) for i in range(4)]
    last_of = {u: max(n for n, j in enumerate(jobs) if j[0] == u) for u in range(units)}
    s.release = {u0 + u: (ready, last_of[u] + 1) for u in range(units)}
    by_act = [j[1] != "v" and j[1] != "q" for j in jobs]
    BANKS = 6

    def freed(n):
        return (copied_a, sum(by_act[:n + 1])) if by_act[n] else (copied_v, n + 1 - sum(by_act[:n + 1]))

    with nc.Block() as block:

        @block.sync
        def _(sp):
            sp.dma_start(bias_row, k.a["h_b_f"].rearrange("o a n -> o (a n)")).then_inc(lb_in, 16)
            sp.dma_start(lb, k.a["h_lb_raw"].rearrange("o a n -> o (a n)").to_broadcast([P, 2 * D])).then_inc(lb_in, 16)
            s.send(sp, u0 + units + RING)

        @block.tensor
        def _(pe):
            pe.wait_ge(lb_in, 32)
            for n, (u, kind, i) in enumerate(jobs):
                if n == 0 or jobs[n - 1][0] != u:
                    s.arrived(pe, u0 + u)
                w = rows_of(HALF)(s.slot(u0 + u))
                bank = n % BANKS
                if n >= BANKS:
                    pe.wait_ge(*freed(n - BANKS))
                rows = kind in ("f_row", "v")
                width = HALF if rows else LAT
                for c in range(KD):
                    if rows:
                        lhs, rhs = k.u_cols[:, c, i * P:(i + 1) * P], w[:, c, :]
                    else:
                        lhs, rhs = w[:, c, i * P:(i + 1) * P], k.u_cols[:, c, CTX:T]
                    last = nc.tensor.matmul(k.ps[:, bank, 0:width], lhs, rhs, start=(c == 0),
                                            stop=(c == KD - 1 and kind != "f_row"))
                if kind == "f_row":
                    last = nc.tensor.matmul(k.ps[:, bank, :], k.ones[0:1, :], bias_row[0:1, u * HALF:(u + 1) * HALF], start=False, stop=True)
                last.then_inc(ready, 1)

        @block.scalar
        def _(act):
            act.wait_ge(lb_row, 1)
            nc.scalar.activation(lb, lb, ACT.Exp).then_inc(lb_row, 1)
            for n, (u, kind, i) in enumerate(jobs):
                if not by_act[n]:
                    continue
                act.wait_ge(ready, n + 1)
                if kind == "f_row":
                    dst = k.f_rows[:, i, u * HALF:(u + 1) * HALF]
                    nc.scalar.activation(dst, k.ps[:, n % BANKS, :], ACT.Sigmoid).then_inc(copied_a, 1)
                elif kind == "f_col":
                    c = (u % 2) * 4 + i
                    col = (u // 2) * KD + c
                    nc.scalar.activation(k.f_cols[:, u // 2, c, :], k.ps[:, n % BANKS, 0:LAT], ACT.Sigmoid,
                                         bias=k.vcol[:, 104 + col:105 + col]).then_inc(copied_a, 1)
                else:
                    c = (u - 8) * 4 + i
                    nc.scalar.activation(k.g_cols(c), k.ps[:, n % BANKS, 0:LAT], ACT.Sigmoid).then_inc(copied_a, 1)
            act.wait_ge(f_made, 16)
            for i in range(2):
                nc.scalar.activation(k.f_rows[:, i, :], k.f_rows[:, i, :], ACT.Ln)

        @block.gpsimd
        def _(pool):
            pool.wait_ge(lb_in, 32)
            pool.tensor_tensor(lb, lb, lb, ALU.subtract).then_inc(lb_row, 1)

        @block.vector
        def _(dve):
            chain = Chain(dve, own)
            dve.wait_ge(lb_row, 2)
            inverse = k.k_rows[:, 0, :]
            chain.link(nc.vector.reciprocal(inverse, lb))
            chain.link(nc.vector.tensor_tensor(inverse, lb, inverse, ALU.mult))
            chain.link(nc.vector.tensor_tensor(lb, inverse, inverse, ALU.subtract))
            for n, (u, kind, i) in enumerate(jobs):
                if kind == "f_row":
                    dve.wait_ge(*freed(n))
                    f = k.f_rows[:, i, u * HALF:(u + 1) * HALF]
                    kk = k.k_rows[:, i, u * HALF:(u + 1) * HALF]
                    chain.link(nc.vector.scalar_tensor_tensor(out=kk, in0=f, scalar=-1.0, in1=lb[:, u * HALF:(u + 1) * HALF],
                                                              op0=ALU.add, op1=ALU.mult))
                    chain.link(nc.vector.tensor_tensor(f, f, kk, ALU.subtract))
                    chain.link(nc.vector.tensor_scalar(kk, f, -1.0, 1.0, ALU.mult, ALU.add))
                    nc.vector.tensor_scalar(f, f, 2.0 ** -63, None, ALU.max).then_inc(f_made, 2)
                elif kind == "f_col":
                    dve.wait_ge(*freed(n))
                    c = (u % 2) * 4 + i
                    col = (u // 2) * KD + c
                    f = k.f_cols[:, u // 2, c, :]
                    nc.vector.tensor_scalar(f, f, k.lb_rest[:, col:col + 1], k.lb_col[:, col:col + 1], ALU.mult, ALU.add)
                elif kind == "v":
                    dve.wait_ge(ready, n + 1)
                    nc.vector.tensor_copy(k.v_rows[:, i, (u - 4) * HALF:(u - 3) * HALF], k.ps[:, n % BANKS, :]).then_inc(copied_v, 1)
                elif kind == "q":
                    dve.wait_ge(ready, n + 1)
                    nc.vector.tensor_copy(k.q_cols[:, (u - 6) * 4 + i, :], k.ps[:, n % BANKS, 0:LAT]).then_inc(copied_v, 1)



def hgrn_state(k):
    nc = k.nc
    summed, decayed, scaled, stated, copied = (k.sem("hs_" + n) for n in ("summed", "decayed", "scaled", "stated", "copied"))
    rest = k.sem("hs_rest")
    decay = k.junk.rearrange("p (b n) -> p b n", b=2)
    jobs = [(d, half, i) for d in range(2) for half in range(2) for i in range(2)]

    with nc.Block() as block:

        @block.tensor
        def _(pe):
            for n, (d, half, i) in enumerate(jobs):
                if n >= 4:
                    pe.wait_ge(decayed, n - 3)
                cols = slice(d * D + half * HALF, d * D + (half + 1) * HALF)
                own = (k.after, k.before)[d]
                other = (i == 0) if d == 0 else (i == 1)
                last = nc.tensor.matmul(k.ps[:, n % 4, :], own[:, :], k.f_rows[:, i, cols], start=True, stop=not other)
                if other:
                    last = nc.tensor.matmul(k.ps[:, n % 4, :], k.ones[:, :], k.f_rows[:, 1 - i, cols], start=False, stop=True)
                last.then_inc(summed, 1)
            for g in range(4):
                d, half = g // 2, g % 2
                pe.wait_ge(scaled, 2 * g + 2)
                for q in range(4):
                    h = half * 4 + q
                    for i in range(2):
                        last = nc.tensor.matmul(k.ps[:, 4 + g, q * P:(q + 1) * P],
                                                k.k_rows[:, i, d * D + h * P:d * D + (h + 1) * P],
                                                k.v_rows[:, i, h * P:(h + 1) * P], start=(i == 0), stop=(i == 1))
                last.then_inc(stated, 1)

        @block.scalar
        def _(act):
            for n in range(len(jobs)):
                act.wait_ge(summed, n + 1)
                if n >= 2:
                    act.wait_ge(scaled, n - 1)
                nc.scalar.activation(decay[:, n % 2, :], k.ps[:, n % 4, :], ACT.Exp).then_inc(decayed, 1)
            for g in range(4):
                act.wait_ge(stated, g + 1)
                nc.scalar.activation(k.state[:, 4 * g:4 * g + 4, :], k.ps[:, 4 + g, :].rearrange("p (h c) -> p h c", h=4), ACT.Copy)

        @block.vector
        def _(dve):
            for n, (d, half, i) in enumerate(jobs):
                cols = slice(d * D + half * HALF, d * D + (half + 1) * HALF)
                dve.wait_ge(decayed, n + 1)
                nc.vector.tensor_tensor(k.k_rows[:, i, cols], k.k_rows[:, i, cols], decay[:, n % 2, :], ALU.mult).then_inc(scaled, 1)



def hgrn_pairs(k):
    nc = k.nc
    q_made, k_made, q_grown, k_grown, ends_made = (k.sem("hp_" + n) for n in ("q_made", "k_made", "q_grown", "k_grown", "ends_made"))
    paired, taken, sum_made = k.sem("hp_paired"), k.sem("hp_taken"), k.sem("hp_sum_made")
    q_f, k_f, ends = k.q_fac, k.k_fac, k.f_cols
    G = 4

    def halves(x, d, g, size):
        v = x[:, d, G * g:G * g + G, :].rearrange("p h (b two l) -> p (h b) two l", two=2, l=size)
        return v[:, :, 0, :], v[:, :, 1, :]

    def end_of(d, g, size):
        v = ends[:, d, G * g:G * g + G, :].rearrange("p h (b two l) -> p (h b) two l", two=2, l=size)
        return v[:, :, 0, 0:1], v[:, :, 1, 0:1]

    def cut(x, size, side):
        return x.rearrange("p (b two l) -> p b two l", two=2, l=size)[:, :, side, :]

    n_blocks = lambda size: G * LAT // (2 * size)

    with nc.Block() as block:

        @block.tensor
        def _(pe):
            for level in range(-1, LEVELS + 1):
                for g in range(2):
                    n = (level + 1) * 2 + g
                    if level < 1:
                        pe.wait_ge(q_made, 2 * g + 2)
                        pe.wait_ge(sum_made, g + 1)
                    else:
                        pe.wait_ge(q_grown, 2 * (n - 3))
                        pe.wait_ge(k_grown, 2 * (n - 3))
                    if n >= 4:
                        pe.wait_ge(taken, 2 * (n - 3))
                    for i in range(2):
                        bank = (n % 4) * 2 + i
                        for q in range(G):
                            h = G * g + q
                            out = k.ps[:, bank, q * P:(q + 1) * P]
                            t = slice(i * P, (i + 1) * P)
                            if level < 0:
                                last = nc.tensor.matmul(out, k.k_sum[:, h, t], k.q_cols[:, h, t], start=True, stop=True)
                            elif level < LEVELS:
                                size = 2 ** level
                                for d, side in ((0, 1), (1, 0)):
                                    last = nc.tensor.matmul(cut(out, size, side), k_f[:, d, h, t], cut(q_f[:, d, h, t], size, side),
                                                            start=True, stop=True)
                            else:
                                last = nc.tensor.matmul(out, k_f[:, i, h, t], q_f[:, i, h, (1 - i) * P:(2 - i) * P],
                                                        start=True, stop=True)
                        last.then_inc(paired, 1)

        @block.vector
        def _(dve):
            for g in range(2):
                for d in range(2):
                    nc.vector.tensor_tensor(q_f[:, d, G * g:G * g + G, :], k.q_cols[:, G * g:G * g + G, :],
                                            ends[:, d, G * g:G * g + G, :], ALU.mult).then_inc(q_made, 1)

            def take(level, g):
                n = (level + 1) * 2 + g
                for i in range(2):
                    bank = (n % 4) * 2 + i
                    dve.wait_ge(paired, 2 * n + i + 1)
                    src = k.ps[:, bank, :].rearrange("p (h t) -> p h t", h=G)
                    near, cross = k.pair_near[:, g, i, :, :], k.pair_cross[:, g, i, :, :]
                    if level < 0:
                        nc.vector.tensor_tensor(near, src, k.ident[:, :].unsqueeze(1).to_broadcast([P, G, P]),
                                                ALU.mult).then_inc(taken, 1)
                    elif level < LEVELS:
                        dve.wait_ge(taken, 2 * (n - 2) + i + 1)
                        nc.vector.copy_predicated(near, k.level_mask[:, level, :].unsqueeze(1).to_broadcast([P, G, P]),
                                                  src).then_inc(taken, 1)
                    else:
                        nc.vector.tensor_copy(cross, src).then_inc(taken, 1)

            for level in range(-1, LEVELS + 1):
                for g in range(2):
                    take(level, g)
                    if level >= 0:
                        size = 2 ** level
                        if level:
                            dve.wait_ge(q_grown, 2 * ((level - 1) * 2 + g + 1))
                            dve.wait_ge(ends_made, 4 * ((level - 1) * 2 + g + 1))
                        else:
                            dve.wait_ge(q_made, 4)
                        for d in range(2):
                            side = halves(q_f, d, g, size)[1 - d]
                            end = end_of(d, g, size)[d]
                            nc.vector.tensor_tensor(side, side, end.to_broadcast([P, n_blocks(size), size]),
                                                    ALU.mult).then_inc(q_grown, 1)

        @block.gpsimd
        def _(pool):
            for g in range(2):
                for d in range(2):
                    pool.tensor_scalar(k_f[:, d, G * g:G * g + G, :], ends[:, d, G * g:G * g + G, :], -1.0, 1.0,
                                       ALU.mult, ALU.add).then_inc(k_made, 1)
                pool.wait_ge(k_made, 2 * g + 2)
                pool.tensor_tensor(k.k_sum[:, G * g:G * g + G, :], k_f[:, 0, G * g:G * g + G, :],
                                   k_f[:, 1, G * g:G * g + G, :], ALU.add).then_inc(sum_made, 1)
            for level in range(LEVELS):
                size = 2 ** level
                for g in range(2):
                    n = (level + 1) * 2 + g
                    turn = level * 2 + g
                    pool.wait_ge(paired, 2 * n + 2)
                    if level:
                        pool.wait_ge(k_grown, 2 * ((level - 1) * 2 + g + 1))
                        pool.wait_ge(ends_made, 4 * ((level - 1) * 2 + g + 1))
                    for d in range(2):
                        side = halves(k_f, d, g, size)[d]
                        end = end_of(d, g, size)[1 - d]
                        pool.tensor_tensor(side, side, end.to_broadcast([P, n_blocks(size), size]),
                                           ALU.mult).then_inc(k_grown, 1)
                    pool.wait_ge(q_grown, 2 * (turn + 1))
                    pool.wait_ge(k_grown, 2 * (turn + 1))
                    for d in range(2):
                        left, right = end_of(d, g, size)
                        pool.tensor_tensor(left, left, right, ALU.mult).then_inc(ends_made, 2)



def hgrn_values(k):
    nc = k.nc
    ready = k.sem("hv_ready")
    with nc.Block() as block:

        @block.tensor
        def _(pe):
            for i in range(2):
                for g in range(2):
                    for q in range(4):
                        h = 4 * g + q
                        out = k.ps[:, 2 * i + g, q * P:(q + 1) * P]
                        v = [k.v_rows[:, 2 + j, h * DV:(h + 1) * DV] for j in range(2)]
                        t = slice(i * P, (i + 1) * P)
                        nc.tensor.matmul(out, k.pair_near[:, g, i, q, :], v[i], start=True, stop=False)
                        nc.tensor.matmul(out, k.pair_cross[:, g, 1 - i, q, :], v[1 - i], start=False, stop=False)
                        nc.tensor.matmul(out, k.q_fac[:, 0, h, t], k.state[:, h, :], start=False, stop=False)
                        last = nc.tensor.matmul(out, k.q_fac[:, 1, h, t], k.state[:, 8 + h, :], start=False, stop=True)
                    last.then_inc(ready, 1)

        @block.vector
        def _(dve):
            for n in range(0, 4, 2):
                dve.wait_ge(ready, n + 1)
                nc.vector.tensor_copy(k.tok[:, 2 + n // 2, (n % 2) * HALF:(n % 2 + 1) * HALF], k.ps[:, n, :])

        @block.scalar
        def _(act):
            for n in range(1, 4, 2):
                act.wait_ge(ready, n + 1)
                nc.scalar.activation(k.tok[:, 2 + n // 2, (n % 2) * HALF:(n % 2 + 1) * HALF], k.ps[:, n, :], ACT.Copy)



def routing(k):
    nc = k.nc
    logits_ready, own, diff, expd, chosen, placed = (k.sem("r_" + n) for n in ("logits_ready", "own", "diff", "expd", "chosen", "placed"))
    r = k.route
    L, EQ, CAND, OH1, OH2, L2, COMB, SEL = (r[:, n, :, :] for n in range(8))
    V1, V2, IDX, W1, W2, EX = (r[:, 8 + n // 4, :, 2 * (n % 4):2 * (n % 4) + 1] for n in range(6))
    per = lambda v: v.to_broadcast([P, 2, EXPERTS])

    with nc.Block() as block:

        @block.tensor
        def _(pe):
            for i in range(2):
                for c in range(KD):
                    nc.tensor.matmul(k.ps[:, 0, i * 8:i * 8 + 8], k.u_cols[:, c, CTX + i * P:CTX + (i + 1) * P],
                                     k.w_router[:, c, :], start=(c == 0), stop=False)
                last = nc.tensor.matmul(k.ps[:, 0, i * 8:i * 8 + 8], k.ones[0:1, :], k.b_router[0:1, :], start=False, stop=True)
            last.then_inc(logits_ready, 1)
            pe.wait_ge(chosen, 1)
            nc.tensor.matmul(k.ps[:, 1, 0:8], k.before[:, :], SEL[:, 0, :], start=True, stop=True)
            nc.tensor.matmul(k.ps[:, 1, 8:16], k.ones[:, :], SEL[:, 0, :], start=True, stop=False)
            nc.tensor.matmul(k.ps[:, 1, 8:16], k.before[:, :], SEL[:, 1, :], start=False, stop=True)
            nc.tensor.matmul(k.ps[:, 1, 16:24], k.ones[:, :], SEL[:, 0, :], start=True, stop=False)
            nc.tensor.matmul(k.ps[:, 1, 16:24], k.ones[:, :], SEL[:, 1, :], start=False, stop=True).then_inc(placed, 1)

        @block.scalar
        def _(act):
            act.wait_ge(diff, 1)
            nc.scalar.activation(EX, EX, ACT.Exp).then_inc(expd, 1)

        @block.gpsimd
        def _(pool):
            pool.memset(k.acc[:, :, :], 0.0)

        @block.vector
        def _(dve):
            chain = Chain(dve, own)
            dve.wait_ge(logits_ready, 1)
            chain.link(nc.vector.tensor_copy(L, k.ps[:, 0, 0:16].rearrange("p (i e) -> p i e", i=2)))

            def pick(logits, value, onehot):
                chain.link(nc.vector.tensor_reduce(out=value, in_=logits, op=ALU.max, axis=AX.X))
                chain.link(nc.vector.tensor_tensor(EQ, logits, per(value), ALU.is_equal))
                chain.link(nc.vector.scalar_tensor_tensor(out=CAND, in0=EQ, scalar=-8.0, in1=k.expert_no[:, :, :],
                                                          op0=ALU.mult, op1=ALU.add))
                chain.link(nc.vector.tensor_reduce(out=IDX, in_=CAND, op=ALU.min, axis=AX.X))
                chain.link(nc.vector.tensor_tensor(onehot, CAND, per(IDX), ALU.is_equal))

            pick(L, V1, OH1)
            chain.link(nc.vector.scalar_tensor_tensor(out=L2, in0=OH1, scalar=-3.0e38, in1=L, op0=ALU.mult, op1=ALU.add))
            pick(L2, V2, OH2)
            chain.link(nc.vector.tensor_tensor(SEL, OH1, OH2, ALU.add))
            nc.vector.tensor_tensor(EX, V2, V1, ALU.subtract).then_inc(diff, 1)
            dve.nop().then_inc(chosen, 1)
            dve.wait_ge(expd, 1)
            chain.link(nc.vector.tensor_scalar(W2, EX, 1.0, None, ALU.add))
            chain.link(nc.vector.reciprocal(W1, W2))
            chain.link(nc.vector.tensor_tensor(W2, EX, W1, ALU.mult))
            chain.link(nc.vector.tensor_tensor(OH1, OH1, per(W1), ALU.mult))
            chain.link(nc.vector.tensor_tensor(OH2, OH2, per(W2), ALU.mult))
            nc.vector.memset(k.place[:, :, EXPERTS:EXPERTS + 1], -1.0)
            nc.vector.tensor_tensor(k.comb[:, :, :], OH1, OH2, ALU.add)
            dve.wait_ge(placed, 1)
            chain.link(nc.vector.scalar_tensor_tensor(out=EQ, in0=k.ps[:, 1, 0:16].rearrange("p (i e) -> p i e", i=2),
                                                      scalar=1.0, in1=SEL, op0=ALU.add, op1=ALU.mult))
            nc.vector.tensor_scalar(k.place[:, :, 0:EXPERTS], EQ, -1.0, None, ALU.add)
            chain.link(nc.vector.tensor_reduce(out=V1[:, 0, :], in_=k.ps[:, 1, 16:24], op=ALU.max, axis=AX.X))
            nc.vector.tensor_scalar(k.passes[:, 0:1], V1[:, 0, :], float(P), 1.0, ALU.is_gt, ALU.add)



def experts(k):
    nc, a = k.nc, k.a
    S = Names()
    S.freed, S.silu_ready, S.hid_done = k.sem("e_freed"), k.sem("e_silu_ready"), k.sem("e_hid_done")
    S.places_ready, S.gathered, S.list_a, S.list_v = (k.sem("e_" + n) for n in ("places_ready", "gathered", "list_a", "list_v"))
    S.wplaces_ready, S.wturned, S.wcopied = (k.sem("e_" + n) for n in ("wplaces_ready", "wturned", "wcopied"))
    S.hturned, S.hcopied, S.y_copied = k.sem("e_hturned"), k.sem("e_hcopied"), k.sem("e_y_copied")
    S.scattered, S.added = k.sem("e_scattered"), k.sem("e_added")
    loaded = [k.sem(f"e_loaded{i}") for i in range(E_RING)]
    HG = -(-FC // 4)
    NQ = D // E_Q
    per_slot = E_UNITS // E_RING
    Y0 = 2 * E_TILES

    def slot(j):
        return k.e_ring[:, (j % E_RING) * E_SLOT:(j % E_RING + 1) * E_SLOT]

    def passes(engine):
        return engine.value_load(k.passes[0:1, 0:1], min_val=1, max_val=2)

    with nc.Block() as block:

        @block.sync
        def _(sp):
            n = passes(sp)
            with sp.Fori(0, n) as ps_:
                with sp.Fori(0, EXPERTS) as e:
                    it = sp.snap(ps_ * EXPERTS + e)
                    gu = a["e_w_gu"][0, e]
                    dn = a["e_w_down"][0, e]
                    for j in range(E_UNITS):
                        if j < Y0:
                            t, side = j // 2, j % 2
                            src = gu[:, side * FFN + t * E_N:side * FFN + (t + 1) * E_N].rearrange("(k p) n -> p k n", p=P)
                            dst = slot(j).rearrange("p (k n) -> p k n", k=KD)
                        else:
                            q, kh = (j - Y0) // 2, (j - Y0) % 2
                            src = dn[kh * E_KH * P:(kh + 1) * E_KH * P, q * E_Q:(q + 1) * E_Q].rearrange("(k p) n -> p k n", p=P)
                            dst = slot(j).rearrange("p (k n) -> p k n", k=E_KH)
                        need = sp.snap(it * E_UNITS + (j + 1))
                        sp.wait_ge(S.freed, need)
                        sp.dma_start(dst, src).then_inc(loaded[j % E_RING], 16)

        @block.tensor
        def _(pe):
            n = passes(pe)
            pe.nop().then_inc(S.freed, E_RING)

            def arrived(it, j):
                pe.wait_ge(loaded[j % E_RING], it * (16 * per_slot) + 16 * (j // E_RING + 1))

            def gather(m):
                pe.wait_ge(S.places_ready, m + 1)
                for c in range(KD):
                    for i in range(2):
                        last = nc.tensor.matmul(k.ps[:, 4 + c // 4, (c % 4) * P:(c % 4 + 1) * P],
                                                k.tok[:, 2 + i, c * P:(c + 1) * P], k.places[:, i, :],
                                                start=(i == 0), stop=(i == 1))
                last.then_inc(S.gathered, 1)

            pe.nop().then_inc(S.gathered, 1)
            pe.nop().then_inc(S.wturned, 1)
            with pe.Fori(0, n) as ps_:
                pe.wait_ge(S.y_copied, ps_ * (EXPERTS * NQ) + 1)
                gather(ps_ * 9)
                with pe.Fori(0, EXPERTS) as e:
                    it = ps_ * EXPERTS + e
                    pe.wait_ge(S.list_a, ps_ * 9 + e + 1)
                    pe.wait_ge(S.list_v, ps_ * 9 + e + 1)
                    pe.wait_ge(S.added, it * 4 + 1)
                    for t in range(E_TILES):
                        pe.wait_ge(S.hid_done, it * E_TILES + t + 1)
                        for side in range(2):
                            arrived(it, 2 * t + side)
                            w = slot(2 * t + side).rearrange("p (k n) -> p k n", k=KD)
                            for c in range(KD):
                                last = nc.tensor.matmul(k.ps[:, 2 * (t % 2) + side, 0:E_N], k.list_cols[:, c, :], w[:, c, :],
                                                        start=(c == 0), stop=(c == KD - 1))
                            last.then_inc(S.freed, 1)
                    pe.wait_ge(S.y_copied, it * NQ + 1)
                    gather(ps_ * 9 + e + 1)
                    pe.wait_ge(S.wplaces_ready, it + 1)
                    pe.wait_ge(S.hcopied, it * HG + 1)
                    for i in range(2):
                        last = nc.tensor.transpose(k.ps[:, 6, i * P:(i + 1) * P], k.wplaces[:, i, :], k.ident[:, :])
                    last.then_inc(S.wturned, 1)
                    pe.wait_ge(S.hid_done, it * E_TILES + E_TILES + 2)
                    for g in range(HG):
                        if g == 1:
                            pe.wait_ge(S.wcopied, it + 1)
                        elif g >= 2:
                            pe.wait_ge(S.hcopied, it * HG + g)
                        for q in range(min(4, FC - 4 * g)):
                            f = 4 * g + q
                            last = nc.tensor.transpose(k.ps[:, 7 - g % 2, q * P:(q + 1) * P], k.e_hid[:, f * P:(f + 1) * P],
                                                       k.ident[:, :])
                        last.then_inc(S.hturned, 1)
                    for q in range(NQ):
                        if q == 0:
                            pe.wait_ge(S.list_a, ps_ * 9 + e + 2)
                            pe.wait_ge(S.list_v, ps_ * 9 + e + 2)
                            pe.wait_ge(S.hcopied, it * HG + HG + 1)
                        if q >= 2:
                            pe.wait_ge(S.y_copied, it * NQ + q)
                        for kh in range(2):
                            j = Y0 + 2 * q + kh
                            arrived(it, j)
                            w = slot(j).rearrange("p (k n) -> p k n", k=E_KH)
                            for c in range(E_KH):
                                f = kh * E_KH + c
                                last = nc.tensor.matmul(k.ps[:, 4 + q % 2, 0:E_Q], k.e_hid_cols[:, f, :], w[:, c, :],
                                                        start=(f == 0), stop=(f == FC - 1))
                            last.then_inc(S.freed, 1)
                    for half in range(2):
                        pe.wait_ge(S.y_copied, it * NQ + 2 * half + 3)
                        for i in range(2):
                            nc.tensor.matmul(k.ps[:, 2 * half + i, :], k.wplace_cols[:, i * P:(i + 1) * P],
                                             k.e_y[:, half * HALF:(half + 1) * HALF], start=True, stop=True).then_inc(S.scattered, 1)

        def take_list(engine, m, banks_half, operation):
            engine.wait_ge(S.gathered, m + 2)
            for c in range(4 * banks_half, 4 * banks_half + 4):
                last = operation(k.list_cols[:, c, :], k.ps[:, 4 + banks_half, (c % 4) * P:(c % 4 + 1) * P],
                                 k.mod_scale[:, 1, c, 1:2], k.mod_cols[:, 3, c, 1:2])
            return last

        @block.scalar
        def _(act):
            n = passes(act)
            act.nop().then_inc(S.y_copied, 1)
            act.nop().then_inc(S.hcopied, 1)

            def take(m):
                take_list(act, m, 0, lambda out, src, scale, shift: nc.scalar.activation(
                    out, src, ACT.Identity, bias=shift, scale=scale)).then_inc(S.list_a, 1)

            with act.Fori(0, n) as ps_:
                take(ps_ * 9)
                with act.Fori(0, EXPERTS) as e:
                    it = ps_ * EXPERTS + e
                    for t in range(E_TILES):
                        act.wait_ge(S.freed, it * E_UNITS + (E_RING + 2 * t + 1))
                        act.wait_ge(S.hid_done, it * E_TILES + t + 1)
                        nc.scalar.activation(k.e_silu[:, t % 2, :], k.ps[:, 2 * (t % 2), 0:E_N], ACT.Silu).then_inc(S.silu_ready, 1)
                    take(ps_ * 9 + e + 1)
                    act.wait_ge(S.wturned, it + 2)
                    nc.scalar.activation(k.wplace_cols[:, :], k.ps[:, 6, 0:256], ACT.Copy).then_inc(S.wcopied, 1)
                    for g in range(HG):
                        m = min(4, FC - 4 * g)
                        act.wait_ge(S.hturned, it * HG + g + 1)
                        nc.scalar.activation(k.e_hid_cols[:, 4 * g:4 * g + m, :],
                                             k.ps[:, 7 - g % 2, 0:m * P].rearrange("p (f t) -> p f t", f=m), ACT.Copy).then_inc(S.hcopied, 1)
                    for q in range(NQ):
                        act.wait_ge(S.freed, it * E_UNITS + (E_RING + Y0 + 2 * q + 2))
                        nc.scalar.activation(k.e_y[:, q * E_Q:(q + 1) * E_Q], k.ps[:, 4 + q % 2, 0:E_Q], ACT.Copy).then_inc(S.y_copied, 1)

        @block.vector
        def _(dve):
            n = passes(dve)
            dve.nop().then_inc(S.hid_done, 2)
            dve.nop().then_inc(S.added, 1)

            def find(ps_, e, m):
                dve.wait_ge(S.gathered, m + 1)
                for i in range(2):
                    last = nc.vector.tensor_scalar(k.places[:, i, :], k.slot_no[:, bass.ds(ps_ * P, P)],
                                                   k.place[:, i, bass.ds(e, 1)], None, ALU.is_equal)
                last.then_inc(S.places_ready, 1)

            def take(m):
                take_list(dve, m, 1, lambda out, src, scale, shift: nc.vector.tensor_scalar(
                    out, src, scale, shift, ALU.mult, ALU.add)).then_inc(S.list_v, 1)

            with dve.Fori(0, n) as ps_:
                find(ps_, 0, ps_ * 9)
                take(ps_ * 9)
                with dve.Fori(0, EXPERTS) as e:
                    it = ps_ * EXPERTS + e
                    find(ps_, e + 1, ps_ * 9 + e + 1)
                    dve.wait_ge(S.wturned, it + 1)
                    for i in range(2):
                        last = nc.vector.tensor_scalar(k.wplaces[:, i, :], k.slot_no[:, bass.ds(ps_ * P, P)],
                                                       k.place[:, i, bass.ds(e, 1)], k.comb[:, i, bass.ds(e, 1)],
                                                       ALU.is_equal, ALU.mult)
                    last.then_inc(S.wplaces_ready, 1)
                    for t in range(E_TILES):
                        dve.wait_ge(S.freed, it * E_UNITS + (E_RING + 2 * t + 2))
                        dve.wait_ge(S.silu_ready, it * E_TILES + t + 1)
                        nc.vector.tensor_tensor(k.e_hid[:, t * E_N:(t + 1) * E_N], k.e_silu[:, t % 2, :],
                                                k.ps[:, 2 * (t % 2) + 1, 0:E_N], ALU.mult).then_inc(S.hid_done, 1)
                    take(ps_ * 9 + e + 1)
                    for half in range(2):
                        for i in range(2):
                            dve.wait_ge(S.scattered, it * 4 + 2 * half + i + 1)
                            part = k.acc[:, i, half * HALF:(half + 1) * HALF]
                            nc.vector.tensor_tensor(part, part, k.ps[:, 2 * half + i, :], ALU.add).then_inc(S.added, 1)


def finish(k):
    nc = k.nc
    r = residual_sems(k, "out_res", None, None)
    stored = k.sem("stored")
    with nc.Block() as block:

        @block.gpsimd
        def _(pool):
            for i in range(2):
                pool.tensor_copy(k.tok[:, 2 + i, :], k.acc[:, i, :]).then_inc(r.copied_a, 1)

        @block.scalar
        def _(act):
            act.wait_ge(r.copied_a, 2)
            residual_scalar(k, act, r, (2, 3), False)

        @block.vector
        def _(dve):
            dve.wait_ge(r.copied_a, 2)
            residual_vector(k, dve, r, (2, 3), 1, False)

        @block.sync
        def _(sp):
            for i in range(2):
                sp.wait_ge(r.added, i + 1)
                sp.dma_start(k.out[0, i * P:(i + 1) * P, :], k.resid[:, 2 + i, :]).then_inc(stored, 16)
            sp.wait_ge(stored, 32)



def hybrid_mlstm_hgrn2_moe(nc, a, out, stages=99):
    with ExitStack() as stack:
        def sb(name, shape, dtype=F32):
            return stack.enter_context(nc.sbuf_tensor(name, shape, dtype))

        stage_sems = []

        def sem(name):
            stage_sems.append(nc.alloc_semaphore(name))
            return stage_sems[-1]

        k = Names()
        k.nc, k.a, k.out, k.sem = nc, a, out, sem
        k.resid = sb("resid", [P, NT, D])
        k.u_area = sb("u_area", [P, KD * T])[:, :]
        k.u_cols = k.u_area.rearrange("p (c t) -> p c t", c=KD)
        k.tok = sb("tok", [P, NT, D])
        k.gate = sb("gate", [P, 2, 2, D])
        k.ring = sb("ring", [P, max(RING * SLOT, E_RING * E_SLOT)])
        k.ex = sb("ex", [P, 4096])[:, :]
        big_words = 2 * KD * T + NT * HEADS * VST
        k.big = sb("big", [P, big_words])[:, :]
        k.junk = sb("junk", [P, D])[:, :]
        k.qk = k.big[:, 0:KD * T].rearrange("p (c t) -> p c t", c=KD)
        k.o_cols = k.big[:, KD * T:2 * KD * T].rearrange("p (c t) -> p c t", c=KD)
        k.vaug = k.big[:, 2 * KD * T:big_words].rearrange("p (i h c) -> p i h c", i=NT, h=HEADS)
        k.sq = k.big[:, 2 * KD * T:2 * KD * T + NT * D].rearrange("p (i n) -> p i n", i=NT)
        k.hidden = k.big[:, 0:FC * T].rearrange("p (f t) -> p f t", f=FC)
        k.f_rows = k.big[:, 0:4 * D].rearrange("p (i n) -> p i n", i=2)
        k.k_rows = k.big[:, 4 * D:8 * D].rearrange("p (i n) -> p i n", i=2)
        k.v_rows = k.big[:, 8 * D:12 * D].rearrange("p (i n) -> p i n", i=NT)
        k.f_cols = k.ex.rearrange("p (d c t) -> p d c t", d=2, c=KD)
        k.q_cols = k.tok[:, 0:2, :].rearrange("p a (c t) -> p (a c) t", t=LAT)
        k.g_cols = lambda c: k.gate[:, c // 4, 0, (c % 4) * LAT:(c % 4 + 1) * LAT]
        k.state = k.resid[:, 0:2, :].rearrange("p a (h c) -> p (a h) c", c=DV)
        k.q_fac = k.big[:, 0:4 * D].rearrange("p (d c t) -> p d c t", d=2, c=KD)
        k.k_fac = k.u_area.rearrange("p (d c t) -> p d c t", d=2, c=KD)
        k.k_sum = k.tok[:, 2:4, :].rearrange("p a (c t) -> p (a c) t", t=LAT)
        k.pair_near = k.big[:, 4 * D:6 * D].rearrange("p (g i h t) -> p g i h t", g=2, i=2, h=4)
        k.pair_cross = k.big[:, 6 * D:8 * D].rearrange("p (g i h t) -> p g i h t", g=2, i=2, h=4)
        k.e_ring = k.ring[:, 0:E_RING * E_SLOT]
        k.acc = k.tok[:, 0:2, :]
        k.list_cols = k.u_cols[:, :, 0:P]
        k.e_hid = k.big[:, 0:FFN]
        k.e_hid_cols = k.big[:, FFN:2 * FFN].rearrange("p (f t) -> p f t", f=FC)
        k.e_y = k.big[:, 2 * FFN:2 * FFN + D]
        k.e_silu = k.big[:, 2 * FFN + D:2 * FFN + D + 2 * E_N].rearrange("p (b n) -> p b n", b=2)
        k.places = k.ex[:, 0:256].rearrange("p (i n) -> p i n", i=2)
        k.wplaces = k.ex[:, 256:512].rearrange("p (i n) -> p i n", i=2)
        k.wplace_cols = k.ex[:, 512:768]
        k.route = k.ex[:, 1024:1024 + 16 * 16].rearrange("p (f i e) -> p f i e", f=16, i=2)
        k.comb = k.ex[:, 1536:1552].rearrange("p (i e) -> p i e", i=2)
        k.place = k.ex[:, 1552:1570].rearrange("p (i e) -> p i e", i=2)
        k.passes = sb("passes", [P, 1], I32)
        scan = k.tok[:, :, :].rearrange("p a n -> p (a n)")
        k.zeros, k.gates_f, k.gates_b = (scan[:, n * HALF:(n + 1) * HALF] for n in range(3))
        (k.scan_t, k.scan_z, k.scan_a, k.scan_a_rev, k.scan_e, k.scan_e_rev, k.scan_m,
         k.scan_m_rev) = (k.ex[:, n * HALF:(n + 1) * HALF] for n in range(8))
        k.ones, k.ident, k.before, k.after = (sb(n, [P, P]) for n in ("ones", "ident", "before", "after"))
        k.level_mask = sb("level_mask", [P, LEVELS, P], U8)
        k.gate_sel = sb("gate_sel", [32, 4, 16])
        k.slot_no = sb("slot_no", [P, 256])
        k.expert_no = sb("expert_no", [P, 2, EXPERTS])
        k.crows = k.junk[:, 0:P]
        k.vrows = k.junk[:, P:2 * P]
        k.vcol = sb("vcol", [P, 120])
        k.c_cols = sb("c_cols", [P, KD, 2])
        k.lb_raw, k.lb_exp, k.lb_col, k.lb_rest = (sb(n, [P, 16]) for n in ("lb_raw", "lb_exp", "lb_col", "lb_rest"))
        k.gate_bias = sb("gate_bias", [16, 2])
        k.w_router = sb("w_router", [P, KD, EXPERTS])
        k.b_router = sb("b_router", [1, EXPERTS])
        k.mod_cols = sb("mod_cols", [P, N_MOD, KD, 2])
        k.mod_scale = sb("mod_scale", [P, 2, KD, 2])
        k.ssq, k.rms, k.rstd = (sb(n, [P, NT]) for n in ("ssq", "rms", "rstd"))
        k.eps = sb("eps", [P, 1])
        k.a_cols = sb("a_cols", [P, NT, 16])
        k.e_cols = sb("e_cols", [P, NT, 16])
        k.den = sb("den", [P, 2, NT])
        k.head_sum = sb("head_sum", [P, NT * HEADS])
        k.ps = stack.enter_context(nc.psum_tensor("ps", [P, 8, HALF], F32))
        k.stream = WeightStream(k.ring, k.ex[:, 4 * HALF:8 * HALF], [stack.enter_context(nc.semaphore(f"loaded{i}")) for i in range(RING)])
        plan_stream(k)

        order = [
            lambda: setup(k),
            lambda: modulation(k, 0),
            lambda: norm_in(k, "n0", 0, range(NT)),
            lambda: mlstm_in(k),
            lambda: mlstm_heads(k),
            lambda: mixer_out(k, "mo", "m_out", range(NT), 88, lambda h: k.o_cols[:, h, :], False),
            lambda: norm_in(k, "n1", 1, range(NT)),
            lambda: feed_forward(k),
            lambda: modulation(k, 1),
            lambda: norm_in(k, "n2", 0, range(NT), True),
            lambda: hgrn_in(k),
            lambda: hgrn_state(k),
            lambda: hgrn_pairs(k),
            lambda: hgrn_values(k),
            lambda: mixer_out(k, "ho", "h_out", (2, 3), 96, k.g_cols, True),
            lambda: norm_in(k, "n3", 1, (2, 3)),
            lambda: routing(k),
            lambda: experts(k),
            lambda: finish(k),
        ]
        for n, stage in enumerate(order[:stages]):
            stage()
            if n == len(order) // 2:
                nc.clear_and_free_semaphores(list(stage_sems))
                stage_sems.clear()
                k.stream.release = {}
                nc.all_engine_barrier()


_INS = ['x', 'c', 'ctx', 'c_ctx', 'mod_w', 'mod_b', 'norm_g', 'm_w_in', 'm_b_gate', 'm_w_conv', 'm_g_head', 'm_w_out',
        'h_w_in', 'h_b_f', 'h_lb_raw', 'h_g_head', 'h_w_out', 'f_w_gu', 'f_w_down',
        'e_w_router', 'e_b_router', 'e_w_gu', 'e_w_down']


def kernel(**inputs):
    import numpy as _np
    import concourse.bacc as _bacc
    from concourse.bass_utils import run_bass_kernel_spmd as _run

    nc = _bacc.Bacc("TRN2", target_bir_lowering=False, num_devices=1)
    arrays, args = {}, {}
    for name in _INS:
        array = _np.ascontiguousarray(inputs[name])
        arrays[f"in_{name}_dram"] = array
        args[name] = nc.dram_tensor(f"in_{name}_dram", array.shape, mybir.dt.from_np(array.dtype), kind="ExternalInput").ap()
    out = nc.dram_tensor("out_0_dram", inputs["x"].shape, F32, kind="ExternalOutput").ap()
    hybrid_mlstm_hgrn2_moe(nc, args, out)
    r = _run(nc, [arrays], core_ids=[0])
    return r.results[0]["out_0_dram"]
```

```python
from contextlib import ExitStack

import concourse.bass as bass
from concourse import mybir
from concourse.alu_op_type import AluOpType as ALU

F32 = mybir.dt.float32
F32R = mybir.dt.float32r
I32 = mybir.dt.int32
U8 = mybir.dt.uint8
ACT = mybir.ActivationFunctionType
AX = mybir.AxisListType

P = 128
D = 1024
KD = D // P
CTX, LAT = 256, 256
T = CTX + LAT
NT = T // P
HALF = 512
EPS = 1e-6
N_MOD = 6
HEADS = 8
DV = 128
M_DK = 64
M_QK = 2 * HEADS * M_DK
M_V = HEADS * DV
VST = DV + 2
FFN = 2816
FC = FFN // P
F_GROUP = 8
W_BUFS = 2
W_PIECE = KD * P
GRID_W = 64
GRID_H = LAT // GRID_W
EXPERTS = 8
SHIFT = 0.125

RING = 3
SLOT = KD * HALF
E_RING = 4
E_N = 352
E_TILES = FFN // E_N
E_SLOT = 6 * HALF
E_UNITS = 2 * E_TILES + 2 * 4
E_BUFS = 3
E_PIECE = 3 * HALF
LEVELS = 7


class Names:
    pass


class Chain:

    def __init__(self, engine, sem):
        self.engine, self.sem, self.n = engine, sem, 0

    def link(self, instruction):
        instruction.then_inc(self.sem, 1)
        self.n += 1
        self.engine.wait_ge(self.sem, self.n)


class WeightStream:

    def __init__(self, ring, rows, loaded):
        self.ring, self.rows, self.loaded = ring, rows, loaded
        self.parts, self.value, self.sent = [], [], 0
        self.count = [0] * RING
        self.release = {}

    def slot(self, n):
        s = n % RING
        return self.ring[:, s * SLOT:(s + 1) * SLOT]

    def aux(self, n, partition):
        s = n % RING
        return self.rows[partition:partition + 1, s * HALF:(s + 1) * HALF]

    def add(self, *parts):
        n = len(self.parts)
        self.parts.append(parts)
        self.count[n % RING] += 16 * len(parts)
        self.value.append(self.count[n % RING])

    def send(self, sp, end):
        for n in range(self.sent, min(end, len(self.parts))):
            if n - RING in self.release:
                sp.wait_ge(*self.release[n - RING])
            for place, source in self.parts[n]:
                sp.dma_start(self.aux(n, place) if isinstance(place, int) else place(self.slot(n)), source).then_inc(self.loaded[n % RING], 16)
        self.sent = max(self.sent, min(end, len(self.parts)))

    def arrived(self, engine, n):
        engine.wait_ge(self.loaded[n % RING], self.value[n])


def rows_of(width):
    return lambda slot: slot[:, 0:KD * width].rearrange("p (k n) -> p k n", k=KD)


def columns(w, first, width):
    return w[:, first:first + width].rearrange("(k p) n -> p k n", p=P)


def row(v, first):
    return v[first:first + HALF].rearrange("(o n) -> o n", o=1)


def plan_stream(k):
    a, s = k.a, k.stream
    wide = rows_of(HALF)
    plan = {}

    def start(name):
        plan[name] = len(s.parts)

    def add_mod(layer):
        start(f"mod{layer}")
        for n in range(2 * N_MOD):
            parts = [(wide, columns(a["mod_w"][layer], n * HALF, HALF)),
                     (0, row(a["mod_b"][layer], n * HALF))]
            if n // 2 in (2, 5):
                gain = a["norm_g"][layer, 1 if n // 2 == 2 else 3]
                parts.append((32, row(gain, (n % 2) * HALF)))
            s.add(*parts)

    add_mod(0)
    w = a["m_w_in"][0]
    start("m_in")
    s.add((rows_of(4 * HEADS), columns(w, M_QK + 2 * M_V, 4 * HEADS)))
    for n in range(0, M_QK + 2 * M_V, HALF):
        s.add((wide, columns(w, n, HALF)))
    start("m_out")
    for n in range(0, D, HALF):
        s.add((wide, columns(a["m_w_out"][0], n, HALF)))
    w = a["f_w_gu"][0]
    start("f_up")
    w_down = a["f_w_down"][0].rearrange("(f p) n -> p f n", p=P)

    def place(side):
        return lambda slot: slot[:, 0:SLOT].rearrange("p (k s n) -> p k s n", k=KD, s=2)[:, :, side, :]

    for first in range(0, FC, F_GROUP):
        end = min(first + F_GROUP, FC)
        for f in range(first, end, 2):
            s.add((place(0), columns(w, f * P, 2 * P)), (place(1), columns(w, FFN + f * P, 2 * P)))
        for f in range(first, end, 4):
            m = min(4, end - f)
            s.add((lambda slot, m=m: slot[:, 0:m * D].rearrange("p (f n) -> p f n", f=m), w_down[:, f:f + m, :]))
    add_mod(1)
    w = a["h_w_in"][0]
    start("h_in")
    for direction in range(2):
        for half in range(2):
            s.add((wide, columns(w, (2 + direction) * D + half * HALF, HALF)))
    for first in (D, 0, 4 * D):
        for half in range(2):
            s.add((wide, columns(w, first + half * HALF, HALF)))
    start("h_out")
    for n in range(0, D, HALF):
        s.add((wide, columns(a["h_w_out"][0], n, HALF)))
    k.plan = plan



def setup(k):
    nc, a = k.nc, k.a
    rows_in, made, same_made = k.sem("rows_in"), k.sem("ones_made"), k.sem("same_made")
    small_in, silu_done, turned = k.sem("small_in"), k.sem("silu_done"), k.sem("rows_turned")
    own, iota_made = k.sem("setup_chain"), k.sem("iota_made")
    same = k.ex[:, 0:1024].rearrange("p (l n) -> p l n", l=8)
    iota_i = k.ex[:, 1024:1024 + 272].bitcast(I32)

    with nc.Block() as block:

        @block.sync
        def _(sp):
            sp.dma_start(k.crows[0:8, :], a["c_ctx"].rearrange("(k p) -> k p", p=P)).then_inc(rows_in, 16)
            sp.dma_start(k.crows[8:16, :], a["c"][0].rearrange("(k p) -> k p", p=P)).then_inc(rows_in, 16)
            sp.dma_start(k.crows[16:32, :], a["h_lb_raw"][0].rearrange("a (k p) -> (a k) p", p=P)).then_inc(rows_in, 16)
            sp.dma_start(k.vrows[0:64, :], a["norm_g"].rearrange("l n (k p) -> (l n k) p", p=P)).then_inc(rows_in, 16)
            sp.dma_start(k.vrows[64:88, :], a["m_w_conv"][0].rearrange("t (k p) -> (t k) p", p=P)).then_inc(rows_in, 16)
            sp.dma_start(k.vrows[88:96, :], a["m_g_head"][0].rearrange("(k p) -> k p", p=P)).then_inc(rows_in, 16)
            sp.dma_start(k.vrows[96:104, :], a["h_g_head"][0].rearrange("(k p) -> k p", p=P)).then_inc(rows_in, 16)
            sp.dma_start(k.vrows[104:120, :], a["h_b_f"][0].rearrange("a (k p) -> (a k) p", p=P)).then_inc(rows_in, 16)
            for g in range(4):
                sp.dma_start(k.gate_bias[(g // 2) * 8:(g // 2) * 8 + 8, g % 2:g % 2 + 1],
                             a["m_b_gate"][0, g].rearrange("(h o) -> h o", o=1)).then_inc(small_in, 16)
            sp.dma_start(k.w_router[:, :, :], a["e_w_router"][0].rearrange("(k p) e -> p k e", p=P)).then_inc(small_in, 16)
            sp.dma_start(k.b_router[0:1, :], a["e_b_router"][0:1, :]).then_inc(small_in, 16)
            k.stream.send(sp, RING)
            sp.dma_start(k.resid[:, 0:2, :], a["ctx"][0].rearrange("(t p) d -> p t d", p=P)).then_inc(k.x_in, 16)
            sp.dma_start(k.resid[:, 2:4, :], a["x"][0].rearrange("(t p) d -> p t d", p=P)).then_inc(k.x_in, 16)
            sp.wait_ge(small_in, 96)

        @block.gpsimd
        def _(pool):
            pool.memset(k.ones[:, :], 1.0).then_inc(made, 1)
            pool.wait_ge(made, 1)
            pool.affine_select(out=k.ident[:, :], in_=k.ones[:, :], compare_op=ALU.is_equal, fill=0.0, base=0,
                               pattern=[[-1, P]], channel_multiplier=1).then_inc(made, 1)
            pool.affine_select(out=k.before[:, :], in_=k.ones[:, :], compare_op=ALU.is_gt, fill=0.0, base=0,
                               pattern=[[1, P]], channel_multiplier=-1).then_inc(made, 1)
            pool.affine_select(out=k.after[:, :], in_=k.ones[:, :], compare_op=ALU.is_gt, fill=0.0, base=0,
                               pattern=[[-1, P]], channel_multiplier=1).then_inc(made, 1)
            pool.iota(iota_i[:, 0:256], pattern=[[1, 256]], base=0, channel_multiplier=0).then_inc(iota_made, 1)
            pool.iota(iota_i[:, 256:272], pattern=[[0, 2], [1, 8]], base=8, channel_multiplier=0).then_inc(iota_made, 1)
            for i in range(8):
                size, n = 2 ** i, P // 2 ** i
                view = same[:, i, :].rearrange("p (b l) -> p b l", l=size)
                pool.affine_select(out=view, in_=k.ones[:, :].rearrange("p (b l) -> p b l", l=size),
                                   compare_op=ALU.is_ge, fill=0.0, base=0, pattern=[[-size, n], [0, size]],
                                   channel_multiplier=1).then_inc(same_made, 1)
                pool.wait_ge(same_made, 2 * i + 1)
                pool.affine_select(out=view, in_=view, compare_op=ALU.is_ge, fill=0.0, base=size - 1,
                                   pattern=[[size, n], [0, size]], channel_multiplier=-1).then_inc(same_made, 1)

        @block.scalar
        def _(act):
            act.wait_ge(rows_in, 128)
            nc.scalar.activation(k.crows[0:16, :], k.crows[0:16, :], ACT.Silu).then_inc(silu_done, 1)
            act.wait_ge(own, 2)
            nc.scalar.activation(k.lb_exp[:, :], k.lb_exp[:, :], ACT.Exp).then_inc(silu_done, 1)

        @block.tensor
        def _(pe):
            pe.wait_ge(made, 2)
            pe.wait_ge(rows_in, 128)
            nc.tensor.transpose(k.ps[:, 0, 0:120], k.vrows[0:120, :], k.ident[0:120, 0:120]).then_inc(turned, 1)
            pe.wait_ge(silu_done, 1)
            nc.tensor.transpose(k.ps[:, 1, 0:32], k.crows[0:32, :], k.ident[0:32, 0:32]).then_inc(turned, 1)

        @block.vector
        def _(dve):
            chain = Chain(dve, own)
            dve.wait_ge(turned, 2)
            chain.link(nc.vector.tensor_copy(k.lb_raw[:, :], k.ps[:, 1, 16:32]))
            chain.link(nc.vector.tensor_tensor(k.lb_exp[:, :], k.lb_raw[:, :], k.lb_raw[:, :], ALU.subtract))
            nc.vector.tensor_copy(k.vcol[:, :], k.ps[:, 0, 0:120])
            nc.vector.tensor_copy(k.c_cols[:, :, :], k.ps[:, 1, 0:16].rearrange("p (j k) -> p k j", j=2))
            nc.vector.memset(k.eps[:, :], EPS)
            nc.vector.memset(k.vaug[:, :, :, DV:DV + 1], 1.0)
            nc.vector.memset(k.gate_sel[:, :, :], 0.0).then_inc(own, 1)
            chain.n += 1
            dve.wait_ge(made, 4)
            dve.wait_ge(own, chain.n)
            for g, (src, dst) in enumerate(((0, 0), (16, 8), (8, 0), (24, 8))):
                nc.vector.tensor_copy(k.gate_sel[0:32, g, dst:dst + 8], k.ident[0:32, src:src + 8])
            dve.wait_ge(iota_made, 2)
            nc.vector.tensor_copy(k.slot_no[:, :], iota_i[:, 0:256])
            nc.vector.tensor_copy(k.expert_no[:, :, :], iota_i[:, 256:272].rearrange("p (i e) -> p i e", i=2))
            dve.wait_ge(same_made, 16)
            nc.vector.tensor_tensor(k.level_mask[:, :, :], same[:, 1:8, :], same[:, 0:7, :], ALU.subtract)
            dve.wait_ge(silu_done, 2)
            chain.link(nc.vector.reciprocal(k.lb_raw[:, :], k.lb_exp[:, :]))
            chain.link(nc.vector.tensor_tensor(k.lb_exp[:, :], k.lb_exp[:, :], k.lb_raw[:, :], ALU.mult))
            chain.link(nc.vector.tensor_tensor(k.lb_col[:, :], k.lb_exp[:, :], k.lb_exp[:, :], ALU.subtract))
            nc.vector.tensor_scalar(k.lb_rest[:, :], k.lb_col[:, :], -1.0, 1.0, ALU.mult, ALU.add)



def modulation(k, layer):
    nc, s, u0 = k.nc, k.stream, k.plan[f"mod{layer}"]
    row_ready, row_copied = k.sem(f"mod{layer}_row_ready"), k.sem(f"mod{layer}_row_copied")
    cols_ready, cols_copied = k.sem(f"mod{layer}_cols_ready"), k.sem(f"mod{layer}_cols_copied")
    scaled, spread, gate_copied = k.sem(f"mod{layer}_scaled"), k.sem(f"mod{layer}_spread"), k.sem(f"mod{layer}_gate_copied")
    units = 2 * N_MOD
    streams = (0, 1) if layer == 0 else (1,)
    gates = [n for n in range(units) if n // 2 in (2, 5)]
    plain = [n for n in range(units) if n not in gates]
    rows = k.ex[0:2, 0:2 * HALF].rearrange("p (b n) -> p b n", b=2)
    scaled_rows = k.ex[0:2, 2 * HALF:4 * HALF].rearrange("p (b n) -> p b n", b=2)
    s.release = {u0 + n: (row_ready, n + 1) for n in range(units)}

    with nc.Block() as block:

        @block.sync
        def _(sp):
            s.send(sp, u0 + units + RING)

        @block.tensor
        def _(pe):
            def finish(n):
                pe.wait_ge(row_copied, n + 1)
                if n in plain:
                    i = plain.index(n)
                    if i >= 2:
                        pe.wait_ge(cols_copied, i - 1)
                    for c in range(4):
                        last = nc.tensor.transpose(k.ps[:, 4 + i % 2, 2 * c:2 * c + 2],
                                                   rows[0:2, n % 2, c * P:(c + 1) * P], k.ident[0:2, 0:2])
                    last.then_inc(cols_ready, 1)
                else:
                    g = gates.index(n)
                    pe.wait_ge(scaled, g + 1)
                    if g:
                        pe.wait_ge(gate_copied, g * len(streams))
                    for j in streams:
                        nc.tensor.matmul(k.ps[:, 6 + j, :], k.ident[0:2, j:j + 1].to_broadcast([2, P]), scaled_rows[0:2, g % 2, :],
                                         start=True, stop=True).then_inc(spread, 1)

            for n in range(units):
                s.arrived(pe, u0 + n)
                slot = s.slot(u0 + n)
                w = rows_of(HALF)(slot)
                if n >= 2:
                    pe.wait_ge(row_copied, n - 1)
                if n in gates:
                    if gates.index(n):
                        pe.wait_ge(scaled, gates.index(n))
                    nc.tensor.matmul(k.ps[0:2, 2, :], k.ones[32:33, 0:2], s.aux(u0 + n, 32), start=True, stop=True)
                for c in range(KD):
                    nc.tensor.matmul(k.ps[0:2, n % 2, :], k.c_cols[:, c, :], w[:, c, :], start=(c == 0), stop=False)
                nc.tensor.matmul(k.ps[0:2, n % 2, :], k.ones[0:1, 0:2], s.aux(u0 + n, 0), start=False,
                                 stop=True).then_inc(row_ready, 1)
                if n:
                    finish(n - 1)
            finish(units - 1)

        @block.scalar
        def _(act):
            for n in range(units):
                act.wait_ge(row_ready, n + 1)
                if n >= 2:
                    if n - 2 in plain:
                        act.wait_ge(cols_ready, plain.index(n - 2) + 1)
                    else:
                        act.wait_ge(scaled, gates.index(n - 2) + 1)
                nc.scalar.activation(rows[0:2, n % 2, :], k.ps[0:2, n % 2, :], ACT.Copy).then_inc(row_copied, 1)

        @block.vector
        def _(dve):
            for n in range(units):
                if n in plain:
                    i = plain.index(n)
                    dve.wait_ge(cols_ready, i + 1)
                    nc.vector.tensor_copy(k.mod_cols[:, n // 2, 4 * (n % 2):4 * (n % 2) + 4, :],
                                          k.ps[:, 4 + i % 2, 0:8].rearrange("p (c j) -> p c j", j=2)).then_inc(cols_copied, 1)
                    continue
                g = gates.index(n)
                dve.wait_ge(row_copied, n + 1)
                if g >= 2:
                    dve.wait_ge(spread, (g - 1) * len(streams))
                nc.vector.tensor_tensor(scaled_rows[0:2, g % 2, :], rows[0:2, n % 2, :], k.ps[0:2, 2, :],
                                        ALU.mult).then_inc(scaled, 1)
                for i, j in enumerate(streams):
                    dve.wait_ge(spread, g * len(streams) + i + 1)
                    nc.vector.tensor_copy(k.gate[:, g // 2, j, (n % 2) * HALF:(n % 2 + 1) * HALF],
                                          k.ps[:, 6 + j, :]).then_inc(gate_copied, 1)
            dve.wait_ge(cols_copied, len(plain))
            for w in range(2):
                gain = k.vcol[:, (layer * 4 + 2 * w) * KD:(layer * 4 + 2 * w + 1) * KD]
                nc.vector.scalar_tensor_tensor(out=k.mod_scale[:, w, :, :], in0=k.mod_cols[:, 1 + 3 * w, :, :], scalar=1.0,
                                               in1=gain.unsqueeze(2).to_broadcast([P, KD, 2]), op0=ALU.add, op1=ALU.mult)



def norm_in(k, name, which, tiles, column_major=False, u_cols=None, arrived=None):
    u_cols = k.u_cols if u_cols is None else u_cols
    nc = k.nc
    squared, root, normed = k.sem(name + "_squared"), k.sem(name + "_root"), k.sem(name + "_normed")
    turned, recip = k.sem(name + "_turned"), k.sem(name + "_recip")
    t0, t1 = tiles[0], tiles[-1] + 1
    streams = [j for j in range(2) if 2 * j in tiles]

    def source(c, j):
        return k.ps[:, c, j * 256:(j + 1) * 256]

    def views(c, j):
        src, dst = source(c, j), u_cols[:, c, j * 256:(j + 1) * 256]
        if column_major and j == 1:
            return (src.rearrange("p (r w) -> p r w", r=GRID_H), dst.rearrange("p (w r) -> p r w", r=GRID_H))
        return src, dst

    with nc.Block() as block:

        @block.scalar
        def _(act):
            if arrived:
                act.wait_ge(*arrived)
            for i in tiles:
                nc.scalar.activation(k.tok[:, i, :], k.resid[:, i, :], ACT.Square,
                                     accum_out=k.ssq[:, i:i + 1]).then_inc(squared, 1)
            act.wait_ge(squared, len(tiles))
            nc.scalar.activation(k.rms[:, t0:t1], k.ssq[:, t0:t1], ACT.Sqrt, bias=k.eps[:, 0:1],
                                 scale=1.0 / D).then_inc(root, 1)
            for c in range(1, KD, 2):
                act.wait_ge(turned, c + 1)
                for j in streams:
                    src, dst = views(c, j)
                    nc.scalar.activation(dst, src, ACT.Identity, bias=k.mod_cols[:, 3 * which, c, j:j + 1],
                                         scale=k.mod_scale[:, which, c, j:j + 1])

        @block.vector
        def _(dve):
            dve.wait_ge(root, 1)
            nc.vector.reciprocal(k.rstd[:, t0:t1], k.rms[:, t0:t1]).then_inc(recip, 1)
            dve.wait_ge(recip, 1)
            for i in tiles:
                nc.vector.tensor_scalar(k.tok[:, i, :], k.resid[:, i, :], k.rstd[:, i:i + 1], None,
                                        ALU.mult).then_inc(normed, 1)
            for c in range(0, KD, 2):
                dve.wait_ge(turned, c + 1)
                for j in streams:
                    src, dst = views(c, j)
                    nc.vector.tensor_scalar(dst, src, k.mod_scale[:, which, c, j:j + 1],
                                            k.mod_cols[:, 3 * which, c, j:j + 1], ALU.mult, ALU.add)

        @block.tensor
        def _(pe):
            for n, i in enumerate(tiles):
                pe.wait_ge(normed, n + 1)
                for c in range(KD):
                    last = nc.tensor.transpose(k.ps[:, c, i * P:(i + 1) * P], k.tok[:, i, c * P:(c + 1) * P], k.ident[:, :])
                    if i == tiles[-1]:
                        last.then_inc(turned, 1)



def residual_scalar(k, act, r, tiles, copies, summed=None):
    nc = k.nc
    if copies:
        for n, i in enumerate(tiles):
            act.wait_ge(r.ready, r.ready_value(i, 0))
            nc.scalar.activation(k.tok[:, i, 0:HALF], k.ps[:, r.bank(i, 0), :], ACT.Copy).then_inc(r.copied_a, 1)
    for n, i in enumerate(tiles):
        if copies:
            act.wait_ge(r.copied_a, n + 1)
            act.wait_ge(r.copied_b, n + 1)
        if summed:
            summed(n)
        nc.scalar.activation(k.junk[:, :], k.tok[:, i, :], ACT.Square, accum_out=k.ssq[:, i:i + 1]).then_inc(r.squared, 1)
        act.wait_ge(r.squared, n + 1)
        nc.scalar.activation(k.rms[:, i:i + 1], k.ssq[:, i:i + 1], ACT.Sqrt, bias=k.eps[:, 0:1],
                             scale=1.0 / D).then_inc(r.root, 1)


def residual_vector(k, dve, r, tiles, which, copies):
    nc = k.nc
    if copies:
        for n, i in enumerate(tiles):
            dve.wait_ge(r.ready, r.ready_value(i, 1))
            nc.vector.tensor_copy(k.tok[:, i, HALF:D], k.ps[:, r.bank(i, 1), :]).then_inc(r.copied_b, 1)
    chain = Chain(dve, r.chain)
    for n, i in enumerate(tiles):
        dve.wait_ge(r.root, n + 1)
        chain.link(nc.vector.reciprocal(k.rstd[:, i:i + 1], k.rms[:, i:i + 1]))
        chain.link(nc.vector.scalar_tensor_tensor(out=k.tok[:, i, :], in0=k.tok[:, i, :], scalar=k.rstd[:, i:i + 1],
                                                  in1=k.gate[:, which, i // 2, :], op0=ALU.mult, op1=ALU.mult))
        nc.vector.tensor_tensor(k.resid[:, i, :], k.resid[:, i, :], k.tok[:, i, :], ALU.add).then_inc(r.added, 1)


def residual_sems(k, name, bank, ready_value):
    r = Names()
    r.bank, r.ready_value = bank, ready_value
    r.ready, r.copied_a, r.copied_b = k.sem(name + "_ready"), k.sem(name + "_copied_a"), k.sem(name + "_copied_b")
    r.squared, r.root, r.chain, r.added = (k.sem(f"{name}_{n}") for n in ("squared", "root", "chain", "added"))
    return r



def mlstm_in(k):
    nc, s, u0 = k.nc, k.stream, k.plan["m_in"]
    gates_ready, gates_copied, picked = k.sem("m_gates_ready"), k.sem("m_gates_copied"), k.sem("m_picked")
    job_ready, conv_done, job_copied = k.sem("m_job_ready"), k.sem("m_conv_done"), k.sem("m_job_copied")
    own, act_own, scan_ready, cols_ready = k.sem("m_chain"), k.sem("m_act_own"), k.sem("m_scan_ready"), k.sem("m_cols_ready")
    conv_own, scan_input, exp_ready = k.sem("m_conv_own"), k.sem("m_scan_input"), k.sem("m_exp_ready")
    units = 7
    s.release = {u0: (gates_ready, 1)}
    for u in range(6):
        s.release[u0 + 1 + u] = (job_ready, 4 * u + 4)
    pre = k.junk

    with nc.Block() as block:

        @block.sync
        def _(sp):
            s.send(sp, u0 + units + RING)

        @block.tensor
        def _(pe):
            s.arrived(pe, u0)
            w = rows_of(4 * HEADS)(s.slot(u0))
            for c in range(KD):
                last = nc.tensor.matmul(k.ps[0:32, 0, :], w[:, c, :], k.u_cols[:, c, :], start=(c == 0), stop=(c == KD - 1))
            last.then_inc(gates_ready, 1)

            def job(r):
                u = u0 + 1 + r // 4
                if r % 4 == 0:
                    s.arrived(pe, u)
                w = rows_of(HALF)(s.slot(u))
                bank = 1 + r % 4
                if r >= 12:
                    pe.wait_ge(job_copied, r - 3)
                elif r >= 4:
                    pe.wait_ge(conv_done, r - 3)
                i = r % 4
                for c in range(KD):
                    if 8 <= r < 16:
                        lhs, rhs = k.u_cols[:, c, i * P:(i + 1) * P], w[:, c, :]
                    else:
                        lhs, rhs = w[:, c, i * P:(i + 1) * P], k.u_cols[:, c, :]
                    last = nc.tensor.matmul(k.ps[:, bank, :], lhs, rhs, start=(c == 0), stop=(c == KD - 1))
                last.then_inc(job_ready, 1)

            for r in range(24):
                job(r)
                if r == 0:
                    pe.wait_ge(gates_copied, 2)
                    for g in range(2):
                        nc.tensor.matmul(k.ps[0:16, 6 + g, :], k.gate_sel[0:32, 2 * g, :], k.gates_f[0:32, :],
                                         start=True, stop=False)
                        last = nc.tensor.matmul(k.ps[0:16, 6 + g, :], k.gate_sel[0:32, 2 * g + 1, :], k.gates_b[0:32, :],
                                                start=False, stop=True)
                    last.then_inc(picked, 1)
                if r == 20:
                    pe.wait_ge(scan_ready, 1)
                    for q, src in enumerate((k.scan_a, k.scan_a_rev, k.scan_e, k.scan_e_rev)):
                        for i in range(NT):
                            n = (q * NT + i) * 16
                            last = nc.tensor.transpose(k.ps[:, 0, n:n + 16], src[0:16, i * P:(i + 1) * P], k.ident[0:16, 0:16])
                    last.then_inc(cols_ready, 1)

        @block.scalar
        def _(act):
            def gates():
                act.wait_ge(picked, 1)
                nc.scalar.activation(k.scan_t[0:16, :], k.ps[0:16, 7, :], ACT.Abs, bias=k.gate_bias[0:16, 1:2]).then_inc(act_own, 1)
                act.wait_ge(act_own, 1)
                nc.scalar.activation(k.scan_t[0:16, :], k.scan_t[0:16, :], ACT.Exp, scale=-1.0).then_inc(act_own, 1)
                act.wait_ge(act_own, 2)
                nc.scalar.activation(k.scan_t[0:16, :], k.scan_t[0:16, :], ACT.Ln, bias=1.0).then_inc(scan_input, 1)

            for r in range(24):
                if r < 8:
                    act.wait_ge(conv_done, r + 1)
                    nc.scalar.activation(k.qk[:, r, :], pre[:, (r % 2) * HALF:(r % 2 + 1) * HALF], ACT.Silu).then_inc(job_copied, 1)
                elif r < 16:
                    i, half = r % 4, (r - 8) // 4
                    act.wait_ge(job_ready, r + 1)
                    nc.scalar.activation(k.vaug[:, i, 4 * half:4 * half + 4, 0:DV],
                                         k.ps[:, 1 + r % 4, :].rearrange("p (h d) -> p h d", h=4), ACT.Copy).then_inc(job_copied, 1)
                else:
                    act.wait_ge(job_ready, r + 1)
                    nc.scalar.activation(k.o_cols[:, r - 16, :], k.ps[:, 1 + r % 4, :], ACT.Sigmoid).then_inc(job_copied, 1)
                if r == 1:
                    gates()
                if r == 15:
                    act.wait_ge(exp_ready, 1)
                    nc.scalar.activation(k.scan_e[0:16, :], k.scan_e[0:16, :], ACT.Exp, scale=-1.0).then_inc(act_own, 1)

        @block.vector
        def _(dve):
            chain = Chain(dve, own)
            chain.link(nc.vector.memset(k.zeros[0:16, :], 0.0))
            dve.wait_ge(gates_ready, 1)
            g = k.ps[0:32, 0, :].rearrange("p (s t) -> p s t", s=2)
            nc.vector.tensor_copy(k.gates_f[0:32, :], k.ps[0:32, 0, :]).then_inc(gates_copied, 1)
            nc.vector.tensor_copy(k.gates_b[0:32, :].rearrange("p (s t) -> p s t", s=2), g[:, :, ::-1]).then_inc(gates_copied, 1)

            def scan():
                z, i_sum, t = k.scan_z[0:16, :], k.scan_a[0:16, :], k.scan_t[0:16, :]
                dve.wait_ge(picked, 1)
                dve.wait_ge(scan_input, 1)
                chain.link(nc.vector.tensor_scalar(z, k.ps[0:16, 7, :], k.gate_bias[0:16, 1:2], None, ALU.add))
                chain.link(nc.vector.scalar_tensor_tensor(out=t, in0=z, scalar=0.0, in1=t, op0=ALU.min, op1=ALU.subtract))
                chain.link(nc.vector.tensor_tensor_scan(z, t, k.zeros[0:16, :], 0.0, ALU.add, ALU.add))
                chain.link(nc.vector.scalar_tensor_tensor(out=i_sum, in0=k.ps[0:16, 6, :], scalar=k.gate_bias[0:16, 0:1],
                                                          in1=z, op0=ALU.add, op1=ALU.subtract))
                chain.link(nc.vector.tensor_tensor_scan(k.scan_m[0:16, :], i_sum, i_sum, 0.0, ALU.max, ALU.max))
                nc.vector.tensor_tensor(k.scan_e[0:16, :], k.scan_m[0:16, :], z, ALU.add).then_inc(exp_ready, 1)

            for r in range(8):
                dve.wait_ge(job_ready, r + 1)
                if r >= 2:
                    dve.wait_ge(job_copied, r - 1)
                x = k.ps[:, 1 + r % 4, :].rearrange("p (s t) -> p s t", s=2)
                y = pre[:, (r % 2) * HALF:(r % 2 + 1) * HALF].rearrange("p (s t) -> p s t", s=2)
                tap = [k.vcol[:, 64 + t * KD + r:65 + t * KD + r] for t in range(3)]
                nc.vector.tensor_scalar(y, x, tap[1], None, ALU.mult).then_inc(conv_own, 1)
                dve.wait_ge(conv_own, 2 * r + 1)
                nc.vector.scalar_tensor_tensor(out=y[:, :, 1:], in0=x[:, :, 0:255], scalar=tap[0], in1=y[:, :, 1:],
                                               op0=ALU.mult, op1=ALU.add).then_inc(conv_own, 1)
                dve.wait_ge(conv_own, 2 * r + 2)
                nc.vector.scalar_tensor_tensor(out=y[:, :, 0:255], in0=x[:, :, 1:], scalar=tap[2], in1=y[:, :, 0:255],
                                               op0=ALU.mult, op1=ALU.add).then_inc(conv_done, 1)
                if r == 3:
                    scan()
            dve.wait_ge(act_own, 3)
            for dst, src in ((k.scan_a_rev, k.scan_a), (k.scan_m_rev, k.scan_m), (k.scan_e_rev, k.scan_e)):
                last = nc.vector.tensor_copy(dst[0:16, :].rearrange("p (s t) -> p s t", s=2),
                                             src[0:16, :].rearrange("p (s t) -> p s t", s=2)[:, :, ::-1])
            last.then_inc(scan_ready, 1)
            dve.wait_ge(cols_ready, 1)
            c = k.ps[:, 0, 0:256].rearrange("p (q r i h) -> p q r i h", q=2, r=2, h=16)
            for d in range(2):
                nc.vector.tensor_copy(k.a_cols[:, :, 8 * d:8 * d + 8], c[:, 0, d, :, 8 * d:8 * d + 8])
                nc.vector.tensor_copy(k.e_cols[:, :, 8 * d:8 * d + 8], c[:, 1, d, :, 8 * d:8 * d + 8])



SEEN = {0: [(0, 4), (1, 4), (2, 4), (3, 4)], 1: [(0, 4), (0, 4), (2, 3), (2, 4)]}
SOURCES = {0: [[0], [0, 1], [0, 1, 2], [0, 1, 2, 3]], 1: [[0, 1], [1], [0, 1, 2, 3], [0, 1, 3]]}


def mlstm_heads(k):
    nc = k.nc
    scored, spread, weighed, probs = k.sem("a_scored"), k.sem("a_spread"), k.sem("a_weighed"), k.sem("a_probs")
    masked, summed, own, added = k.sem("a_masked"), k.sem("a_summed"), k.sem("a_chain"), k.sem("a_added")
    turn_done, squares = k.sem("a_turn_done"), k.sem("a_squares")
    prob = k.u_area.rearrange("p (b s t) -> p b s t", b=2, s=NT)
    decay = k.ex[:, 0:4 * HALF].rearrange("p (s t) -> p s t", s=NT)
    part = k.ex[:, 4 * HALF:6 * HALF].rearrange("p (b t) -> p b t", b=2)
    turns = 2 * HEADS

    def score_cols(j):
        return (j, 0) if j < 2 else (2, (j - 2) * 256 - 256)

    with nc.Block() as block:

        @block.sync
        def _(sp):
            s = k.stream
            s.release = {}
            s.send(sp, s.sent)

        @block.tensor
        def _(pe):
            def scores(h):
                if h:
                    pe.wait_ge(probs, 8 * h)
                base = (h % 2) * 64
                for j in range(NT):
                    bank, col = score_cols(j)
                    t0 = 0 if j < 2 else 256
                    last = nc.tensor.matmul(k.ps[:, bank, col + t0:col + T], k.qk[base:base + 64, 4 + h // 2, j * P:(j + 1) * P],
                                            k.qk[base:base + 64, h // 2, t0:T], start=True, stop=True)
                last.then_inc(scored, 1)

            def spread_m(n):
                h, d = n // 2, n % 2
                if n >= 2:
                    pe.wait_ge(weighed, 4 * (n - 1))
                src = (k.scan_m, k.scan_m_rev)[d]
                nc.tensor.matmul(k.ps[:, 3 + d, :], k.ident[0:16, 8 * d + h:8 * d + h + 1].to_broadcast([16, P]),
                                 src[0:16, :], start=True, stop=True).then_inc(spread, 1)

            def values(n):
                h, d = n // 2, n % 2
                pe.wait_ge(masked, n + 1)
                if n:
                    pe.wait_ge(summed, n)
                for i in range(NT):
                    js = SOURCES[d][i]
                    for m, j in enumerate(js):
                        last = nc.tensor.matmul(k.ps[:, 5 + i // 2, (i % 2) * 256:(i % 2) * 256 + DV + 1],
                                                prob[:, n % 2, j, i * P:(i + 1) * P], k.vaug[:, j, h, 0:DV + 1],
                                                start=(m == 0), stop=(m == len(js) - 1))
                last.then_inc(turn_done, 1)

            scores(0)
            spread_m(0)
            spread_m(1)
            for n in range(turns):
                if n % 2 == 0 and n:
                    scores(n // 2)
                    spread_m(n)
                    spread_m(n + 1)
                if n:
                    values(n - 1)
            values(turns - 1)

        @block.scalar
        def _(act):
            for n in range(turns):
                h, d = n // 2, n % 2
                act.wait_ge(spread, n + 1)
                for j in range(NT):
                    t0, t1 = (x * P for x in SEEN[d][j])
                    if n:
                        act.wait_ge(probs, 4 * (n - 1) + j + 1)
                    nc.scalar.activation(decay[:, j, t0:t1], k.ps[:, 3 + d, t0:t1], ACT.Exp, scale=-1.0,
                                         bias=k.a_cols[:, j, 8 * d + h:8 * d + h + 1]).then_inc(weighed, 1)

        @block.vector
        def _(dve):
            chain = Chain(dve, own)

            def weigh(n):
                h, d = n // 2, n % 2
                dve.wait_ge(scored, h + 1)
                if n >= 2:
                    dve.wait_ge(turn_done, n - 1)
                for j in range(NT):
                    t0, t1 = (x * P for x in SEEN[d][j])
                    bank, col = score_cols(j)
                    dve.wait_ge(weighed, 4 * n + j + 1)
                    nc.vector.scalar_tensor_tensor(out=prob[:, n % 2, j, t0:t1], in0=k.ps[:, bank, col + t0:col + t1],
                                                   scalar=SHIFT, in1=decay[:, j, t0:t1], op0=ALU.mult,
                                                   op1=ALU.mult).then_inc(probs, 1)

            def finish(n):
                h, d = n // 2, n % 2
                dve.wait_ge(turn_done, n + 1)
                out = k.ps[:, 5:7, :].rearrange("p b (i c) -> p (b i) c", i=2)
                den = k.den[:, n % 2, :]
                chain.link(nc.vector.tensor_tensor(den, out[:, :, DV], k.e_cols[:, :, 8 * d + h], ALU.max))
                chain.link(nc.vector.scalar_tensor_tensor(out=den, in0=out[:, :, DV], scalar=-1.0, in1=den,
                                                          op0=ALU.mult, op1=ALU.max))
                chain.link(nc.vector.reciprocal(den, den))
                if n >= 2:
                    dve.wait_ge(added, n // 2)
                nc.vector.tensor_tensor(part[:, d, :].rearrange("p (i c) -> p i c", i=NT), out[:, :, 0:DV],
                                        den.unsqueeze(2).to_broadcast([P, NT, DV]), ALU.mult).then_inc(summed, 1)

            for n in range(turns):
                weigh(n)
                if n:
                    finish(n - 1)
            finish(turns - 1)

        @block.gpsimd
        def _(pool):
            def add(h):
                pool.wait_ge(summed, 2 * h + 2)
                hv = k.tok[:, :, h * DV:(h + 1) * DV]
                pool.tensor_tensor(hv, part[:, 0, :].rearrange("p (i c) -> p i c", i=NT),
                                   part[:, 1, :].rearrange("p (i c) -> p i c", i=NT), ALU.add).then_inc(added, 1)

            for n in range(turns):
                d = n % 2
                pool.wait_ge(probs, 4 * n + 4)
                flat = k.u_area[:, d * NT * T:(d + 1) * NT * T]
                diag = bass.AP(flat.tensor, flat.offset, [list(flat.ap[0]), [T + P, NT], [1, P]])
                sign = 1 if d == 0 else -1
                pool.affine_select(out=diag, in_=diag, compare_op=ALU.is_ge, fill=0.0, base=0,
                                   pattern=[[0, NT], [sign, P]], channel_multiplier=-sign).then_inc(masked, 1)
                if d == 1 and n > 1:
                    add(n // 2 - 1)
            add(HEADS - 1)



def mixer_out(k, name, unit, tiles, gain0, gate_of, column_major):
    nc, s, u0 = k.nc, k.stream, k.plan[unit]
    n_t = len(tiles)
    t0 = tiles[0]
    squared, rooted, normed = k.sem(name + "_hsq"), k.sem(name + "_hroot"), k.sem(name + "_hnormed")
    turned, cols_copied, own = k.sem(name + "_hturned"), k.sem(name + "_hcols"), k.sem(name + "_hown")
    r = residual_sems(k, name + "_res", lambda i, half: 4 * half + i,
                      lambda i, half: (n_t if half == 0 else n_t + 1 + i - t0))
    s.release = {u0: (r.ready, n_t), u0 + 1: (r.ready, 2 * n_t)}
    width = n_t * P
    col0 = t0 * P
    sums = k.head_sum[:, 0:n_t * HEADS]
    h_cols = k.u_area.rearrange("p (c t) -> p c t", c=KD)

    with nc.Block() as block:

        @block.sync
        def _(sp):
            s.send(sp, u0 + 2 + RING)

        @block.scalar
        def _(act):
            for n, i in enumerate(tiles):
                nc.scalar.activation(k.sq[:, n, :], k.tok[:, i, :], ACT.Square).then_inc(squared, 1)
            act.wait_ge(own, 1)
            nc.scalar.activation(sums, sums, ACT.Sqrt, bias=k.eps[:, 0:1], scale=1.0 / DV).then_inc(rooted, 1)
            residual_scalar(k, act, r, tiles, True)

        @block.vector
        def _(dve):
            dve.wait_ge(squared, n_t)
            nc.vector.tensor_reduce(out=sums, in_=k.sq[:, 0:n_t, :].rearrange("p i (h c) -> p (i h) c", h=HEADS),
                                    op=ALU.add, axis=AX.X).then_inc(own, 1)
            dve.wait_ge(rooted, 1)
            nc.vector.reciprocal(sums, sums).then_inc(own, 1)
            dve.wait_ge(own, 2)
            for n, i in enumerate(tiles):
                nc.vector.tensor_tensor(k.tok[:, i, :].rearrange("p (h c) -> p h c", h=HEADS),
                                        k.tok[:, i, :].rearrange("p (h c) -> p h c", h=HEADS),
                                        sums[:, n * HEADS:(n + 1) * HEADS].unsqueeze(2).to_broadcast([P, HEADS, DV]),
                                        ALU.mult).then_inc(normed, 1)
            for h in range(HEADS):
                dve.wait_ge(turned, h + 1)
                src, gate, dst = k.ps[:, 4 + h % 4, 0:width], gate_of(h), h_cols[:, h, col0:col0 + width]
                if column_major:
                    src = src.rearrange("p (w r) -> p r w", r=GRID_H)
                    gate = gate.rearrange("p (w r) -> p r w", r=GRID_H)
                    dst = dst.rearrange("p (r w) -> p r w", r=GRID_H)
                nc.vector.scalar_tensor_tensor(out=dst, in0=src, scalar=k.vcol[:, gain0 + h:gain0 + h + 1], in1=gate,
                                               op0=ALU.mult, op1=ALU.mult).then_inc(cols_copied, 1)
            residual_vector(k, dve, r, tiles, 0, True)

        @block.tensor
        def _(pe):
            def turn(h):
                if h >= 4:
                    pe.wait_ge(cols_copied, h - 3)
                for n, i in enumerate(tiles):
                    last = nc.tensor.transpose(k.ps[:, 4 + h % 4, n * P:(n + 1) * P], k.tok[:, i, h * DV:(h + 1) * DV],
                                               k.ident[:, :])
                last.then_inc(turned, 1)

            pe.wait_ge(normed, n_t)
            for h in range(3):
                turn(h)
            s.arrived(pe, u0)
            w = rows_of(HALF)(s.slot(u0))
            for h in range(HEADS):
                if h + 3 < HEADS:
                    turn(h + 3)
                pe.wait_ge(cols_copied, h + 1)
                for i in tiles:
                    last = nc.tensor.matmul(k.ps[:, i, :], h_cols[:, h, i * P:(i + 1) * P], w[:, h, :],
                                            start=(h == 0), stop=(h == HEADS - 1))
                    if h == HEADS - 1:
                        last.then_inc(r.ready, 1)
            s.arrived(pe, u0 + 1)
            w = rows_of(HALF)(s.slot(u0 + 1))
            for i in tiles:
                for h in range(HEADS):
                    last = nc.tensor.matmul(k.ps[:, 4 + i, :], h_cols[:, h, i * P:(i + 1) * P], w[:, h, :],
                                            start=(h == 0), stop=(h == HEADS - 1))
                last.then_inc(r.ready, 1)



def feed_forward(k):
    nc, s, u0 = k.nc, k.stream, k.plan["f_up"]
    chunks = [min(F_GROUP, FC - f) for f in range(0, FC, F_GROUP)]
    units = [c // 2 + -(-c // 4) for c in chunks]
    per = 3 * F_GROUP
    last_g = len(chunks) - 1
    assert all(c == F_GROUP for c in chunks[:-1]) and units[0] % RING == 0 and per % W_BUFS == 0
    u_high, u_low = k.sem("f_u_high"), k.sem("f_u_low")
    high_done, low_done, used = k.sem("f_high_done"), k.sem("f_low_done"), k.sem("f_used")
    silu_ready, mult_done = k.sem("f_silu_ready"), k.sem("f_mult_done")
    hid_high, hid_low = k.sem("f_hid_high"), k.sem("f_hid_low")
    y_ready, y_added, zeroed = k.sem("f_y_ready"), k.sem("f_y_added"), k.sem("f_zeroed")
    r = residual_sems(k, "f_res", None, None)
    silu = k.ex[:, 0:2 * HALF].rearrange("p (b t) -> p b t", b=2)
    hid_raw = k.ex[:, 2 * HALF:4 * HALF].rearrange("p (b t) -> p b t", b=2)

    def unit_of(c, p):
        if p < 2 * c:
            return p // 4, p % 4 == 0
        return c // 2 + (p - 2 * c) // 4, (p - 2 * c) % 4 == 0

    def raw(c, p):
        slot = s.slot(u0 + unit_of(c, p)[0])
        if p < 2 * c:
            return slot[:, 0:SLOT].rearrange("p (k s n) -> p k s n", k=KD, s=2)[:, :, p % 2, (p // 2 % 2) * P:(p // 2 % 2 + 1) * P]
        return slot[:, ((p - 2 * c) % 4) * D:((p - 2 * c) % 4 + 1) * D]

    def piece(area, c, p):
        b = area[:, (p % W_BUFS) * W_PIECE:(p % W_BUFS + 1) * W_PIECE]
        return b.rearrange("p (k n) -> p k n", k=KD) if p < 2 * c else b

    s.release = {}
    for g, c in enumerate(chunks):
        for p in range(3 * c):
            s.release[u0 + g * units[0] + unit_of(c, p)[0]] = (low_done, g * per + p + 1)

    with nc.Block() as block:

        @block.sync
        def _(sp):
            s.send(sp, u0 + sum(units) + RING)

        @block.tensor
        def _(pe):
            pe.nop().then_inc(used, W_BUFS)

            def group(g, c):
                for p in range(2 * c):
                    q, side = p // 2, p % 2
                    bank = 2 * (q % 4) + side
                    if q < 4:
                        pe.wait_ge(y_added, g * 8 + (bank + 1))
                    else:
                        pe.wait_ge(mult_done, g * F_GROUP + (q - 1))
                    pe.wait_ge(low_done, g * per + (p + 1))
                    wh, wl = piece(k.fw_high, c, p), piece(k.fw_low, c, p)
                    for m in range(KD):
                        if p == 0:
                            pe.wait_ge(u_low, m + 1)
                        nc.tensor.matmul(k.ps[:, bank, :], wh[:, m, :], k.u_high[:, m, :], start=(m == 0), stop=False)
                        nc.tensor.matmul(k.ps[:, bank, :], wh[:, m, :], k.u_low[:, m, :], start=False, stop=False)
                        last = nc.tensor.matmul(k.ps[:, bank, :], wl[:, m, :], k.u_high[:, m, :], start=False, stop=(m == KD - 1))
                    last.then_inc(used, 1)
                for f in range(c):
                    p = 2 * c + f
                    pe.wait_ge(low_done, g * per + (p + 1))
                    pe.wait_ge(hid_low, g * F_GROUP + (f + 1))
                    wh, wl = piece(k.fw_high, c, p), piece(k.fw_low, c, p)
                    for i in range(NT):
                        if f == 0:
                            pe.wait_ge(mult_done, g * F_GROUP + (2 + max(q for q in range(c) if q % 4 == i) + 1))
                        hh, hl = (h[:, f, i * P:(i + 1) * P] for h in (k.fh_high, k.fh_low))
                        for half in range(2):
                            cols = slice(half * HALF, (half + 1) * HALF)
                            out = k.ps[:, 2 * i + half, :]
                            nc.tensor.matmul(out, hh, wh[:, cols], start=(f == 0), stop=False)
                            nc.tensor.matmul(out, hh, wl[:, cols], start=False, stop=False)
                            last = nc.tensor.matmul(out, hl, wh[:, cols], start=False, stop=(f == c - 1))
                            if f == c - 1 and (i, half) != (NT - 1, 1):
                                last.then_inc(y_ready, 1)
                    last.then_inc(used, 1)

            with pe.Fori(0, last_g) as g:
                group(g, F_GROUP)
            group(last_g, chunks[-1])

        def steps(engine, split, post, g, c, last):
            for p in range(3 * c):
                if p == 3 * c - 1:
                    post(g, c, p)
                if p + W_BUFS < 3 * c:
                    split(g, c, p + W_BUFS)
                elif not last:
                    split(g + 1, F_GROUP, p + W_BUFS - 3 * c)
                if p < 3 * c - 1:
                    post(g, c, p)

        @block.scalar
        def _(act):
            def split(g, c, p):
                n, first = unit_of(c, p)
                if first:
                    n += u0
                    act.wait_ge(s.loaded[n % RING], s.value[n] + g * (s.value[n + units[0]] - s.value[n])
                                if c == F_GROUP else s.value[n + last_g * units[0]])
                act.wait_ge(used, g * per + (p + 1))
                nc.scalar.activation(piece(k.fw_high, c, p), raw(c, p), ACT.Copy).then_inc(high_done, 1)

            def post(g, c, p):
                q = p // 2
                if p < 2 * c and p % 2:
                    act.wait_ge(used, g * per + (p + W_BUFS + 1))
                    act.wait_ge(mult_done, g * F_GROUP + (q + 1))
                    nc.scalar.activation(silu[:, q % 2, :], k.ps[:, 2 * (q % 4), :], ACT.Silu).then_inc(silu_ready, 1)
                elif 0 < p <= 2 * c and p % 2 == 0:
                    q -= 1
                    act.wait_ge(mult_done, g * F_GROUP + (2 + q + 1))
                    nc.scalar.activation(k.fh_high[:, q, :], hid_raw[:, q % 2, :], ACT.Copy).then_inc(hid_high, 1)

            for m in range(KD):
                nc.scalar.activation(k.u_high[:, m, :], k.u_raw[:, m, :], ACT.Copy).then_inc(u_high, 1)
                if m in (1, 3):
                    split(0, F_GROUP, m // 2)
            with act.Fori(0, last_g) as g:
                steps(act, split, post, g, F_GROUP, False)
            steps(act, split, post, last_g, chunks[-1], True)
            residual_scalar(k, act, r, range(NT), False, lambda n: act.wait_ge(y_added, 8 * (last_g + 1) + 2 * (n + 1)))

        @block.gpsimd
        def _(pool):
            pool.memset(k.tok[:, :, :], 0.0).then_inc(zeroed, 1)

        @block.vector
        def _(dve):
            dve.nop().then_inc(y_added, 8)
            dve.nop().then_inc(mult_done, 2)

            def split(g, c, p):
                dve.wait_ge(high_done, g * per + (p + 1))
                nc.vector.tensor_tensor(piece(k.fw_low, c, p), raw(c, p), piece(k.fw_high, c, p).bitcast(F32), ALU.subtract).then_inc(low_done, 1)

            def post(g, c, p):
                q = p // 2
                if p < 2 * c and p % 2:
                    dve.wait_ge(silu_ready, g * F_GROUP + (q + 1))
                    nc.vector.tensor_tensor(hid_raw[:, q % 2, :], silu[:, q % 2, :], k.ps[:, 2 * (q % 4) + 1, :],
                                            ALU.mult).then_inc(mult_done, 1)
                elif 0 < p <= 2 * c and p % 2 == 0:
                    q -= 1
                    dve.wait_ge(hid_high, g * F_GROUP + (q + 1))
                    nc.vector.tensor_tensor(k.fh_low[:, q, :], hid_raw[:, q % 2, :], k.fh_high[:, q, :].bitcast(F32),
                                            ALU.subtract).then_inc(hid_low, 1)
                elif p == 3 * c - 1:
                    for b in range(8):
                        if b < 7:
                            dve.wait_ge(y_ready, g * 7 + (b + 1))
                        else:
                            dve.wait_ge(used, g * per + (W_BUFS + 3 * c))
                        y = k.tok[:, b // 2, (b % 2) * HALF:(b % 2 + 1) * HALF]
                        nc.vector.tensor_tensor(y, y, k.ps[:, b, :], ALU.add).then_inc(y_added, 1)

            for m in range(KD):
                dve.wait_ge(u_high, m + 1)
                nc.vector.tensor_tensor(k.u_low[:, m, :], k.u_raw[:, m, :], k.u_high[:, m, :].bitcast(F32), ALU.subtract).then_inc(u_low, 1)
                if m in (1, 3):
                    split(0, F_GROUP, m // 2)
            dve.wait_ge(zeroed, 1)
            with dve.Fori(0, last_g) as g:
                steps(dve, split, post, g, F_GROUP, False)
            steps(dve, split, post, last_g, chunks[-1], True)
            residual_vector(k, dve, r, range(NT), 1, False)



def hgrn_in(k):
    nc, s, u0 = k.nc, k.stream, k.plan["h_in"]
    ready, copied_a, copied_v = k.sem("hi_ready"), k.sem("hi_copied_a"), k.sem("hi_copied_v")
    row_sig, lb_in, lb_row, f_made, act_own, own = (k.sem("hi_" + n) for n in ("row_sig", "lb_in", "lb_row", "f_made", "act_own", "own"))
    raised = k.sem("hi_raised")
    lb = k.tok[:, 2:4, :].rearrange("p a n -> p (a n)")
    bias_row = k.resid[0:1, 0:2, :].rearrange("p a n -> p (a n)")
    units = 10
    jobs = []
    for u in range(4):
        jobs += [(u, "f_row", i) for i in range(2)] + [(u, "f_col", i) for i in range(4)]
    jobs += [(u, "v", i) for u in (4, 5) for i in range(4)]
    jobs += [(u, "q", i) for u in (6, 7) for i in range(4)]
    jobs += [(u, "g", i) for u in (8, 9) for i in range(4)]
    last_of = {u: max(n for n, j in enumerate(jobs) if j[0] == u) for u in range(units)}
    s.release = {u0 + u: (ready, last_of[u] + 1) for u in range(units)}
    by_act = [j[1] != "v" and j[1] != "q" for j in jobs]
    BANKS = 6

    def freed(n):
        return (copied_a, sum(by_act[:n + 1])) if by_act[n] else (copied_v, n + 1 - sum(by_act[:n + 1]))

    with nc.Block() as block:

        @block.sync
        def _(sp):
            sp.dma_start(bias_row, k.a["h_b_f"].rearrange("o a n -> o (a n)")).then_inc(lb_in, 16)
            sp.dma_start(lb, k.a["h_lb_raw"].rearrange("o a n -> o (a n)").to_broadcast([P, 2 * D])).then_inc(lb_in, 16)
            s.send(sp, u0 + units + RING)

        @block.tensor
        def _(pe):
            pe.wait_ge(lb_in, 32)
            for n, (u, kind, i) in enumerate(jobs):
                if n == 0 or jobs[n - 1][0] != u:
                    s.arrived(pe, u0 + u)
                w = rows_of(HALF)(s.slot(u0 + u))
                bank = n % BANKS
                if n >= BANKS:
                    pe.wait_ge(*freed(n - BANKS))
                rows = kind in ("f_row", "v")
                width = HALF if rows else LAT
                for c in range(KD):
                    if rows:
                        lhs, rhs = k.u_cols[:, c, i * P:(i + 1) * P], w[:, c, :]
                    else:
                        lhs, rhs = w[:, c, i * P:(i + 1) * P], k.u_cols[:, c, CTX:T]
                    last = nc.tensor.matmul(k.ps[:, bank, 0:width], lhs, rhs, start=(c == 0),
                                            stop=(c == KD - 1 and kind != "f_row"))
                if kind == "f_row":
                    last = nc.tensor.matmul(k.ps[:, bank, :], k.ones[0:1, :], bias_row[0:1, u * HALF:(u + 1) * HALF], start=False, stop=True)
                last.then_inc(ready, 1)

        @block.scalar
        def _(act):
            act.wait_ge(lb_row, 1)
            nc.scalar.activation(lb, lb, ACT.Exp).then_inc(lb_row, 1)
            for n, (u, kind, i) in enumerate(jobs):
                if not by_act[n]:
                    continue
                act.wait_ge(ready, n + 1)
                if kind == "f_row":
                    dst = k.f_rows[:, i, u * HALF:(u + 1) * HALF]
                    nc.scalar.activation(dst, k.ps[:, n % BANKS, :], ACT.Sigmoid).then_inc(copied_a, 1)
                elif kind == "f_col":
                    c = (u % 2) * 4 + i
                    col = (u // 2) * KD + c
                    nc.scalar.activation(k.f_cols[:, u // 2, c, :], k.ps[:, n % BANKS, 0:LAT], ACT.Sigmoid,
                                         bias=k.vcol[:, 104 + col:105 + col]).then_inc(copied_a, 1)
                else:
                    c = (u - 8) * 4 + i
                    nc.scalar.activation(k.g_cols(c), k.ps[:, n % BANKS, 0:LAT], ACT.Sigmoid).then_inc(copied_a, 1)
            act.wait_ge(f_made, 16)
            for i in range(2):
                nc.scalar.activation(k.f_rows[:, i, :], k.f_rows[:, i, :], ACT.Ln)

        @block.gpsimd
        def _(pool):
            pool.wait_ge(lb_in, 32)
            pool.tensor_tensor(lb, lb, lb, ALU.subtract).then_inc(lb_row, 1)

        @block.vector
        def _(dve):
            chain = Chain(dve, own)
            dve.wait_ge(lb_row, 2)
            inverse = k.k_rows[:, 0, :]
            chain.link(nc.vector.reciprocal(inverse, lb))
            chain.link(nc.vector.tensor_tensor(inverse, lb, inverse, ALU.mult))
            chain.link(nc.vector.tensor_tensor(lb, inverse, inverse, ALU.subtract))
            for n, (u, kind, i) in enumerate(jobs):
                if kind == "f_row":
                    dve.wait_ge(*freed(n))
                    f = k.f_rows[:, i, u * HALF:(u + 1) * HALF]
                    kk = k.k_rows[:, i, u * HALF:(u + 1) * HALF]
                    chain.link(nc.vector.scalar_tensor_tensor(out=kk, in0=f, scalar=-1.0, in1=lb[:, u * HALF:(u + 1) * HALF],
                                                              op0=ALU.add, op1=ALU.mult))
                    chain.link(nc.vector.tensor_tensor(f, f, kk, ALU.subtract))
                    chain.link(nc.vector.tensor_scalar(kk, f, -1.0, 1.0, ALU.mult, ALU.add))
                    nc.vector.tensor_scalar(f, f, 2.0 ** -63, None, ALU.max).then_inc(f_made, 2)
                elif kind == "f_col":
                    dve.wait_ge(*freed(n))
                    c = (u % 2) * 4 + i
                    col = (u // 2) * KD + c
                    f = k.f_cols[:, u // 2, c, :]
                    nc.vector.tensor_scalar(f, f, k.lb_rest[:, col:col + 1], k.lb_col[:, col:col + 1], ALU.mult, ALU.add)
                elif kind == "v":
                    dve.wait_ge(ready, n + 1)
                    nc.vector.tensor_copy(k.v_rows[:, i, (u - 4) * HALF:(u - 3) * HALF], k.ps[:, n % BANKS, :]).then_inc(copied_v, 1)
                elif kind == "q":
                    dve.wait_ge(ready, n + 1)
                    nc.vector.tensor_copy(k.q_cols[:, (u - 6) * 4 + i, :], k.ps[:, n % BANKS, 0:LAT]).then_inc(copied_v, 1)



def hgrn_state(k):
    nc = k.nc
    summed, decayed, scaled, stated, copied = (k.sem("hs_" + n) for n in ("summed", "decayed", "scaled", "stated", "copied"))
    rest = k.sem("hs_rest")
    decay = k.junk.rearrange("p (b n) -> p b n", b=2)
    jobs = [(d, half, i) for d in range(2) for half in range(2) for i in range(2)]

    with nc.Block() as block:

        @block.tensor
        def _(pe):
            for n, (d, half, i) in enumerate(jobs):
                if n >= 4:
                    pe.wait_ge(decayed, n - 3)
                cols = slice(d * D + half * HALF, d * D + (half + 1) * HALF)
                own = (k.after, k.before)[d]
                other = (i == 0) if d == 0 else (i == 1)
                last = nc.tensor.matmul(k.ps[:, n % 4, :], own[:, :], k.f_rows[:, i, cols], start=True, stop=not other)
                if other:
                    last = nc.tensor.matmul(k.ps[:, n % 4, :], k.ones[:, :], k.f_rows[:, 1 - i, cols], start=False, stop=True)
                last.then_inc(summed, 1)
            for g in range(4):
                d, half = g // 2, g % 2
                pe.wait_ge(scaled, 2 * g + 2)
                for q in range(4):
                    h = half * 4 + q
                    for i in range(2):
                        last = nc.tensor.matmul(k.ps[:, 4 + g, q * P:(q + 1) * P],
                                                k.k_rows[:, i, d * D + h * P:d * D + (h + 1) * P],
                                                k.v_rows[:, i, h * P:(h + 1) * P], start=(i == 0), stop=(i == 1))
                last.then_inc(stated, 1)

        @block.scalar
        def _(act):
            for n in range(len(jobs)):
                act.wait_ge(summed, n + 1)
                if n >= 2:
                    act.wait_ge(scaled, n - 1)
                nc.scalar.activation(decay[:, n % 2, :], k.ps[:, n % 4, :], ACT.Exp).then_inc(decayed, 1)
            for g in range(4):
                act.wait_ge(stated, g + 1)
                nc.scalar.activation(k.state[:, 4 * g:4 * g + 4, :], k.ps[:, 4 + g, :].rearrange("p (h c) -> p h c", h=4), ACT.Copy)

        @block.vector
        def _(dve):
            for n, (d, half, i) in enumerate(jobs):
                cols = slice(d * D + half * HALF, d * D + (half + 1) * HALF)
                dve.wait_ge(decayed, n + 1)
                nc.vector.tensor_tensor(k.k_rows[:, i, cols], k.k_rows[:, i, cols], decay[:, n % 2, :], ALU.mult).then_inc(scaled, 1)



def hgrn_pairs(k):
    nc = k.nc
    q_made, k_made, q_grown, k_grown, ends_made = (k.sem("hp_" + n) for n in ("q_made", "k_made", "q_grown", "k_grown", "ends_made"))
    paired, taken, sum_made = k.sem("hp_paired"), k.sem("hp_taken"), k.sem("hp_sum_made")
    q_f, k_f, ends = k.q_fac, k.k_fac, k.f_cols
    G = 4

    def halves(x, d, g, size):
        v = x[:, d, G * g:G * g + G, :].rearrange("p h (b two l) -> p (h b) two l", two=2, l=size)
        return v[:, :, 0, :], v[:, :, 1, :]

    def end_of(d, g, size):
        v = ends[:, d, G * g:G * g + G, :].rearrange("p h (b two l) -> p (h b) two l", two=2, l=size)
        return v[:, :, 0, 0:1], v[:, :, 1, 0:1]

    def cut(x, size, side):
        return x.rearrange("p (b two l) -> p b two l", two=2, l=size)[:, :, side, :]

    n_blocks = lambda size: G * LAT // (2 * size)

    with nc.Block() as block:

        @block.tensor
        def _(pe):
            for level in range(-1, LEVELS + 1):
                for g in range(2):
                    n = (level + 1) * 2 + g
                    if level < 1:
                        pe.wait_ge(q_made, 2 * g + 2)
                        pe.wait_ge(sum_made, g + 1)
                    else:
                        pe.wait_ge(q_grown, 2 * (n - 3))
                        pe.wait_ge(k_grown, 2 * (n - 3))
                    if n >= 4:
                        pe.wait_ge(taken, 2 * (n - 3))
                    for i in range(2):
                        bank = (n % 4) * 2 + i
                        for q in range(G):
                            h = G * g + q
                            out = k.ps[:, bank, q * P:(q + 1) * P]
                            t = slice(i * P, (i + 1) * P)
                            if level < 0:
                                last = nc.tensor.matmul(out, k.k_sum[:, h, t], k.q_cols[:, h, t], start=True, stop=True)
                            elif level < LEVELS:
                                size = 2 ** level
                                for d, side in ((0, 1), (1, 0)):
                                    last = nc.tensor.matmul(cut(out, size, side), k_f[:, d, h, t], cut(q_f[:, d, h, t], size, side),
                                                            start=True, stop=True)
                            else:
                                last = nc.tensor.matmul(out, k_f[:, i, h, t], q_f[:, i, h, (1 - i) * P:(2 - i) * P],
                                                        start=True, stop=True)
                        last.then_inc(paired, 1)

        @block.vector
        def _(dve):
            for g in range(2):
                for d in range(2):
                    nc.vector.tensor_tensor(q_f[:, d, G * g:G * g + G, :], k.q_cols[:, G * g:G * g + G, :],
                                            ends[:, d, G * g:G * g + G, :], ALU.mult).then_inc(q_made, 1)

            def take(level, g):
                n = (level + 1) * 2 + g
                for i in range(2):
                    bank = (n % 4) * 2 + i
                    dve.wait_ge(paired, 2 * n + i + 1)
                    src = k.ps[:, bank, :].rearrange("p (h t) -> p h t", h=G)
                    near, cross = k.pair_near[:, g, i, :, :], k.pair_cross[:, g, i, :, :]
                    if level < 0:
                        nc.vector.tensor_tensor(near, src, k.ident[:, :].unsqueeze(1).to_broadcast([P, G, P]),
                                                ALU.mult).then_inc(taken, 1)
                    elif level < LEVELS:
                        dve.wait_ge(taken, 2 * (n - 2) + i + 1)
                        nc.vector.copy_predicated(near, k.level_mask[:, level, :].unsqueeze(1).to_broadcast([P, G, P]),
                                                  src).then_inc(taken, 1)
                    else:
                        nc.vector.tensor_copy(cross, src).then_inc(taken, 1)

            for level in range(-1, LEVELS + 1):
                for g in range(2):
                    take(level, g)
                    if level >= 0:
                        size = 2 ** level
                        if level:
                            dve.wait_ge(q_grown, 2 * ((level - 1) * 2 + g + 1))
                            dve.wait_ge(ends_made, 4 * ((level - 1) * 2 + g + 1))
                        else:
                            dve.wait_ge(q_made, 4)
                        for d in range(2):
                            side = halves(q_f, d, g, size)[1 - d]
                            end = end_of(d, g, size)[d]
                            nc.vector.tensor_tensor(side, side, end.to_broadcast([P, n_blocks(size), size]),
                                                    ALU.mult).then_inc(q_grown, 1)

        @block.gpsimd
        def _(pool):
            for g in range(2):
                for d in range(2):
                    pool.tensor_scalar(k_f[:, d, G * g:G * g + G, :], ends[:, d, G * g:G * g + G, :], -1.0, 1.0,
                                       ALU.mult, ALU.add).then_inc(k_made, 1)
                pool.wait_ge(k_made, 2 * g + 2)
                pool.tensor_tensor(k.k_sum[:, G * g:G * g + G, :], k_f[:, 0, G * g:G * g + G, :],
                                   k_f[:, 1, G * g:G * g + G, :], ALU.add).then_inc(sum_made, 1)
            for level in range(LEVELS):
                size = 2 ** level
                for g in range(2):
                    n = (level + 1) * 2 + g
                    turn = level * 2 + g
                    pool.wait_ge(paired, 2 * n + 2)
                    if level:
                        pool.wait_ge(k_grown, 2 * ((level - 1) * 2 + g + 1))
                        pool.wait_ge(ends_made, 4 * ((level - 1) * 2 + g + 1))
                    for d in range(2):
                        side = halves(k_f, d, g, size)[d]
                        end = end_of(d, g, size)[1 - d]
                        pool.tensor_tensor(side, side, end.to_broadcast([P, n_blocks(size), size]),
                                           ALU.mult).then_inc(k_grown, 1)
                    pool.wait_ge(q_grown, 2 * (turn + 1))
                    pool.wait_ge(k_grown, 2 * (turn + 1))
                    for d in range(2):
                        left, right = end_of(d, g, size)
                        pool.tensor_tensor(left, left, right, ALU.mult).then_inc(ends_made, 2)



def hgrn_values(k):
    nc = k.nc
    ready = k.sem("hv_ready")
    with nc.Block() as block:

        @block.tensor
        def _(pe):
            for i in range(2):
                for g in range(2):
                    for q in range(4):
                        h = 4 * g + q
                        out = k.ps[:, 2 * i + g, q * P:(q + 1) * P]
                        v = [k.v_rows[:, 2 + j, h * DV:(h + 1) * DV] for j in range(2)]
                        t = slice(i * P, (i + 1) * P)
                        nc.tensor.matmul(out, k.pair_near[:, g, i, q, :], v[i], start=True, stop=False)
                        nc.tensor.matmul(out, k.pair_cross[:, g, 1 - i, q, :], v[1 - i], start=False, stop=False)
                        nc.tensor.matmul(out, k.q_fac[:, 0, h, t], k.state[:, h, :], start=False, stop=False)
                        last = nc.tensor.matmul(out, k.q_fac[:, 1, h, t], k.state[:, 8 + h, :], start=False, stop=True)
                    last.then_inc(ready, 1)

        @block.vector
        def _(dve):
            for n in range(0, 4, 2):
                dve.wait_ge(ready, n + 1)
                nc.vector.tensor_copy(k.tok[:, 2 + n // 2, (n % 2) * HALF:(n % 2 + 1) * HALF], k.ps[:, n, :])

        @block.scalar
        def _(act):
            for n in range(1, 4, 2):
                act.wait_ge(ready, n + 1)
                nc.scalar.activation(k.tok[:, 2 + n // 2, (n % 2) * HALF:(n % 2 + 1) * HALF], k.ps[:, n, :], ACT.Copy)



def routing(k):
    nc = k.nc
    logits_ready, own, diff, expd, chosen, placed = (k.sem("r_" + n) for n in ("logits_ready", "own", "diff", "expd", "chosen", "placed"))
    r = k.route
    L, EQ, CAND, OH1, OH2, L2, COMB, SEL = (r[:, n, :, :] for n in range(8))
    V1, V2, IDX, W1, W2, EX = (r[:, 8 + n // 4, :, 2 * (n % 4):2 * (n % 4) + 1] for n in range(6))
    per = lambda v: v.to_broadcast([P, 2, EXPERTS])

    with nc.Block() as block:

        @block.tensor
        def _(pe):
            for i in range(2):
                for c in range(KD):
                    nc.tensor.matmul(k.ps[:, 0, i * 8:i * 8 + 8], k.u_cols[:, c, CTX + i * P:CTX + (i + 1) * P],
                                     k.w_router[:, c, :], start=(c == 0), stop=False)
                last = nc.tensor.matmul(k.ps[:, 0, i * 8:i * 8 + 8], k.ones[0:1, :], k.b_router[0:1, :], start=False, stop=True)
            last.then_inc(logits_ready, 1)
            pe.wait_ge(chosen, 1)
            nc.tensor.matmul(k.ps[:, 1, 0:8], k.before[:, :], SEL[:, 0, :], start=True, stop=True)
            nc.tensor.matmul(k.ps[:, 1, 8:16], k.ones[:, :], SEL[:, 0, :], start=True, stop=False)
            nc.tensor.matmul(k.ps[:, 1, 8:16], k.before[:, :], SEL[:, 1, :], start=False, stop=True)
            nc.tensor.matmul(k.ps[:, 1, 16:24], k.ones[:, :], SEL[:, 0, :], start=True, stop=False)
            nc.tensor.matmul(k.ps[:, 1, 16:24], k.ones[:, :], SEL[:, 1, :], start=False, stop=True).then_inc(placed, 1)

        @block.scalar
        def _(act):
            act.wait_ge(diff, 1)
            nc.scalar.activation(EX, EX, ACT.Exp).then_inc(expd, 1)

        @block.gpsimd
        def _(pool):
            pool.memset(k.acc[:, :, :], 0.0)

        @block.vector
        def _(dve):
            chain = Chain(dve, own)
            dve.wait_ge(logits_ready, 1)
            chain.link(nc.vector.tensor_copy(L, k.ps[:, 0, 0:16].rearrange("p (i e) -> p i e", i=2)))

            def pick(logits, value, onehot):
                chain.link(nc.vector.tensor_reduce(out=value, in_=logits, op=ALU.max, axis=AX.X))
                chain.link(nc.vector.tensor_tensor(EQ, logits, per(value), ALU.is_equal))
                chain.link(nc.vector.scalar_tensor_tensor(out=CAND, in0=EQ, scalar=-8.0, in1=k.expert_no[:, :, :],
                                                          op0=ALU.mult, op1=ALU.add))
                chain.link(nc.vector.tensor_reduce(out=IDX, in_=CAND, op=ALU.min, axis=AX.X))
                chain.link(nc.vector.tensor_tensor(onehot, CAND, per(IDX), ALU.is_equal))

            pick(L, V1, OH1)
            chain.link(nc.vector.scalar_tensor_tensor(out=L2, in0=OH1, scalar=-3.0e38, in1=L, op0=ALU.mult, op1=ALU.add))
            pick(L2, V2, OH2)
            chain.link(nc.vector.tensor_tensor(SEL, OH1, OH2, ALU.add))
            nc.vector.tensor_tensor(EX, V2, V1, ALU.subtract).then_inc(diff, 1)
            dve.nop().then_inc(chosen, 1)
            dve.wait_ge(expd, 1)
            chain.link(nc.vector.tensor_scalar(W2, EX, 1.0, None, ALU.add))
            chain.link(nc.vector.reciprocal(W1, W2))
            chain.link(nc.vector.tensor_tensor(W2, EX, W1, ALU.mult))
            chain.link(nc.vector.tensor_tensor(OH1, OH1, per(W1), ALU.mult))
            chain.link(nc.vector.tensor_tensor(OH2, OH2, per(W2), ALU.mult))
            nc.vector.memset(k.place[:, :, EXPERTS:EXPERTS + 1], -1.0)
            nc.vector.tensor_tensor(k.comb[:, :, :], OH1, OH2, ALU.add)
            dve.wait_ge(placed, 1)
            chain.link(nc.vector.scalar_tensor_tensor(out=EQ, in0=k.ps[:, 1, 0:16].rearrange("p (i e) -> p i e", i=2),
                                                      scalar=1.0, in1=SEL, op0=ALU.add, op1=ALU.mult))
            nc.vector.tensor_scalar(k.place[:, :, 0:EXPERTS], EQ, -1.0, None, ALU.add)
            chain.link(nc.vector.tensor_reduce(out=V1[:, 0, :], in_=k.ps[:, 1, 16:24], op=ALU.max, axis=AX.X))
            nc.vector.tensor_scalar(k.passes[:, 0:1], V1[:, 0, :], float(P), 1.0, ALU.is_gt, ALU.add)



def experts(k):
    nc, a = k.nc, k.a
    S = Names()
    S.used, S.high_done, S.low_done = k.sem("e_used"), k.sem("e_high_done"), k.sem("e_low_done")
    S.silu_ready, S.hid_done = k.sem("e_silu_ready"), k.sem("e_hid_done")
    S.places_ready, S.gathered = k.sem("e_places_ready"), k.sem("e_gathered")
    S.list_made, S.list_high, S.list_low = k.sem("e_list_made"), k.sem("e_list_high"), k.sem("e_list_low")
    S.pturned, S.pcopied, S.pcleared = (k.sem("e_" + n) for n in ("pturned", "pcopied", "pcleared"))
    S.hturned, S.hid_high, S.hid_low = k.sem("e_hturned"), k.sem("e_hid_high"), k.sem("e_hid_low")
    S.y_high, S.y_low, S.scattered, S.added = (k.sem("e_" + n) for n in ("y_high", "y_low", "scattered", "added"))
    loaded = [k.sem(f"e_loaded{i}") for i in range(E_RING)]
    HG = -(-FC // 4)
    per_slot = E_UNITS // E_RING
    Y0 = 2 * E_TILES
    PIECES = 2 * E_UNITS
    GS = KD // 2
    HIDDEN_TURNS = (15, 19, 23, 27, 33, 35)
    assert len(HIDDEN_TURNS) == HG

    down_units = [(0, 6), (6, 5), (11, 6), (17, 5)]
    down_pieces = [x for f, m in down_units for x in ((f, 3), (f + 3, m - 3))]

    def slot(j):
        return k.e_ring[:, (j % E_RING) * E_SLOT:(j % E_RING + 1) * E_SLOT]

    def piece_shape(p):
        if p < 2 * Y0:
            return GS, E_N, (p % 2) * GS * E_N
        m = down_pieces[(p - 2 * Y0) % len(down_pieces)][1]
        return m, HALF, (p % 2) * 3 * HALF

    def piece(buffer, p):
        m, n, _ = piece_shape(p)
        return buffer[:, (p % E_BUFS) * E_PIECE:(p % E_BUFS) * E_PIECE + m * n].rearrange("p (c n) -> p c n", c=m)

    def raw(p):
        m, n, first = piece_shape(p)
        return slot(p // 2)[:, first:first + m * n].rearrange("p (c n) -> p c n", c=m)

    def passes(engine):
        return engine.value_load(k.passes[0:1, 0:1], min_val=1, max_val=2)

    with nc.Block() as block:

        @block.sync
        def _(sp):
            n = passes(sp)
            with sp.Fori(0, n) as ps_:
                with sp.Fori(0, EXPERTS) as e:
                    it = sp.snap(ps_ * EXPERTS + e)
                    gu = a["e_w_gu"][0, e]
                    dn = a["e_w_down"][0, e]
                    for j in range(E_UNITS):
                        if j < Y0:
                            t, side = j // 2, j % 2
                            src = gu[:, side * FFN + t * E_N:side * FFN + (t + 1) * E_N].rearrange("(k p) n -> p k n", p=P)
                            dst = slot(j)[:, 0:KD * E_N].rearrange("p (k n) -> p k n", k=KD)
                        else:
                            half, (f, m) = (j - Y0) // 4, down_units[(j - Y0) % 4]
                            src = dn[f * P:(f + m) * P, half * HALF:(half + 1) * HALF].rearrange("(k p) n -> p k n", p=P)
                            dst = slot(j)[:, 0:m * HALF].rearrange("p (k n) -> p k n", k=m)
                        need = sp.snap(it * PIECES + (2 * j + 2))
                        sp.wait_ge(S.low_done, need)
                        sp.dma_start(dst, src).then_inc(loaded[j % E_RING], 16)

        @block.tensor
        def _(pe):
            n = passes(pe)
            pe.nop().then_inc(S.used, E_BUFS)

            def gather(m):
                pe.wait_ge(S.places_ready, m + 1)
                for c in range(KD):
                    for i in range(2):
                        last = nc.tensor.matmul(k.ps[:, 4 + c // 4, (c % 4) * P:(c % 4 + 1) * P],
                                                k.tok[:, 2 + i, c * P:(c + 1) * P], k.places[:, i, :],
                                                start=(i == 0), stop=(i == 1))
                last.then_inc(S.gathered, 1)

            def three_passes(it, p, out, high, low, first, chunks, total):
                pe.wait_ge(S.low_done, it * PIECES + (p + 1 + 2 * E_RING))
                w_high, w_low = piece(k.w_high, p), piece(k.w_low, p)
                for c in range(chunks):
                    f = first + c
                    nc.tensor.matmul(out, high[:, f, :], w_high[:, c, :], start=(f == 0), stop=False)
                    nc.tensor.matmul(out, high[:, f, :], w_low[:, c, :], start=False, stop=False)
                    last = nc.tensor.matmul(out, low[:, f, :], w_high[:, c, :], start=False, stop=(f == total - 1))
                last.then_inc(S.used, 1)

            def scatter(y_count, add_count, half):
                pe.wait_ge(S.y_low, y_count)
                pe.wait_ge(S.added, add_count + 1)
                for i in range(2):
                    for n, part in enumerate((k.ey_high, k.ey_low)):
                        last = nc.tensor.matmul(k.ps[:, 6 + i, :], k.place_cols[:, i * P:(i + 1) * P],
                                                part[:, half * HALF:(half + 1) * HALF], start=(n == 0), stop=(n == 1))
                    last.then_inc(S.scattered, 1)

            def turn_places(it, adds, e):
                pe.wait_ge(S.added, adds + 3)
                for i in range(2):
                    nc.tensor.transpose(k.ps[:, 6, i * P:(i + 1) * P], k.places[:, i, :], k.ident[:, :])
                for i in range(2):
                    last = nc.tensor.matmul(k.ps[:, 6, 256:257], k.places[:, i, :], k.comb[:, i, bass.ds(e, 1)],
                                            start=(i == 0), stop=(i == 1))
                last.then_inc(S.pturned, 1)

            def turn_hidden(it, g):
                m = min(4, FC - 4 * g)
                tiles = min(E_TILES, -(-(4 * g + m) * P // E_N))
                pe.wait_ge(S.hid_done, it * E_TILES + tiles + 2)
                if g == 1:
                    pe.wait_ge(S.pcopied, it + 1)
                elif g >= 2:
                    pe.wait_ge(S.hid_low, it * HG + g - 1)
                for q in range(m):
                    f = 4 * g + q
                    last = nc.tensor.transpose(k.ps[:, 7 - g % 2, q * P:(q + 1) * P], k.e_hid[:, f * P:(f + 1) * P],
                                               k.ident[:, :])
                last.then_inc(S.hturned, 1)

            with pe.Fori(0, n) as ps_:
                gather(ps_ * 9)
                with pe.Fori(0, EXPERTS) as e:
                    it = ps_ * EXPERTS + e
                    ys = ps_ * 17 + 2 * e
                    adds = ps_ * 34 + 4 * e
                    pe.wait_ge(S.list_low, ps_ * 9 + e + 1)

                    def after(p):
                        if p == 3:
                            scatter(ys + 1, adds, 1)
                        elif p == 11:
                            turn_places(it, adds, e)
                        elif p == 21:
                            gather(ps_ * 9 + e + 1)
                        elif p in HIDDEN_TURNS:
                            turn_hidden(it, HIDDEN_TURNS.index(p))
                        elif p == 42:
                            pe.wait_ge(S.hid_low, it * HG + HG)
                            scatter(ys + 2, adds + 2, 0)

                    for t in range(E_TILES):
                        pe.wait_ge(S.hid_done, it * E_TILES + t + 1)
                        for side in range(2):
                            for b in range(2):
                                p = 4 * t + 2 * side + b
                                three_passes(it, p, k.ps[:, 2 * (t % 2) + side, 0:E_N], k.list_h, k.list_l, b * GS, GS, KD)
                                after(p)
                    pe.wait_ge(S.list_made, ps_ * 9 + e + 2)
                    for half in range(2):
                        for b, (f, m) in enumerate(down_pieces):
                            if half == 0:
                                pe.wait_ge(S.hid_low, it * HG + ((f + m - 1) // 4 + 1))
                            p = 2 * Y0 + 8 * half + b
                            three_passes(it, p, k.ps[:, 4 + half, :], k.hid_h, k.hid_l, f, m, FC)
                            after(p)
                scatter(ps_ * 17 + 17, ps_ * 34 + 32, 1)

        @block.scalar
        def _(act):
            n = passes(act)

            def split(it, p):
                if p % 2 == 0:
                    j = p // 2
                    act.wait_ge(loaded[j % E_RING], it * (16 * per_slot) + 16 * (j // E_RING + 1))
                act.wait_ge(S.used, it * PIECES + (p + 1))
                nc.scalar.activation(piece(k.w_high, p), raw(p), ACT.Copy).then_inc(S.high_done, 1)

            def list_high(m):
                act.wait_ge(S.list_made, m + 1)
                nc.scalar.activation(k.list_h, k.list_raw, ACT.Copy).then_inc(S.list_high, 1)

            def silu(it, t):
                act.wait_ge(S.used, it * PIECES + (E_BUFS + 4 * t + 2))
                act.wait_ge(S.hid_done, it * E_TILES + (t + 1))
                nc.scalar.activation(k.e_silu[:, t % 2, :], k.ps[:, 2 * (t % 2), 0:E_N], ACT.Silu).then_inc(S.silu_ready, 1)

            def y_high(pieces, half):
                act.wait_ge(S.used, pieces + E_BUFS)
                nc.scalar.activation(k.ey_high[:, half * HALF:(half + 1) * HALF], k.ps[:, 4 + half, :], ACT.Copy,
                                     scale=k.list_weight[:, 0:1]).then_inc(S.y_high, 1)

            with act.Fori(0, n) as ps_:
                act.wait_ge(S.scattered, ps_ * 34 + 1)
                nc.scalar.activation(k.place_cols[:, :], k.slot_no[:, :], ACT.Copy, scale=0.0)
                nc.scalar.activation(k.list_weight[:, 0:1], k.slot_no[:, 0:1], ACT.Copy, scale=0.0).then_inc(S.pcleared, 1)
                list_high(ps_ * 9)
                act.wait_ge(S.pcleared, ps_ + 1)
                with act.Fori(0, EXPERTS) as e:
                    it = ps_ * EXPERTS + e
                    for p in range(E_BUFS):
                        split(it, p)
                    act.wait_ge(S.gathered, ps_ * 9 + e + 1)
                    y_high(it * PIECES, 1)
                    for p in range(PIECES):
                        if p + E_BUFS < PIECES:
                            split(it, p + E_BUFS)
                        if p < 2 * Y0 and p % 4 == 1:
                            silu(it, p // 4)
                        if p == 12:
                            act.wait_ge(S.pturned, it + 1)
                            nc.scalar.activation(k.place_cols[:, :], k.ps[:, 6, 0:256], ACT.Copy)
                            nc.scalar.activation(k.list_weight[:, 0:1], k.ps[:, 6, 256:257], ACT.Copy).then_inc(S.pcopied, 1)
                        if p - 1 in HIDDEN_TURNS:
                            g = HIDDEN_TURNS.index(p - 1)
                            m = min(4, FC - 4 * g)
                            act.wait_ge(S.hturned, it * HG + g + 1)
                            nc.scalar.activation(k.hid_h[:, 4 * g:4 * g + m, :],
                                                 k.ps[:, 7 - g % 2, 0:m * P].rearrange("p (f t) -> p f t", f=m), ACT.Copy).then_inc(S.hid_high, 1)
                        if p == 32:
                            list_high(ps_ * 9 + e + 1)
                        if p == 39:
                            act.wait_ge(S.pcopied, it + 1)
                            y_high(it * PIECES + 40, 0)
                y_high(ps_ * (EXPERTS * PIECES) + EXPERTS * PIECES, 1)

        @block.vector
        def _(dve):
            n = passes(dve)
            dve.nop().then_inc(S.hid_done, 2)
            dve.nop().then_inc(S.added, 1)
            dve.nop().then_inc(S.scattered, 1)
            dve.nop().then_inc(S.low_done, 2 * E_RING)

            def split(it, p):
                dve.wait_ge(S.high_done, it * PIECES + (p + 1))
                nc.vector.tensor_tensor(piece(k.w_low, p), raw(p), piece(k.w_high, p).bitcast(F32), ALU.subtract).then_inc(S.low_done, 1)

            def find(ps_, e):
                for i in range(2):
                    last = nc.vector.tensor_scalar(k.places[:, i, :], k.slot_no[:, bass.ds(ps_ * P, P)],
                                                   k.place[:, i, bass.ds(e, 1)], None, ALU.is_equal)
                last.then_inc(S.places_ready, 1)

            def take(m):
                dve.wait_ge(S.gathered, m + 1)
                for c in range(KD):
                    last = nc.vector.tensor_scalar(k.list_raw[:, c, :], k.ps[:, 4 + c // 4, (c % 4) * P:(c % 4 + 1) * P],
                                                   k.mod_scale[:, 1, c, 1:2], k.mod_cols[:, 3, c, 1:2], ALU.mult, ALU.add)
                last.then_inc(S.list_made, 1)

            def list_low(m):
                dve.wait_ge(S.list_high, m + 1)
                nc.vector.tensor_tensor(k.list_l, k.list_raw, k.list_h.bitcast(F32), ALU.subtract).then_inc(S.list_low, 1)

            def hidden(it, t):
                dve.wait_ge(S.used, it * PIECES + (E_BUFS + 4 * t + 4))
                dve.wait_ge(S.silu_ready, it * E_TILES + (t + 1))
                nc.vector.tensor_tensor(k.e_hid[:, t * E_N:(t + 1) * E_N], k.e_silu[:, t % 2, :],
                                        k.ps[:, 2 * (t % 2) + 1, 0:E_N], ALU.mult).then_inc(S.hid_done, 1)

            def y_low(count, half):
                dve.wait_ge(S.y_high, count)
                cols = slice(half * HALF, (half + 1) * HALF)
                nc.vector.scalar_tensor_tensor(out=k.ey_low[:, cols], in0=k.ps[:, 4 + half, :], scalar=k.list_weight[:, 0:1],
                                               in1=k.ey_high[:, cols].bitcast(F32), op0=ALU.mult, op1=ALU.subtract).then_inc(S.y_low, 1)

            def add(count, half):
                for i in range(2):
                    dve.wait_ge(S.scattered, count + i + 2)
                    part = k.acc[:, i, half * HALF:(half + 1) * HALF]
                    nc.vector.tensor_tensor(part, part, k.ps[:, 6 + i, :], ALU.add).then_inc(S.added, 1)

            with dve.Fori(0, n) as ps_:
                find(ps_, 0)
                take(ps_ * 9)
                list_low(ps_ * 9)
                with dve.Fori(0, EXPERTS) as e:
                    it = ps_ * EXPERTS + e
                    ys, adds = ps_ * 17 + 2 * e, ps_ * 34 + 4 * e
                    for p in range(E_BUFS):
                        split(it, p)
                    y_low(ys + 1, 1)
                    for p in range(PIECES):
                        if p + E_BUFS < PIECES:
                            split(it, p + E_BUFS)
                        if p < 2 * Y0 and p % 4 == 3:
                            hidden(it, p // 4)
                        if p == 4:
                            add(adds, 1)
                        if p == 13:
                            dve.wait_ge(S.pturned, it + 1)
                            find(ps_, e + 1)
                        if p == 22:
                            take(ps_ * 9 + e + 1)
                        if p - 1 in HIDDEN_TURNS:
                            g = HIDDEN_TURNS.index(p - 1)
                            m = min(4, FC - 4 * g)
                            dve.wait_ge(S.hid_high, it * HG + g + 1)
                            nc.vector.tensor_tensor(k.hid_l[:, 4 * g:4 * g + m, :],
                                                    k.ps[:, 7 - g % 2, 0:m * P].rearrange("p (f t) -> p f t", f=m),
                                                    k.hid_h[:, 4 * g:4 * g + m, :].bitcast(F32), ALU.subtract).then_inc(S.hid_low, 1)
                        if p == 33:
                            list_low(ps_ * 9 + e + 1)
                        if p == 40:
                            y_low(ys + 2, 0)
                        if p == 43:
                            add(adds + 2, 0)
                y_low(ps_ * 17 + 17, 1)
                add(ps_ * 34 + 32, 1)


def finish(k):
    nc = k.nc
    r = residual_sems(k, "out_res", None, None)
    stored = k.sem("stored")
    with nc.Block() as block:

        @block.gpsimd
        def _(pool):
            for i in range(2):
                pool.tensor_copy(k.tok[:, 2 + i, :], k.acc[:, i, :]).then_inc(r.copied_a, 1)

        @block.scalar
        def _(act):
            act.wait_ge(r.copied_a, 2)
            residual_scalar(k, act, r, (2, 3), False)

        @block.vector
        def _(dve):
            dve.wait_ge(r.copied_a, 2)
            residual_vector(k, dve, r, (2, 3), 1, False)

        @block.sync
        def _(sp):
            for i in range(2):
                sp.wait_ge(r.added, i + 1)
                sp.dma_start(k.out[0, i * P:(i + 1) * P, :], k.resid[:, 2 + i, :]).then_inc(stored, 16)
            sp.wait_ge(stored, 32)



def hybrid_mlstm_hgrn2_moe(nc, a, out, stages=99):
    with ExitStack() as stack:
        def sb(name, shape, dtype=F32):
            return stack.enter_context(nc.sbuf_tensor(name, shape, dtype))

        stage_sems = []

        def sem(name):
            stage_sems.append(nc.alloc_semaphore(name))
            return stage_sems[-1]

        k = Names()
        k.nc, k.a, k.out, k.sem = nc, a, out, sem
        resid_at = -(-nc.sbuf_base // 64) * 64
        nc.bump_sbuf(resid_at - nc.sbuf_base)
        k.resid = sb("resid", [P, NT, D])
        k.tok = sb("tok", [P, NT, D])
        k.gate = sb("gate", [P, 2, 2, D])
        k.ex = sb("ex", [P, 4096])[:, :]
        k.junk = sb("junk", [P, D])[:, :]
        k.passes = sb("passes", [P, 1], I32)
        k.ones, k.ident, k.before, k.after = (sb(n, [P, P]) for n in ("ones", "ident", "before", "after"))
        k.level_mask = sb("level_mask", [P, LEVELS, P], U8)
        k.gate_sel = sb("gate_sel", [32, 4, 16])
        k.slot_no = sb("slot_no", [P, 256])
        k.expert_no = sb("expert_no", [P, 2, EXPERTS])
        k.crows = k.junk[:, 0:P]
        k.vrows = k.junk[:, P:2 * P]
        k.vcol = sb("vcol", [P, 120])
        k.c_cols = sb("c_cols", [P, KD, 2])
        k.lb_raw, k.lb_exp, k.lb_col, k.lb_rest = (sb(n, [P, 16]) for n in ("lb_raw", "lb_exp", "lb_col", "lb_rest"))
        k.gate_bias = sb("gate_bias", [16, 2])
        k.w_router = sb("w_router", [P, KD, EXPERTS])
        k.b_router = sb("b_router", [1, EXPERTS])
        k.mod_cols = sb("mod_cols", [P, N_MOD, KD, 2])
        k.mod_scale = sb("mod_scale", [P, 2, KD, 2])
        k.ssq, k.rms, k.rstd = (sb(n, [P, NT]) for n in ("ssq", "rms", "rstd"))
        k.eps = sb("eps", [P, 1])
        k.a_cols = sb("a_cols", [P, NT, 16])
        k.e_cols = sb("e_cols", [P, NT, 16])
        k.den = sb("den", [P, 2, NT])
        k.head_sum = sb("head_sum", [P, NT * HEADS])
        base = -(-nc.sbuf_base // 64) * 64

        def at(name, words, first, dtype=F32):
            return nc.alloc_sbuf_tensor_at(name, [P, words], dtype, offset=base + 4 * first)[:, :]

        chunked = lambda area: area.rearrange("p (c t) -> p c t", c=KD)
        k.u_area = at("u_area", KD * T, 0)
        k.u_cols = k.u_area.rearrange("p (c t) -> p c t", c=KD)
        k.u_high, k.u_low = chunked(at("u_high", KD * T, 0, F32R)), chunked(at("u_low", KD * T, KD * T, F32R))
        k.ring = at("ring", RING * SLOT, 2 * KD * T)
        big_words = 2 * KD * T + NT * HEADS * VST
        big_at = 2 * KD * T + RING * SLOT
        k.big = at("big", big_words, big_at)
        k.u_raw = chunked(k.big[:, KD * T:2 * KD * T])
        parts = W_BUFS * W_PIECE
        k.fh_high, k.fh_low = (at(n, F_GROUP * T, big_at + m * F_GROUP * T, F32R).rearrange("p (f t) -> p f t", f=F_GROUP)
                               for m, n in enumerate(("fh_high", "fh_low")))
        k.fw_high = at("fw_high", parts, big_at + 2 * F_GROUP * T, F32R)
        k.fw_low = at("fw_low", parts, big_at + 2 * F_GROUP * T + parts, F32R)
        k.qk = k.big[:, 0:KD * T].rearrange("p (c t) -> p c t", c=KD)
        k.o_cols = k.big[:, KD * T:2 * KD * T].rearrange("p (c t) -> p c t", c=KD)
        k.vaug = k.big[:, 2 * KD * T:big_words].rearrange("p (i h c) -> p i h c", i=NT, h=HEADS)
        k.sq = k.big[:, 2 * KD * T:2 * KD * T + NT * D].rearrange("p (i n) -> p i n", i=NT)
        k.f_rows = k.big[:, 0:4 * D].rearrange("p (i n) -> p i n", i=2)
        k.k_rows = k.big[:, 4 * D:8 * D].rearrange("p (i n) -> p i n", i=2)
        k.v_rows = k.big[:, 8 * D:12 * D].rearrange("p (i n) -> p i n", i=NT)
        k.f_cols = k.ex.rearrange("p (d c t) -> p d c t", d=2, c=KD)
        k.q_cols = k.tok[:, 0:2, :].rearrange("p a (c t) -> p (a c) t", t=LAT)
        k.g_cols = lambda c: k.gate[:, c // 4, 0, (c % 4) * LAT:(c % 4 + 1) * LAT]
        k.state = k.resid[:, 0:2, :].rearrange("p a (h c) -> p (a h) c", c=DV)
        k.q_fac = k.big[:, 0:4 * D].rearrange("p (d c t) -> p d c t", d=2, c=KD)
        k.k_fac = k.u_area.rearrange("p (d c t) -> p d c t", d=2, c=KD)
        k.k_sum = k.tok[:, 2:4, :].rearrange("p a (c t) -> p (a c) t", t=LAT)
        k.pair_near = k.big[:, 4 * D:6 * D].rearrange("p (g i h t) -> p g i h t", g=2, i=2, h=4)
        k.pair_cross = k.big[:, 6 * D:8 * D].rearrange("p (g i h t) -> p g i h t", g=2, i=2, h=4)
        k.acc = k.tok[:, 0:2, :]
        k.e_silu = k.resid[:, 1, 0:2 * E_N].rearrange("p (b n) -> p b n", b=2)
        k.list_raw = k.ex[:, 2048:2048 + KD * P].rearrange("p (c t) -> p c t", c=KD)
        k.places = k.ex[:, 0:256].rearrange("p (i n) -> p i n", i=2)
        k.list_weight = k.ex[:, 512:513]
        k.route = k.ex[:, 1024:1024 + 16 * 16].rearrange("p (f i e) -> p f i e", f=16, i=2)
        k.comb = k.ex[:, 1536:1552].rearrange("p (i e) -> p i e", i=2)
        k.place = k.ex[:, 1552:1570].rearrange("p (i e) -> p i e", i=2)
        scan = k.tok[:, :, :].rearrange("p a n -> p (a n)")
        k.zeros, k.gates_f, k.gates_b = (scan[:, n * HALF:(n + 1) * HALF] for n in range(3))
        (k.scan_t, k.scan_z, k.scan_a, k.scan_a_rev, k.scan_e, k.scan_e_rev, k.scan_m,
         k.scan_m_rev) = (k.ex[:, n * HALF:(n + 1) * HALF] for n in range(8))
        k.ps = stack.enter_context(nc.psum_tensor("ps", [P, 8, HALF], F32))
        k.x_in = stack.enter_context(nc.semaphore("x_in"))
        k.stream = WeightStream(k.ring, k.ex[:, 4 * HALF:8 * HALF], [stack.enter_context(nc.semaphore(f"loaded{i}")) for i in range(RING)])
        plan_stream(k)

        area = {}

        def place_experts():
            first = 0
            for name, words, dtype in (("e_ring", E_RING * E_SLOT, F32), ("e_hid", FFN, F32),
                                       ("w_high", E_BUFS * E_PIECE, F32R), ("w_low", E_BUFS * E_PIECE, F32R),
                                       ("list_h", KD * P, F32R), ("list_l", KD * P, F32R),
                                       ("hid_h", FC * P, F32R), ("hid_l", FC * P, F32R),
                                       ("ey_high", D, F32R), ("ey_low", D, F32R)):
                area[name] = at(name, words, first, dtype)
                first += words
            k.ey_high, k.ey_low = area["ey_high"], area["ey_low"]
            k.place_cols = nc.alloc_sbuf_tensor_at("place_cols", [P, 2 * P], F32R, offset=resid_at)[:, :]
            k.e_ring, k.e_hid, k.w_high, k.w_low = (area[n] for n in ("e_ring", "e_hid", "w_high", "w_low"))
            k.list_h, k.list_l, k.hid_h, k.hid_l = (area[n].rearrange("p (c t) -> p c t", t=P) for n in ("list_h", "list_l", "hid_h", "hid_l"))

        order = [
            lambda: setup(k),
            lambda: modulation(k, 0),
            lambda: norm_in(k, "n0", 0, range(NT), arrived=(k.x_in, 32)),
            lambda: mlstm_in(k),
            lambda: mlstm_heads(k),
            lambda: mixer_out(k, "mo", "m_out", range(NT), 88, lambda h: k.o_cols[:, h, :], False),
            lambda: norm_in(k, "n1", 1, range(NT), u_cols=k.u_raw),
            lambda: feed_forward(k),
            lambda: modulation(k, 1),
            lambda: norm_in(k, "n2", 0, range(NT), True),
            lambda: hgrn_in(k),
            lambda: hgrn_state(k),
            lambda: hgrn_pairs(k),
            lambda: hgrn_values(k),
            lambda: mixer_out(k, "ho", "h_out", (2, 3), 96, k.g_cols, True),
            lambda: norm_in(k, "n3", 1, (2, 3)),
            lambda: routing(k),
            lambda: (place_experts(), experts(k)),
            lambda: finish(k),
        ]
        for n, stage in enumerate(order[:stages]):
            stage()
            if n == len(order) // 2:
                nc.clear_and_free_semaphores(list(stage_sems))
                stage_sems.clear()
                k.stream.release = {}
                nc.all_engine_barrier()


_INS = ['x', 'c', 'ctx', 'c_ctx', 'mod_w', 'mod_b', 'norm_g', 'm_w_in', 'm_b_gate', 'm_w_conv', 'm_g_head', 'm_w_out',
        'h_w_in', 'h_b_f', 'h_lb_raw', 'h_g_head', 'h_w_out', 'f_w_gu', 'f_w_down',
        'e_w_router', 'e_b_router', 'e_w_gu', 'e_w_down']


def kernel(**inputs):
    import numpy as _np
    import concourse.bacc as _bacc
    from concourse.bass_utils import run_bass_kernel_spmd as _run

    nc = _bacc.Bacc("TRN2", target_bir_lowering=False, num_devices=1)
    arrays, args = {}, {}
    for name in _INS:
        array = _np.ascontiguousarray(inputs[name])
        arrays[f"in_{name}_dram"] = array
        args[name] = nc.dram_tensor(f"in_{name}_dram", array.shape, mybir.dt.from_np(array.dtype), kind="ExternalInput").ap()
    out = nc.dram_tensor("out_0_dram", inputs["x"].shape, F32, kind="ExternalOutput").ap()
    hybrid_mlstm_hgrn2_moe(nc, args, out)
    r = _run(nc, [arrays], core_ids=[0])
    return r.results[0]["out_0_dram"]
```

```python
from contextlib import ExitStack

import concourse.bass as bass
from concourse import mybir
from concourse.alu_op_type import AluOpType as ALU

F32 = mybir.dt.float32
F32R = mybir.dt.float32r
I32 = mybir.dt.int32
U8 = mybir.dt.uint8
ACT = mybir.ActivationFunctionType
AX = mybir.AxisListType

P = 128
D = 1024
KD = D // P
CTX, LAT = 256, 256
T = CTX + LAT
NT = T // P
HALF = 512
EPS = 1e-6
N_MOD = 6
HEADS = 8
DV = 128
M_DK = 64
M_QK = 2 * HEADS * M_DK
M_V = HEADS * DV
VST = DV + 2
FFN = 2816
FC = FFN // P
F_GROUP = 8
W_BUFS = 2
W_PIECE = KD * P
GRID_W = 64
GRID_H = LAT // GRID_W
EXPERTS = 8
SHIFT = 0.125

RING = 3
SLOT = KD * HALF
E_RING = 4
E_N = 352
E_TILES = FFN // E_N
E_SLOT = 6 * HALF
E_UNITS = 2 * E_TILES + 2 * 4
E_BUFS = 3
E_PIECE = 3 * HALF
LEVELS = 7


class Names:
    pass


class Chain:

    def __init__(self, engine, sem):
        self.engine, self.sem, self.n = engine, sem, 0

    def link(self, instruction):
        instruction.then_inc(self.sem, 1)
        self.n += 1
        self.engine.wait_ge(self.sem, self.n)


class WeightStream:

    def __init__(self, ring, rows, loaded):
        self.ring, self.rows, self.loaded = ring, rows, loaded
        self.parts, self.value, self.sent = [], [], 0
        self.count = [0] * RING
        self.release = {}

    def slot(self, n):
        s = n % RING
        return self.ring[:, s * SLOT:(s + 1) * SLOT]

    def aux(self, n, partition):
        s = n % (RING + 1)
        return self.rows[partition:partition + 1, s * HALF:(s + 1) * HALF]

    def add(self, *parts):
        n = len(self.parts)
        self.parts.append(parts)
        self.count[n % RING] += 16 * len(parts)
        self.value.append(self.count[n % RING])

    def send(self, sp, end):
        for n in range(self.sent, min(end, len(self.parts))):
            if n - RING in self.release:
                sp.wait_ge(*self.release[n - RING])
            for place, source in self.parts[n]:
                sp.dma_start(self.aux(n, place) if isinstance(place, int) else place(self.slot(n)), source).then_inc(self.loaded[n % RING], 16)
        self.sent = max(self.sent, min(end, len(self.parts)))

    def arrived(self, engine, n):
        engine.wait_ge(self.loaded[n % RING], self.value[n])


def rows_of(width):
    return lambda slot: slot[:, 0:KD * width].rearrange("p (k n) -> p k n", k=KD)


def columns(w, first, width):
    return w[:, first:first + width].rearrange("(k p) n -> p k n", p=P)


def row(v, first):
    return v[first:first + HALF].rearrange("(o n) -> o n", o=1)


def plan_stream(k):
    a, s = k.a, k.stream
    wide = rows_of(HALF)
    plan = {}

    def start(name):
        plan[name] = len(s.parts)

    def add_mod(layer):
        start(f"mod{layer}")
        for n in range(2 * N_MOD):
            parts = [(wide, columns(a["mod_w"][layer], n * HALF, HALF)),
                     (0, row(a["mod_b"][layer], n * HALF))]
            if n // 2 in (2, 5):
                gain = a["norm_g"][layer, 1 if n // 2 == 2 else 3]
                parts.append((32, row(gain, (n % 2) * HALF)))
            s.add(*parts)

    add_mod(0)
    w = a["m_w_in"][0]
    start("m_in")
    s.add((rows_of(4 * HEADS), columns(w, M_QK + 2 * M_V, 4 * HEADS)))
    for n in range(0, M_QK + 2 * M_V, HALF):
        s.add((wide, columns(w, n, HALF)))
    start("m_out")
    for n in range(0, D, HALF):
        s.add((wide, columns(a["m_w_out"][0], n, HALF)))
    w = a["f_w_gu"][0]
    start("f_up")
    w_down = a["f_w_down"][0].rearrange("(f p) n -> p f n", p=P)

    def place(side):
        return lambda slot: slot[:, 0:SLOT].rearrange("p (k s n) -> p k s n", k=KD, s=2)[:, :, side, :]

    for first in range(0, FC, F_GROUP):
        end = min(first + F_GROUP, FC)
        for f in range(first, end, 2):
            s.add((place(0), columns(w, f * P, 2 * P)), (place(1), columns(w, FFN + f * P, 2 * P)))
        for f in range(first, end, 4):
            m = min(4, end - f)
            s.add((lambda slot, m=m: slot[:, 0:m * D].rearrange("p (f n) -> p f n", f=m), w_down[:, f:f + m, :]))
    add_mod(1)
    w = a["h_w_in"][0]
    start("h_in")
    for direction in range(2):
        for half in range(2):
            s.add((wide, columns(w, (2 + direction) * D + half * HALF, HALF)))
    for first in (D, 0, 4 * D):
        for half in range(2):
            s.add((wide, columns(w, first + half * HALF, HALF)))
    start("h_out")
    for n in range(0, D, HALF):
        s.add((wide, columns(a["h_w_out"][0], n, HALF)))
    k.plan = plan



def setup(k):
    nc, a = k.nc, k.a
    rows_in, made, same_made = k.sem("rows_in"), k.sem("ones_made"), k.sem("same_made")
    small_in, silu_done, turned = k.sem("small_in"), k.sem("silu_done"), k.sem("rows_turned")
    own, iota_made = k.sem("setup_chain"), k.sem("iota_made")
    same = k.ex[:, 0:1024].rearrange("p (l n) -> p l n", l=8)
    iota_i = k.ex[:, 1024:1024 + 272].bitcast(I32)

    with nc.Block() as block:

        @block.sync
        def _(sp):
            sp.dma_start(k.crows[0:8, :], a["c_ctx"].rearrange("(k p) -> k p", p=P)).then_inc(rows_in, 16)
            sp.dma_start(k.crows[8:16, :], a["c"][0].rearrange("(k p) -> k p", p=P)).then_inc(rows_in, 16)
            sp.dma_start(k.crows[16:32, :], a["h_lb_raw"][0].rearrange("a (k p) -> (a k) p", p=P)).then_inc(rows_in, 16)
            sp.dma_start(k.vrows[0:64, :], a["norm_g"].rearrange("l n (k p) -> (l n k) p", p=P)).then_inc(rows_in, 16)
            sp.dma_start(k.vrows[64:88, :], a["m_w_conv"][0].rearrange("t (k p) -> (t k) p", p=P)).then_inc(rows_in, 16)
            sp.dma_start(k.vrows[88:96, :], a["m_g_head"][0].rearrange("(k p) -> k p", p=P)).then_inc(rows_in, 16)
            sp.dma_start(k.vrows[96:104, :], a["h_g_head"][0].rearrange("(k p) -> k p", p=P)).then_inc(rows_in, 16)
            sp.dma_start(k.vrows[104:120, :], a["h_b_f"][0].rearrange("a (k p) -> (a k) p", p=P)).then_inc(rows_in, 16)
            for g in range(4):
                sp.dma_start(k.gate_bias[(g // 2) * 8:(g // 2) * 8 + 8, g % 2:g % 2 + 1],
                             a["m_b_gate"][0, g].rearrange("(h o) -> h o", o=1)).then_inc(small_in, 16)
            sp.dma_start(k.w_router[:, :, :], a["e_w_router"][0].rearrange("(k p) e -> p k e", p=P)).then_inc(small_in, 16)
            sp.dma_start(k.b_router[0:1, :], a["e_b_router"][0:1, :]).then_inc(small_in, 16)
            k.stream.send(sp, RING)
            sp.dma_start(k.resid[:, 0:2, :], a["ctx"][0].rearrange("(t p) d -> p t d", p=P)).then_inc(k.x_in, 16)
            sp.dma_start(k.resid[:, 2:4, :], a["x"][0].rearrange("(t p) d -> p t d", p=P)).then_inc(k.x_in, 16)
            sp.wait_ge(small_in, 96)

        @block.gpsimd
        def _(pool):
            pool.memset(k.ones[:, :], 1.0).then_inc(made, 1)
            pool.wait_ge(made, 1)
            pool.affine_select(out=k.ident[:, :], in_=k.ones[:, :], compare_op=ALU.is_equal, fill=0.0, base=0,
                               pattern=[[-1, P]], channel_multiplier=1).then_inc(made, 1)
            pool.affine_select(out=k.before[:, :], in_=k.ones[:, :], compare_op=ALU.is_gt, fill=0.0, base=0,
                               pattern=[[1, P]], channel_multiplier=-1).then_inc(made, 1)
            pool.affine_select(out=k.after[:, :], in_=k.ones[:, :], compare_op=ALU.is_gt, fill=0.0, base=0,
                               pattern=[[-1, P]], channel_multiplier=1).then_inc(made, 1)
            pool.iota(iota_i[:, 0:256], pattern=[[1, 256]], base=0, channel_multiplier=0).then_inc(iota_made, 1)
            pool.iota(iota_i[:, 256:272], pattern=[[0, 2], [1, 8]], base=8, channel_multiplier=0).then_inc(iota_made, 1)
            for i in range(8):
                size, n = 2 ** i, P // 2 ** i
                view = same[:, i, :].rearrange("p (b l) -> p b l", l=size)
                pool.affine_select(out=view, in_=k.ones[:, :].rearrange("p (b l) -> p b l", l=size),
                                   compare_op=ALU.is_ge, fill=0.0, base=0, pattern=[[-size, n], [0, size]],
                                   channel_multiplier=1).then_inc(same_made, 1)
                pool.wait_ge(same_made, 2 * i + 1)
                pool.affine_select(out=view, in_=view, compare_op=ALU.is_ge, fill=0.0, base=size - 1,
                                   pattern=[[size, n], [0, size]], channel_multiplier=-1).then_inc(same_made, 1)

        @block.scalar
        def _(act):
            act.wait_ge(rows_in, 128)
            nc.scalar.activation(k.crows[0:16, :], k.crows[0:16, :], ACT.Silu).then_inc(silu_done, 1)
            act.wait_ge(own, 2)
            nc.scalar.activation(k.lb_exp[:, :], k.lb_exp[:, :], ACT.Exp).then_inc(silu_done, 1)

        @block.tensor
        def _(pe):
            pe.wait_ge(made, 2)
            pe.wait_ge(rows_in, 128)
            nc.tensor.transpose(k.ps[:, 0, 0:120], k.vrows[0:120, :], k.ident[0:120, 0:120]).then_inc(turned, 1)
            pe.wait_ge(silu_done, 1)
            nc.tensor.transpose(k.ps[:, 1, 0:32], k.crows[0:32, :], k.ident[0:32, 0:32]).then_inc(turned, 1)

        @block.vector
        def _(dve):
            chain = Chain(dve, own)
            dve.wait_ge(turned, 2)
            chain.link(nc.vector.tensor_copy(k.lb_raw[:, :], k.ps[:, 1, 16:32]))
            chain.link(nc.vector.tensor_tensor(k.lb_exp[:, :], k.lb_raw[:, :], k.lb_raw[:, :], ALU.subtract))
            nc.vector.tensor_copy(k.vcol[:, :], k.ps[:, 0, 0:120])
            c_cols = k.ps[:, 1, 0:16].rearrange("p (j k) -> p k j", j=2)
            chain.link(nc.vector.tensor_copy(k.c_parts[:, :, 0:2], c_cols))
            nc.vector.tensor_tensor(k.c_parts[:, :, 2:4], c_cols, k.c_parts[:, :, 0:2].bitcast(F32), ALU.subtract)
            nc.vector.tensor_copy(k.first_rows[0:1, 0:2], k.ones[0:1, 0:2])
            nc.vector.memset(k.first_rows[0:1, 2:4], 0.0)
            nc.vector.tensor_tensor(k.pair_sum[0:4, :], k.ident[0:4, 0:2], k.ident[0:4, 2:4], ALU.add)
            nc.vector.memset(k.eps[:, :], EPS)
            nc.vector.memset(k.gate_sel[:, :, :], 0.0).then_inc(own, 1)
            chain.n += 1
            dve.wait_ge(made, 4)
            dve.wait_ge(own, chain.n)
            for g, (src, dst) in enumerate(((0, 0), (16, 8), (8, 0), (24, 8))):
                nc.vector.tensor_copy(k.gate_sel[0:32, g, dst:dst + 8], k.ident[0:32, src:src + 8])
            dve.wait_ge(iota_made, 2)
            nc.vector.tensor_copy(k.slot_no[:, :], iota_i[:, 0:256])
            nc.vector.tensor_copy(k.expert_no[:, :, :], iota_i[:, 256:272].rearrange("p (i e) -> p i e", i=2))
            dve.wait_ge(same_made, 16)
            nc.vector.tensor_tensor(k.level_mask[:, :, :], same[:, 1:8, :], same[:, 0:7, :], ALU.subtract)
            dve.wait_ge(silu_done, 2)
            chain.link(nc.vector.reciprocal(k.lb_raw[:, :], k.lb_exp[:, :]))
            chain.link(nc.vector.tensor_tensor(k.lb_exp[:, :], k.lb_exp[:, :], k.lb_raw[:, :], ALU.mult))
            chain.link(nc.vector.tensor_tensor(k.lb_col[:, :], k.lb_exp[:, :], k.lb_exp[:, :], ALU.subtract))
            nc.vector.tensor_scalar(k.lb_rest[:, :], k.lb_col[:, :], -1.0, 1.0, ALU.mult, ALU.add)



def modulation(k, layer):
    nc, s, u0 = k.nc, k.stream, k.plan[f"mod{layer}"]

    def sem(name):
        return k.sem(f"mod{layer}_{name}")

    high_done, low_done, used, row_ready, row_copied = (sem(n) for n in ("high_done", "low_done", "used", "row_ready", "row_copied"))
    cols_ready, cols_copied, scaled, spread, gate_copied = (sem(n) for n in ("cols_ready", "cols_copied", "scaled", "spread", "gate_copied"))
    units = 2 * N_MOD
    streams = (0, 1) if layer == 0 else (1,)
    gates = [n for n in range(units) if n // 2 in (2, 5)]
    plain = [n for n in range(units) if n not in gates]
    rows = k.ex[0:4, 0:2 * HALF].rearrange("p (b n) -> p b n", b=2)
    scaled_rows = k.ex[0:4, 2 * HALF:4 * HALF].rearrange("p (b n) -> p b n", b=2)
    QUARTERS = 4
    s.release = {u0 + n: (low_done, QUARTERS * (n + 1)) for n in range(units)}

    def raw(n, q):
        return rows_of(HALF)(s.slot(u0 + n))[:, 2 * q:2 * q + 2, :]

    def part(area, q):
        return area[:, 2 * q:2 * q + 2, :]

    with nc.Block() as block:

        @block.sync
        def _(sp):
            s.send(sp, u0 + units + RING)

        @block.tensor
        def _(pe):
            def finish(n):
                pe.wait_ge(row_copied, n + 1)
                if n in plain:
                    i = plain.index(n)
                    if i >= 2:
                        pe.wait_ge(cols_copied, i - 1)
                    for c in range(4):
                        last = nc.tensor.matmul(k.ps[:, 4 + i % 2, 2 * c:2 * c + 2], rows[0:4, n % 2, c * P:(c + 1) * P],
                                                k.pair_sum[0:4, :], start=True, stop=True)
                    last.then_inc(cols_ready, 1)
                else:
                    g = gates.index(n)
                    pe.wait_ge(scaled, g + 1)
                    if g:
                        pe.wait_ge(gate_copied, g * len(streams))
                    for j in streams:
                        nc.tensor.matmul(k.ps[:, 6 + j, :], k.pair_sum[0:4, j:j + 1].to_broadcast([4, P]), scaled_rows[0:4, g % 2, :],
                                         start=True, stop=True).then_inc(spread, 1)

            for n in range(units):
                s.arrived(pe, u0 + n)
                if n >= 2:
                    pe.wait_ge(row_copied, n - 1)
                if n in gates:
                    if gates.index(n):
                        pe.wait_ge(scaled, gates.index(n))
                    nc.tensor.matmul(k.ps[0:4, 2, :], k.ones[32:33, 0:4], s.aux(u0 + n, 32), start=True, stop=True)
                nc.tensor.matmul(k.ps[0:4, n % 2, :], k.first_rows[0:1, 0:4], s.aux(u0 + n, 0), start=True, stop=False)
                for q in range(QUARTERS):
                    pe.wait_ge(low_done, QUARTERS * n + q + 1)
                    for m in range(2):
                        c = 2 * q + m
                        nc.tensor.matmul(k.ps[0:4, n % 2, :], k.c_parts[:, c, :], part(k.u_high, q)[:, m, :], start=False, stop=False)
                        last = nc.tensor.matmul(k.ps[0:4, n % 2, :], k.c_parts[:, c, :], part(k.u_low, q)[:, m, :],
                                                start=False, stop=(c == KD - 1))
                    last.then_inc(row_ready if q == QUARTERS - 1 else used, 1)
                    if q == 1 and n:
                        finish(n - 1)
            finish(units - 1)

        @block.scalar
        def _(act):
            def copy_row(n):
                act.wait_ge(row_ready, n + 1)
                if n >= 2:
                    if n - 2 in plain:
                        act.wait_ge(cols_ready, plain.index(n - 2) + 1)
                    else:
                        act.wait_ge(scaled, gates.index(n - 2) + 1)
                nc.scalar.activation(rows[0:4, n % 2, :], k.ps[0:4, n % 2, :], ACT.Copy).then_inc(row_copied, 1)

            for n in range(units):
                s.arrived(act, u0 + n)
                for q in range(QUARTERS):
                    if n:
                        if q == QUARTERS - 1:
                            act.wait_ge(row_ready, n)
                        else:
                            act.wait_ge(used, (QUARTERS - 1) * (n - 1) + q + 1)
                    nc.scalar.activation(part(k.u_high, q), raw(n, q), ACT.Copy).then_inc(high_done, 1)
                    if q == 2 and n:
                        copy_row(n - 1)
            copy_row(units - 1)

        @block.vector
        def _(dve):
            def scale_or_take(n):
                if n in plain:
                    i = plain.index(n)
                    dve.wait_ge(cols_ready, i + 1)
                    nc.vector.tensor_copy(k.mod_cols[:, n // 2, 4 * (n % 2):4 * (n % 2) + 4, :],
                                          k.ps[:, 4 + i % 2, 0:8].rearrange("p (c j) -> p c j", j=2)).then_inc(cols_copied, 1)
                    return
                g = gates.index(n)
                dve.wait_ge(row_copied, n + 1)
                if g >= 2:
                    dve.wait_ge(spread, (g - 1) * len(streams))
                nc.vector.tensor_tensor(scaled_rows[0:4, g % 2, :], rows[0:4, n % 2, :], k.ps[0:4, 2, :],
                                        ALU.mult).then_inc(scaled, 1)

            def take_gate(n):
                if n in gates:
                    g = gates.index(n)
                    for i, j in enumerate(streams):
                        dve.wait_ge(spread, g * len(streams) + i + 1)
                        nc.vector.tensor_copy(k.gate[:, g // 2, j, (n % 2) * HALF:(n % 2 + 1) * HALF],
                                              k.ps[:, 6 + j, :]).then_inc(gate_copied, 1)

            for n in range(units):
                for q in range(QUARTERS):
                    dve.wait_ge(high_done, QUARTERS * n + q + 1)
                    nc.vector.tensor_tensor(part(k.u_low, q), raw(n, q), part(k.u_high, q).bitcast(F32), ALU.subtract).then_inc(low_done, 1)
                    if q == 2 and n:
                        scale_or_take(n - 1)
                if n:
                    take_gate(n - 1)
            scale_or_take(units - 1)
            take_gate(units - 1)
            dve.wait_ge(cols_copied, len(plain))
            for w in range(2):
                gain = k.vcol[:, (layer * 4 + 2 * w) * KD:(layer * 4 + 2 * w + 1) * KD]
                nc.vector.scalar_tensor_tensor(out=k.mod_scale[:, w, :, :], in0=k.mod_cols[:, 1 + 3 * w, :, :], scalar=1.0,
                                               in1=gain.unsqueeze(2).to_broadcast([P, KD, 2]), op0=ALU.add, op1=ALU.mult)



def norm_in(k, name, which, tiles, column_major=False, u_cols=None, arrived=None):
    u_cols = k.u_cols if u_cols is None else u_cols
    nc = k.nc
    squared, root, normed = k.sem(name + "_squared"), k.sem(name + "_root"), k.sem(name + "_normed")
    turned, recip = k.sem(name + "_turned"), k.sem(name + "_recip")
    t0, t1 = tiles[0], tiles[-1] + 1
    streams = [j for j in range(2) if 2 * j in tiles]

    def source(c, j):
        return k.ps[:, c, j * 256:(j + 1) * 256]

    def views(c, j):
        src, dst = source(c, j), u_cols[:, c, j * 256:(j + 1) * 256]
        if column_major and j == 1:
            return (src.rearrange("p (r w) -> p r w", r=GRID_H), dst.rearrange("p (w r) -> p r w", r=GRID_H))
        return src, dst

    with nc.Block() as block:

        @block.scalar
        def _(act):
            if arrived:
                act.wait_ge(*arrived)
            for i in tiles:
                nc.scalar.activation(k.tok[:, i, :], k.resid[:, i, :], ACT.Square,
                                     accum_out=k.ssq[:, i:i + 1]).then_inc(squared, 1)
            act.wait_ge(squared, len(tiles))
            nc.scalar.activation(k.rms[:, t0:t1], k.ssq[:, t0:t1], ACT.Sqrt, bias=k.eps[:, 0:1],
                                 scale=1.0 / D).then_inc(root, 1)
            for c in range(1, KD, 2):
                act.wait_ge(turned, c + 1)
                for j in streams:
                    src, dst = views(c, j)
                    nc.scalar.activation(dst, src, ACT.Identity, bias=k.mod_cols[:, 3 * which, c, j:j + 1],
                                         scale=k.mod_scale[:, which, c, j:j + 1])

        @block.vector
        def _(dve):
            dve.wait_ge(root, 1)
            nc.vector.reciprocal(k.rstd[:, t0:t1], k.rms[:, t0:t1]).then_inc(recip, 1)
            dve.wait_ge(recip, 1)
            for i in tiles:
                nc.vector.tensor_scalar(k.tok[:, i, :], k.resid[:, i, :], k.rstd[:, i:i + 1], None,
                                        ALU.mult).then_inc(normed, 1)
            for c in range(0, KD, 2):
                dve.wait_ge(turned, c + 1)
                for j in streams:
                    src, dst = views(c, j)
                    nc.vector.tensor_scalar(dst, src, k.mod_scale[:, which, c, j:j + 1],
                                            k.mod_cols[:, 3 * which, c, j:j + 1], ALU.mult, ALU.add)

        @block.tensor
        def _(pe):
            for n, i in enumerate(tiles):
                pe.wait_ge(normed, n + 1)
                for c in range(KD):
                    last = nc.tensor.transpose(k.ps[:, c, i * P:(i + 1) * P], k.tok[:, i, c * P:(c + 1) * P], k.ident[:, :])
                    if i == tiles[-1]:
                        last.then_inc(turned, 1)



def residual_scalar(k, act, r, tiles, copies, summed=None):
    nc = k.nc
    if copies:
        for n, i in enumerate(tiles):
            act.wait_ge(r.ready, r.ready_value(i, 0))
            nc.scalar.activation(k.tok[:, i, 0:HALF], k.ps[:, r.bank(i, 0), :], ACT.Copy).then_inc(r.copied_a, 1)
    for n, i in enumerate(tiles):
        if copies:
            act.wait_ge(r.copied_a, n + 1)
            act.wait_ge(r.copied_b, n + 1)
        if summed:
            summed(n)
        nc.scalar.activation(k.junk[:, :], k.tok[:, i, :], ACT.Square, accum_out=k.ssq[:, i:i + 1]).then_inc(r.squared, 1)
        act.wait_ge(r.squared, n + 1)
        nc.scalar.activation(k.rms[:, i:i + 1], k.ssq[:, i:i + 1], ACT.Sqrt, bias=k.eps[:, 0:1],
                             scale=1.0 / D).then_inc(r.root, 1)


def residual_vector(k, dve, r, tiles, which, copies):
    nc = k.nc
    if copies:
        for n, i in enumerate(tiles):
            dve.wait_ge(r.ready, r.ready_value(i, 1))
            nc.vector.tensor_copy(k.tok[:, i, HALF:D], k.ps[:, r.bank(i, 1), :]).then_inc(r.copied_b, 1)
    chain = Chain(dve, r.chain)
    for n, i in enumerate(tiles):
        dve.wait_ge(r.root, n + 1)
        chain.link(nc.vector.reciprocal(k.rstd[:, i:i + 1], k.rms[:, i:i + 1]))
        chain.link(nc.vector.scalar_tensor_tensor(out=k.tok[:, i, :], in0=k.tok[:, i, :], scalar=k.rstd[:, i:i + 1],
                                                  in1=k.gate[:, which, i // 2, :], op0=ALU.mult, op1=ALU.mult))
        nc.vector.tensor_tensor(k.resid[:, i, :], k.resid[:, i, :], k.tok[:, i, :], ALU.add).then_inc(r.added, 1)


def residual_sems(k, name, bank, ready_value):
    r = Names()
    r.bank, r.ready_value = bank, ready_value
    r.ready, r.copied_a, r.copied_b = k.sem(name + "_ready"), k.sem(name + "_copied_a"), k.sem(name + "_copied_b")
    r.squared, r.root, r.chain, r.added = (k.sem(f"{name}_{n}") for n in ("squared", "root", "chain", "added"))
    return r



class Pieces:

    def __init__(self, k, name, u0, kinds, jobs, ready, high, low):
        self.nc, self.s, self.u0, self.kinds, self.jobs, self.ready = k.nc, k.stream, u0, kinds, jobs, ready
        self.high, self.low = high, low
        self.high_done, self.low_done, self.rows_used = (k.sem(f"{name}_{n}") for n in ("high_done", "low_done", "rows_used"))
        self.u_high_done, self.u_low_done = k.sem(name + "_u_high_done"), k.sem(name + "_u_low_done")
        self.k = k
        self.count = 4 * len(kinds)
        self.s.release = {u0 + u: (self.low_done, 4 * (u + 1)) for u in range(len(kinds))}

    def by_rows(self, p):
        return self.kinds[p // 4] == "rows"

    def raw(self, p):
        w = rows_of(HALF)(self.s.slot(self.u0 + p // 4))
        q = p % 4
        return w[:, 2 * q:2 * q + 2, :] if self.by_rows(p) else w[:, :, q * P:(q + 1) * P]

    def view(self, buffer, p):
        return buffer.rearrange("p (k n) -> p k n", k=2 if self.by_rows(p) else KD)

    def parts(self, p):
        return self.view(self.high[p % 2], p), self.view(self.low[p % 2], p)

    def done(self, p):
        if self.by_rows(p) and p % 4 < 3:
            return self.rows_used, sum(self.by_rows(i) and i % 4 < 3 for i in range(p + 1))
        return self.ready, (self.jobs[p // 4][-1] if self.by_rows(p) else self.jobs[p // 4][p % 4]) + 1

    def split_high(self, act, p):
        if p >= self.count:
            return
        if p % 4 == 0:
            self.s.arrived(act, self.u0 + p // 4)
        if p >= 2:
            act.wait_ge(*self.done(p - 2))
        self.nc.scalar.activation(self.view(self.high[p % 2], p), self.raw(p), ACT.Copy).then_inc(self.high_done, 1)

    def split_low(self, dve, p):
        if p >= self.count:
            return
        dve.wait_ge(self.high_done, p + 1)
        self.nc.vector.tensor_tensor(self.view(self.low[p % 2], p), self.raw(p), self.view(self.high[p % 2], p).bitcast(F32),
                                     ALU.subtract).then_inc(self.low_done, 1)

    def split_u_high(self, act):
        for c in range(KD):
            self.nc.scalar.activation(self.k.u_high[:, c, :], self.k.u_raw[:, c, :], ACT.Copy).then_inc(self.u_high_done, 1)
            if c in (1, 3):
                self.split_high(act, c // 2)

    def split_u_low(self, dve):
        for c in range(KD):
            dve.wait_ge(self.u_high_done, c + 1)
            self.nc.vector.tensor_tensor(self.k.u_low[:, c, :], self.k.u_raw[:, c, :], self.k.u_high[:, c, :].bitcast(F32),
                                         ALU.subtract).then_inc(self.u_low_done, 1)
            if c in (1, 3):
                self.split_low(dve, c // 2)



def mlstm_in(k):
    nc, s, u0 = k.nc, k.stream, k.plan["m_in"]
    gates_ready, gates_copied, picked = k.sem("m_gates_ready"), k.sem("m_gates_copied"), k.sem("m_picked")
    job_ready, conv_done, job_copied = k.sem("m_job_ready"), k.sem("m_conv_done"), k.sem("m_job_copied")
    own, act_own, scan_ready, cols_ready = k.sem("m_chain"), k.sem("m_act_own"), k.sem("m_scan_ready"), k.sem("m_cols_ready")
    conv_own, scan_input, exp_ready = k.sem("m_conv_own"), k.sem("m_scan_input"), k.sem("m_exp_ready")
    units = 7
    jobs = [list(range(4 * u, 4 * u + 4)) for u in range(6)]
    w = Pieces(k, "m", u0 + 1, ["columns"] * 2 + ["rows"] * 2 + ["columns"] * 2, jobs, job_ready, k.m_high, k.m_low)
    s.release[u0] = (gates_ready, 1)
    pre = k.junk

    with nc.Block() as block:

        @block.sync
        def _(sp):
            s.send(sp, u0 + units + RING)

        @block.tensor
        def _(pe):
            s.arrived(pe, u0)
            w_gate = rows_of(4 * HEADS)(s.slot(u0))
            for c in range(KD):
                last = nc.tensor.matmul(k.ps[0:32, 0, :], w_gate[:, c, :], k.u_raw[:, c, :], start=(c == 0), stop=(c == KD - 1))
            last.then_inc(gates_ready, 1)

            def bank_free(r):
                if r >= 12:
                    pe.wait_ge(job_copied, r - 3)
                elif r >= 4:
                    pe.wait_ge(conv_done, r - 3)

            def columns_piece(r):
                bank_free(r)
                pe.wait_ge(w.low_done, r + 1)
                wh, wl = w.parts(r)
                for c in range(KD):
                    if r == 0:
                        pe.wait_ge(w.u_low_done, c + 1)
                    out = k.ps[:, 1 + r % 4, :]
                    nc.tensor.matmul(out, wh[:, c, :], k.u_high[:, c, :], start=(c == 0), stop=False)
                    nc.tensor.matmul(out, wh[:, c, :], k.u_low[:, c, :], start=False, stop=False)
                    last = nc.tensor.matmul(out, wl[:, c, :], k.u_high[:, c, :], start=False, stop=(c == KD - 1))
                last.then_inc(job_ready, 1)

            def rows_piece(p):
                q, first = p % 4, p - p % 4
                pe.wait_ge(w.low_done, p + 1)
                wh, wl = w.parts(p)
                for i in range(NT):
                    if q == 0:
                        bank_free(first + i)
                    for m in range(2):
                        c = 2 * q + m
                        uh, ul = (u[:, c, i * P:(i + 1) * P] for u in (k.u_high, k.u_low))
                        out = k.ps[:, 1 + i, :]
                        nc.tensor.matmul(out, uh, wh[:, m, :], start=(c == 0), stop=False)
                        nc.tensor.matmul(out, uh, wl[:, m, :], start=False, stop=False)
                        last = nc.tensor.matmul(out, ul, wh[:, m, :], start=False, stop=(c == KD - 1))
                    if q == 3:
                        last.then_inc(job_ready, 1)
                if q < 3:
                    last.then_inc(w.rows_used, 1)

            for r in range(24):
                (rows_piece if w.by_rows(r) else columns_piece)(r)
                if r == 0:
                    pe.wait_ge(gates_copied, 2)
                    for g in range(2):
                        nc.tensor.matmul(k.ps[0:16, 6 + g, :], k.gate_sel[0:32, 2 * g, :], k.gates_f[0:32, :],
                                         start=True, stop=False)
                        last = nc.tensor.matmul(k.ps[0:16, 6 + g, :], k.gate_sel[0:32, 2 * g + 1, :], k.gates_b[0:32, :],
                                                start=False, stop=True)
                    last.then_inc(picked, 1)
                if r == 20:
                    pe.wait_ge(scan_ready, 1)
                    for q, src in enumerate((k.scan_a, k.scan_a_rev, k.scan_e, k.scan_e_rev)):
                        for i in range(NT):
                            n = (q * NT + i) * 16
                            last = nc.tensor.transpose(k.ps[:, 0, n:n + 16], src[0:16, i * P:(i + 1) * P], k.ident[0:16, 0:16])
                    last.then_inc(cols_ready, 1)

        @block.scalar
        def _(act):
            def gates():
                act.wait_ge(picked, 1)
                nc.scalar.activation(k.scan_t[0:16, :], k.ps[0:16, 7, :], ACT.Abs, bias=k.gate_bias[0:16, 1:2]).then_inc(act_own, 1)
                act.wait_ge(act_own, 1)
                nc.scalar.activation(k.scan_t[0:16, :], k.scan_t[0:16, :], ACT.Exp, scale=-1.0).then_inc(act_own, 1)
                act.wait_ge(act_own, 2)
                nc.scalar.activation(k.scan_t[0:16, :], k.scan_t[0:16, :], ACT.Ln, bias=1.0).then_inc(scan_input, 1)

            def copy(r):
                if r < 8:
                    act.wait_ge(conv_done, r + 1)
                    nc.scalar.activation(k.qk[:, r, :], pre[:, (r % 2) * HALF:(r % 2 + 1) * HALF], ACT.Silu).then_inc(job_copied, 1)
                elif r < 16:
                    i, half = r % 4, (r - 8) // 4
                    act.wait_ge(job_ready, r + 1)
                    nc.scalar.activation(k.vaug[:, i, 4 * half:4 * half + 4, 0:DV],
                                         k.ps[:, 1 + r % 4, :].rearrange("p (h d) -> p h d", h=4), ACT.Copy).then_inc(job_copied, 1)
                else:
                    act.wait_ge(job_ready, r + 1)
                    nc.scalar.activation(k.o_cols[:, r - 16, :], k.ps[:, 1 + r % 4, :], ACT.Sigmoid).then_inc(job_copied, 1)

            w.split_u_high(act)
            for r in range(24):
                if not (8 <= r < 16):
                    w.split_high(act, r + 2)
                    copy(r)
                elif r % 4 < 3:
                    w.split_high(act, r + 2)
                else:
                    for n in range(r - 3, r + 1):
                        copy(n)
                    w.split_high(act, r + 2)
                if r == 1:
                    gates()
                if r == 15:
                    act.wait_ge(exp_ready, 1)
                    nc.scalar.activation(k.scan_e[0:16, :], k.scan_e[0:16, :], ACT.Exp, scale=-1.0).then_inc(act_own, 1)

        @block.vector
        def _(dve):
            chain = Chain(dve, own)
            w.split_u_low(dve)
            nc.vector.memset(k.vaug[:, :, :, DV:DV + 1], 1.0)
            chain.link(nc.vector.memset(k.zeros[0:16, :], 0.0))
            dve.wait_ge(gates_ready, 1)
            g = k.ps[0:32, 0, :].rearrange("p (s t) -> p s t", s=2)
            nc.vector.tensor_copy(k.gates_f[0:32, :], k.ps[0:32, 0, :]).then_inc(gates_copied, 1)
            nc.vector.tensor_copy(k.gates_b[0:32, :].rearrange("p (s t) -> p s t", s=2), g[:, :, ::-1]).then_inc(gates_copied, 1)

            def scan():
                z, i_sum, t = k.scan_z[0:16, :], k.scan_a[0:16, :], k.scan_t[0:16, :]
                dve.wait_ge(picked, 1)
                dve.wait_ge(scan_input, 1)
                chain.link(nc.vector.tensor_scalar(z, k.ps[0:16, 7, :], k.gate_bias[0:16, 1:2], None, ALU.add))
                chain.link(nc.vector.scalar_tensor_tensor(out=t, in0=z, scalar=0.0, in1=t, op0=ALU.min, op1=ALU.subtract))
                chain.link(nc.vector.tensor_tensor_scan(z, t, k.zeros[0:16, :], 0.0, ALU.add, ALU.add))
                chain.link(nc.vector.scalar_tensor_tensor(out=i_sum, in0=k.ps[0:16, 6, :], scalar=k.gate_bias[0:16, 0:1],
                                                          in1=z, op0=ALU.add, op1=ALU.subtract))
                chain.link(nc.vector.tensor_tensor_scan(k.scan_m[0:16, :], i_sum, i_sum, 0.0, ALU.max, ALU.max))
                nc.vector.tensor_tensor(k.scan_e[0:16, :], k.scan_m[0:16, :], z, ALU.add).then_inc(exp_ready, 1)

            for r in range(8):
                dve.wait_ge(job_ready, r + 1)
                w.split_low(dve, r + 2)
                if r >= 2:
                    dve.wait_ge(job_copied, r - 1)
                x = k.ps[:, 1 + r % 4, :].rearrange("p (s t) -> p s t", s=2)
                y = pre[:, (r % 2) * HALF:(r % 2 + 1) * HALF].rearrange("p (s t) -> p s t", s=2)
                tap = [k.vcol[:, 64 + t * KD + r:65 + t * KD + r] for t in range(3)]
                nc.vector.tensor_scalar(y, x, tap[1], None, ALU.mult).then_inc(conv_own, 1)
                dve.wait_ge(conv_own, 2 * r + 1)
                nc.vector.scalar_tensor_tensor(out=y[:, :, 1:], in0=x[:, :, 0:255], scalar=tap[0], in1=y[:, :, 1:],
                                               op0=ALU.mult, op1=ALU.add).then_inc(conv_own, 1)
                dve.wait_ge(conv_own, 2 * r + 2)
                nc.vector.scalar_tensor_tensor(out=y[:, :, 0:255], in0=x[:, :, 1:], scalar=tap[2], in1=y[:, :, 0:255],
                                               op0=ALU.mult, op1=ALU.add).then_inc(conv_done, 1)
                if r == 3:
                    scan()
            for r in range(8, 18):
                w.split_low(dve, r + 2)
            dve.wait_ge(act_own, 3)
            for dst, src in ((k.scan_a_rev, k.scan_a), (k.scan_m_rev, k.scan_m), (k.scan_e_rev, k.scan_e)):
                last = nc.vector.tensor_copy(dst[0:16, :].rearrange("p (s t) -> p s t", s=2),
                                             src[0:16, :].rearrange("p (s t) -> p s t", s=2)[:, :, ::-1])
            last.then_inc(scan_ready, 1)
            for r in range(18, 24):
                w.split_low(dve, r + 2)
            dve.wait_ge(cols_ready, 1)
            c = k.ps[:, 0, 0:256].rearrange("p (q r i h) -> p q r i h", q=2, r=2, h=16)
            for d in range(2):
                nc.vector.tensor_copy(k.a_cols[:, :, 8 * d:8 * d + 8], c[:, 0, d, :, 8 * d:8 * d + 8])
                nc.vector.tensor_copy(k.e_cols[:, :, 8 * d:8 * d + 8], c[:, 1, d, :, 8 * d:8 * d + 8])



SEEN = {0: [(0, 4), (1, 4), (2, 4), (3, 4)], 1: [(0, 4), (0, 4), (2, 3), (2, 4)]}
SOURCES = {0: [[0], [0, 1], [0, 1, 2], [0, 1, 2, 3]], 1: [[0, 1], [1], [0, 1, 2, 3], [0, 1, 3]]}


def mlstm_heads(k):
    nc = k.nc
    scored, spread, weighed, probs = k.sem("a_scored"), k.sem("a_spread"), k.sem("a_weighed"), k.sem("a_probs")
    masked, summed, own, added = k.sem("a_masked"), k.sem("a_summed"), k.sem("a_chain"), k.sem("a_added")
    turn_done, squares = k.sem("a_turn_done"), k.sem("a_squares")
    prob = k.u_area.rearrange("p (b s t) -> p b s t", b=2, s=NT)
    decay = k.ex[:, 0:4 * HALF].rearrange("p (s t) -> p s t", s=NT)
    part = k.ex[:, 4 * HALF:6 * HALF].rearrange("p (b t) -> p b t", b=2)
    turns = 2 * HEADS

    def score_cols(j):
        return (j, 0) if j < 2 else (2, (j - 2) * 256 - 256)

    with nc.Block() as block:

        @block.sync
        def _(sp):
            s = k.stream
            s.release = {}
            s.send(sp, s.sent)

        @block.tensor
        def _(pe):
            def scores(h):
                if h:
                    pe.wait_ge(probs, 8 * h)
                base = (h % 2) * 64
                for j in range(NT):
                    bank, col = score_cols(j)
                    t0 = 0 if j < 2 else 256
                    last = nc.tensor.matmul(k.ps[:, bank, col + t0:col + T], k.qk[base:base + 64, 4 + h // 2, j * P:(j + 1) * P],
                                            k.qk[base:base + 64, h // 2, t0:T], start=True, stop=True)
                last.then_inc(scored, 1)

            def spread_m(n):
                h, d = n // 2, n % 2
                if n >= 2:
                    pe.wait_ge(weighed, 4 * (n - 1))
                src = (k.scan_m, k.scan_m_rev)[d]
                nc.tensor.matmul(k.ps[:, 3 + d, :], k.ident[0:16, 8 * d + h:8 * d + h + 1].to_broadcast([16, P]),
                                 src[0:16, :], start=True, stop=True).then_inc(spread, 1)

            def values(n):
                h, d = n // 2, n % 2
                pe.wait_ge(masked, n + 1)
                if n:
                    pe.wait_ge(summed, n)
                for i in range(NT):
                    js = SOURCES[d][i]
                    for m, j in enumerate(js):
                        last = nc.tensor.matmul(k.ps[:, 5 + i // 2, (i % 2) * 256:(i % 2) * 256 + DV + 1],
                                                prob[:, n % 2, j, i * P:(i + 1) * P], k.vaug[:, j, h, 0:DV + 1],
                                                start=(m == 0), stop=(m == len(js) - 1))
                last.then_inc(turn_done, 1)

            scores(0)
            spread_m(0)
            spread_m(1)
            for n in range(turns):
                if n % 2 == 0 and n:
                    scores(n // 2)
                    spread_m(n)
                    spread_m(n + 1)
                if n:
                    values(n - 1)
            values(turns - 1)

        @block.scalar
        def _(act):
            for n in range(turns):
                h, d = n // 2, n % 2
                act.wait_ge(spread, n + 1)
                for j in range(NT):
                    t0, t1 = (x * P for x in SEEN[d][j])
                    if n:
                        act.wait_ge(probs, 4 * (n - 1) + j + 1)
                    nc.scalar.activation(decay[:, j, t0:t1], k.ps[:, 3 + d, t0:t1], ACT.Exp, scale=-1.0,
                                         bias=k.a_cols[:, j, 8 * d + h:8 * d + h + 1]).then_inc(weighed, 1)

        @block.vector
        def _(dve):
            chain = Chain(dve, own)

            def weigh(n):
                h, d = n // 2, n % 2
                dve.wait_ge(scored, h + 1)
                if n >= 2:
                    dve.wait_ge(turn_done, n - 1)
                for j in range(NT):
                    t0, t1 = (x * P for x in SEEN[d][j])
                    bank, col = score_cols(j)
                    dve.wait_ge(weighed, 4 * n + j + 1)
                    nc.vector.scalar_tensor_tensor(out=prob[:, n % 2, j, t0:t1], in0=k.ps[:, bank, col + t0:col + t1],
                                                   scalar=SHIFT, in1=decay[:, j, t0:t1], op0=ALU.mult,
                                                   op1=ALU.mult).then_inc(probs, 1)

            def finish(n):
                h, d = n // 2, n % 2
                dve.wait_ge(turn_done, n + 1)
                out = k.ps[:, 5:7, :].rearrange("p b (i c) -> p (b i) c", i=2)
                den = k.den[:, n % 2, :]
                chain.link(nc.vector.tensor_tensor(den, out[:, :, DV], k.e_cols[:, :, 8 * d + h], ALU.max))
                chain.link(nc.vector.scalar_tensor_tensor(out=den, in0=out[:, :, DV], scalar=-1.0, in1=den,
                                                          op0=ALU.mult, op1=ALU.max))
                chain.link(nc.vector.reciprocal(den, den))
                if n >= 2:
                    dve.wait_ge(added, n // 2)
                nc.vector.tensor_tensor(part[:, d, :].rearrange("p (i c) -> p i c", i=NT), out[:, :, 0:DV],
                                        den.unsqueeze(2).to_broadcast([P, NT, DV]), ALU.mult).then_inc(summed, 1)

            for n in range(turns):
                weigh(n)
                if n:
                    finish(n - 1)
            finish(turns - 1)

        @block.gpsimd
        def _(pool):
            def add(h):
                pool.wait_ge(summed, 2 * h + 2)
                hv = k.tok[:, :, h * DV:(h + 1) * DV]
                pool.tensor_tensor(hv, part[:, 0, :].rearrange("p (i c) -> p i c", i=NT),
                                   part[:, 1, :].rearrange("p (i c) -> p i c", i=NT), ALU.add).then_inc(added, 1)

            for n in range(turns):
                d = n % 2
                pool.wait_ge(probs, 4 * n + 4)
                flat = k.u_area[:, d * NT * T:(d + 1) * NT * T]
                diag = bass.AP(flat.tensor, flat.offset, [list(flat.ap[0]), [T + P, NT], [1, P]])
                sign = 1 if d == 0 else -1
                pool.affine_select(out=diag, in_=diag, compare_op=ALU.is_ge, fill=0.0, base=0,
                                   pattern=[[0, NT], [sign, P]], channel_multiplier=-sign).then_inc(masked, 1)
                if d == 1 and n > 1:
                    add(n // 2 - 1)
            add(HEADS - 1)



def mixer_out(k, name, unit, tiles, gain0, gate_of, column_major):
    nc, s, u0 = k.nc, k.stream, k.plan[unit]
    n_t = len(tiles)
    t0 = tiles[0]
    squared, rooted, normed = k.sem(name + "_hsq"), k.sem(name + "_hroot"), k.sem(name + "_hnormed")
    turned, cols_copied, own = k.sem(name + "_hturned"), k.sem(name + "_hcols"), k.sem(name + "_hown")
    r = residual_sems(k, name + "_res", lambda i, half: 4 * half + i,
                      lambda i, half: (n_t if half == 0 else n_t + 1 + i - t0))
    w = Pieces(k, name, u0, ["rows"] * 2, [range(n_t), range(n_t, 2 * n_t)], r.ready, k.out_parts[:2], k.out_parts[2:])
    width = n_t * P
    col0 = t0 * P
    sums_of = lambda n: k.head_sum[:, n * HEADS:(n + 1) * HEADS]
    split_behind = (0, 2, 5, 7)
    h_cols = k.big[:, 0:KD * T].rearrange("p (c t) -> p c t", c=KD)

    with nc.Block() as block:

        @block.sync
        def _(sp):
            s.send(sp, u0 + 2 + RING)

        @block.scalar
        def _(act):
            for n, i in enumerate(tiles):
                nc.scalar.activation(k.sq[:, n, :], k.tok[:, i, :], ACT.Square).then_inc(squared, 1)
            for n in range(n_t):
                act.wait_ge(own, n + 1)
                nc.scalar.activation(sums_of(n), sums_of(n), ACT.Sqrt, bias=k.eps[:, 0:1], scale=1.0 / DV).then_inc(rooted, 1)
            for h in range(HEADS):
                act.wait_ge(cols_copied, h + 1)
                nc.scalar.activation(k.u_high[:, h, col0:col0 + width], h_cols[:, h, col0:col0 + width], ACT.Copy).then_inc(w.u_high_done, 1)
                if h in split_behind:
                    w.split_high(act, split_behind.index(h))
            for p in range(len(split_behind), w.count):
                w.split_high(act, p)
            residual_scalar(k, act, r, tiles, True)

        @block.vector
        def _(dve):
            def low(h):
                dve.wait_ge(w.u_high_done, h + 1)
                cols = slice(col0, col0 + width)
                nc.vector.tensor_tensor(k.u_low[:, h, cols], h_cols[:, h, cols], k.u_high[:, h, cols].bitcast(F32),
                                        ALU.subtract).then_inc(w.u_low_done, 1)

            for n in range(n_t):
                dve.wait_ge(squared, n + 1)
                nc.vector.tensor_reduce(out=sums_of(n), in_=k.sq[:, n, :].rearrange("p (h c) -> p h c", h=HEADS),
                                        op=ALU.add, axis=AX.X).then_inc(own, 1)
            for n, i in enumerate(tiles):
                dve.wait_ge(rooted, n + 1)
                nc.vector.reciprocal(sums_of(n), sums_of(n)).then_inc(own, 1)
                dve.wait_ge(own, n_t + n + 1)
                nc.vector.tensor_tensor(k.tok[:, i, :].rearrange("p (h c) -> p h c", h=HEADS),
                                        k.tok[:, i, :].rearrange("p (h c) -> p h c", h=HEADS),
                                        sums_of(n).unsqueeze(2).to_broadcast([P, HEADS, DV]),
                                        ALU.mult).then_inc(normed, 1)
            for h in range(HEADS):
                dve.wait_ge(turned, h + 1)
                src, gate, dst = k.ps[:, 4 + h % 4, 0:width], gate_of(h), h_cols[:, h, col0:col0 + width]
                if column_major:
                    src = src.rearrange("p (w r) -> p r w", r=GRID_H)
                    gate = gate.rearrange("p (w r) -> p r w", r=GRID_H)
                    dst = dst.rearrange("p (r w) -> p r w", r=GRID_H)
                nc.vector.scalar_tensor_tensor(out=dst, in0=src, scalar=k.vcol[:, gain0 + h:gain0 + h + 1], in1=gate,
                                               op0=ALU.mult, op1=ALU.mult).then_inc(cols_copied, 1)
                if h:
                    low(h - 1)
                if h in split_behind:
                    w.split_low(dve, split_behind.index(h))
            low(HEADS - 1)
            for p in range(len(split_behind), w.count):
                w.split_low(dve, p)
            residual_vector(k, dve, r, tiles, 0, True)

        @block.tensor
        def _(pe):
            def turn(h):
                if h >= 4:
                    pe.wait_ge(cols_copied, h - 3)
                for n, i in enumerate(tiles):
                    last = nc.tensor.transpose(k.ps[:, 4 + h % 4, n * P:(n + 1) * P], k.tok[:, i, h * DV:(h + 1) * DV],
                                               k.ident[:, :])
                last.then_inc(turned, 1)

            pe.wait_ge(normed, n_t)
            for h in range(4):
                turn(h)
            for p in range(w.count):
                half, q = p // 4, p % 4
                pe.wait_ge(w.low_done, p + 1)
                wh, wl = w.parts(p)
                for n, i in enumerate(tiles):
                    for m in range(2):
                        c = 2 * q + m
                        pe.wait_ge(w.u_low_done, HEADS if half else c + 1)
                        hh, hl = (x[:, c, i * P:(i + 1) * P] for x in (k.u_high, k.u_low))
                        out = k.ps[:, 4 * half + i, :]
                        nc.tensor.matmul(out, hh, wh[:, m, :], start=(c == 0), stop=False)
                        nc.tensor.matmul(out, hh, wl[:, m, :], start=False, stop=False)
                        last = nc.tensor.matmul(out, hl, wh[:, m, :], start=False, stop=(c == KD - 1))
                    if q == 3:
                        last.then_inc(r.ready, 1)
                if q < 3:
                    last.then_inc(w.rows_used, 1)
                if p < 2:
                    turn(2 * p + 4)
                    turn(2 * p + 5)



def feed_forward(k):
    nc, s, u0 = k.nc, k.stream, k.plan["f_up"]
    chunks = [min(F_GROUP, FC - f) for f in range(0, FC, F_GROUP)]
    units = [c // 2 + -(-c // 4) for c in chunks]
    per = 3 * F_GROUP
    last_g = len(chunks) - 1
    assert all(c == F_GROUP for c in chunks[:-1]) and units[0] % RING == 0 and per % W_BUFS == 0
    u_high, u_low = k.sem("f_u_high"), k.sem("f_u_low")
    high_done, low_done, used = k.sem("f_high_done"), k.sem("f_low_done"), k.sem("f_used")
    silu_ready, mult_done = k.sem("f_silu_ready"), k.sem("f_mult_done")
    hid_high, hid_low = k.sem("f_hid_high"), k.sem("f_hid_low")
    y_ready, y_added, zeroed = k.sem("f_y_ready"), k.sem("f_y_added"), k.sem("f_zeroed")
    r = residual_sems(k, "f_res", None, None)
    silu = k.ex[:, 0:2 * HALF].rearrange("p (b t) -> p b t", b=2)
    hid_raw = k.ex[:, 2 * HALF:4 * HALF].rearrange("p (b t) -> p b t", b=2)

    def unit_of(c, p):
        if p < 2 * c:
            return p // 4, p % 4 == 0
        return c // 2 + (p - 2 * c) // 4, (p - 2 * c) % 4 == 0

    def raw(c, p):
        slot = s.slot(u0 + unit_of(c, p)[0])
        if p < 2 * c:
            return slot[:, 0:SLOT].rearrange("p (k s n) -> p k s n", k=KD, s=2)[:, :, p % 2, (p // 2 % 2) * P:(p // 2 % 2 + 1) * P]
        return slot[:, ((p - 2 * c) % 4) * D:((p - 2 * c) % 4 + 1) * D]

    def piece(area, c, p):
        b = area[:, (p % W_BUFS) * W_PIECE:(p % W_BUFS + 1) * W_PIECE]
        return b.rearrange("p (k n) -> p k n", k=KD) if p < 2 * c else b

    s.release = {}
    for g, c in enumerate(chunks):
        for p in range(3 * c):
            s.release[u0 + g * units[0] + unit_of(c, p)[0]] = (low_done, g * per + p + 1)

    with nc.Block() as block:

        @block.sync
        def _(sp):
            s.send(sp, u0 + sum(units) + RING)

        @block.tensor
        def _(pe):
            pe.nop().then_inc(used, W_BUFS)

            def group(g, c):
                for p in range(2 * c):
                    q, side = p // 2, p % 2
                    bank = 2 * (q % 4) + side
                    if q < 4:
                        pe.wait_ge(y_added, g * 8 + (bank + 1))
                    else:
                        pe.wait_ge(mult_done, g * F_GROUP + (q - 1))
                    pe.wait_ge(low_done, g * per + (p + 1))
                    wh, wl = piece(k.fw_high, c, p), piece(k.fw_low, c, p)
                    for m in range(KD):
                        if p == 0:
                            pe.wait_ge(u_low, m + 1)
                        nc.tensor.matmul(k.ps[:, bank, :], wh[:, m, :], k.u_high[:, m, :], start=(m == 0), stop=False)
                        nc.tensor.matmul(k.ps[:, bank, :], wh[:, m, :], k.u_low[:, m, :], start=False, stop=False)
                        last = nc.tensor.matmul(k.ps[:, bank, :], wl[:, m, :], k.u_high[:, m, :], start=False, stop=(m == KD - 1))
                    last.then_inc(used, 1)
                for f in range(c):
                    p = 2 * c + f
                    pe.wait_ge(low_done, g * per + (p + 1))
                    pe.wait_ge(hid_low, g * F_GROUP + (f + 1))
                    wh, wl = piece(k.fw_high, c, p), piece(k.fw_low, c, p)
                    for i in range(NT):
                        if f == 0:
                            pe.wait_ge(mult_done, g * F_GROUP + (2 + max(q for q in range(c) if q % 4 == i) + 1))
                        hh, hl = (h[:, f, i * P:(i + 1) * P] for h in (k.fh_high, k.fh_low))
                        for half in range(2):
                            cols = slice(half * HALF, (half + 1) * HALF)
                            out = k.ps[:, 2 * i + half, :]
                            nc.tensor.matmul(out, hh, wh[:, cols], start=(f == 0), stop=False)
                            nc.tensor.matmul(out, hh, wl[:, cols], start=False, stop=False)
                            last = nc.tensor.matmul(out, hl, wh[:, cols], start=False, stop=(f == c - 1))
                            if f == c - 1 and (i, half) != (NT - 1, 1):
                                last.then_inc(y_ready, 1)
                    last.then_inc(used, 1)

            with pe.Fori(0, last_g) as g:
                group(g, F_GROUP)
            group(last_g, chunks[-1])

        def steps(engine, split, post, g, c, last):
            for p in range(3 * c):
                if p == 3 * c - 1:
                    post(g, c, p)
                if p + W_BUFS < 3 * c:
                    split(g, c, p + W_BUFS)
                elif not last:
                    split(g + 1, F_GROUP, p + W_BUFS - 3 * c)
                if p < 3 * c - 1:
                    post(g, c, p)

        @block.scalar
        def _(act):
            def split(g, c, p):
                n, first = unit_of(c, p)
                if first:
                    n += u0
                    act.wait_ge(s.loaded[n % RING], s.value[n] + g * (s.value[n + units[0]] - s.value[n])
                                if c == F_GROUP else s.value[n + last_g * units[0]])
                act.wait_ge(used, g * per + (p + 1))
                nc.scalar.activation(piece(k.fw_high, c, p), raw(c, p), ACT.Copy).then_inc(high_done, 1)

            def post(g, c, p):
                q = p // 2
                if p < 2 * c and p % 2:
                    act.wait_ge(used, g * per + (p + W_BUFS + 1))
                    act.wait_ge(mult_done, g * F_GROUP + (q + 1))
                    nc.scalar.activation(silu[:, q % 2, :], k.ps[:, 2 * (q % 4), :], ACT.Silu).then_inc(silu_ready, 1)
                elif 0 < p <= 2 * c and p % 2 == 0:
                    q -= 1
                    act.wait_ge(mult_done, g * F_GROUP + (2 + q + 1))
                    nc.scalar.activation(k.fh_high[:, q, :], hid_raw[:, q % 2, :], ACT.Copy).then_inc(hid_high, 1)

            for m in range(KD):
                nc.scalar.activation(k.u_high[:, m, :], k.u_raw[:, m, :], ACT.Copy).then_inc(u_high, 1)
                if m in (1, 3):
                    split(0, F_GROUP, m // 2)
            with act.Fori(0, last_g) as g:
                steps(act, split, post, g, F_GROUP, False)
            steps(act, split, post, last_g, chunks[-1], True)
            residual_scalar(k, act, r, range(NT), False, lambda n: act.wait_ge(y_added, 8 * (last_g + 1) + 2 * (n + 1)))

        @block.gpsimd
        def _(pool):
            pool.memset(k.tok[:, :, :], 0.0).then_inc(zeroed, 1)

        @block.vector
        def _(dve):
            dve.nop().then_inc(y_added, 8)
            dve.nop().then_inc(mult_done, 2)

            def split(g, c, p):
                dve.wait_ge(high_done, g * per + (p + 1))
                nc.vector.tensor_tensor(piece(k.fw_low, c, p), raw(c, p), piece(k.fw_high, c, p).bitcast(F32), ALU.subtract).then_inc(low_done, 1)

            def post(g, c, p):
                q = p // 2
                if p < 2 * c and p % 2:
                    dve.wait_ge(silu_ready, g * F_GROUP + (q + 1))
                    nc.vector.tensor_tensor(hid_raw[:, q % 2, :], silu[:, q % 2, :], k.ps[:, 2 * (q % 4) + 1, :],
                                            ALU.mult).then_inc(mult_done, 1)
                elif 0 < p <= 2 * c and p % 2 == 0:
                    q -= 1
                    dve.wait_ge(hid_high, g * F_GROUP + (q + 1))
                    nc.vector.tensor_tensor(k.fh_low[:, q, :], hid_raw[:, q % 2, :], k.fh_high[:, q, :].bitcast(F32),
                                            ALU.subtract).then_inc(hid_low, 1)
                elif p == 3 * c - 1:
                    for b in range(8):
                        if b < 7:
                            dve.wait_ge(y_ready, g * 7 + (b + 1))
                        else:
                            dve.wait_ge(used, g * per + (W_BUFS + 3 * c))
                        y = k.tok[:, b // 2, (b % 2) * HALF:(b % 2 + 1) * HALF]
                        nc.vector.tensor_tensor(y, y, k.ps[:, b, :], ALU.add).then_inc(y_added, 1)

            for m in range(KD):
                dve.wait_ge(u_high, m + 1)
                nc.vector.tensor_tensor(k.u_low[:, m, :], k.u_raw[:, m, :], k.u_high[:, m, :].bitcast(F32), ALU.subtract).then_inc(u_low, 1)
                if m in (1, 3):
                    split(0, F_GROUP, m // 2)
            dve.wait_ge(zeroed, 1)
            with dve.Fori(0, last_g) as g:
                steps(dve, split, post, g, F_GROUP, False)
            steps(dve, split, post, last_g, chunks[-1], True)
            residual_vector(k, dve, r, range(NT), 1, False)



def hgrn_in(k):
    nc, s, u0 = k.nc, k.stream, k.plan["h_in"]
    ready, copied_a, copied_v = k.sem("hi_ready"), k.sem("hi_copied_a"), k.sem("hi_copied_v")
    row_sig, lb_in, lb_row, f_made, act_own, own = (k.sem("hi_" + n) for n in ("row_sig", "lb_in", "lb_row", "f_made", "act_own", "own"))
    raised = k.sem("hi_raised")
    lb = k.tok[:, 2:4, :].rearrange("p a n -> p (a n)")
    bias_row = k.big[0:1, 8 * D:10 * D]
    jobs = []
    for u in range(4):
        jobs += [(u, "f_row", i) for i in range(2)] + [(u, "f_col", i) for i in range(4)]
    jobs += [(u, "v", i) for u in (4, 5) for i in range(4)]
    jobs += [(u, "q", i) for u in (6, 7) for i in range(4)]
    jobs += [(u, "g", i) for u in (8, 9) for i in range(4)]
    units = 10
    jobs_of = [[n for n, job in enumerate(jobs) if job[0] == u] for u in range(units)]
    w = Pieces(k, "h", u0, ["rows"] * 6 + ["columns"] * 4, jobs_of, ready, k.h_high, k.h_low)
    by_act = [j[1] != "v" and j[1] != "q" for j in jobs]
    BANKS = 8

    def freed(n):
        return (copied_a, sum(by_act[:n + 1])) if by_act[n] else (copied_v, n + 1 - sum(by_act[:n + 1]))

    def jobs_after(p):
        if not w.by_rows(p):
            return [jobs_of[p // 4][p % 4]]
        return jobs_of[p // 4] if p % 4 == 3 else []

    with nc.Block() as block:

        @block.sync
        def _(sp):
            sp.dma_start(bias_row, k.a["h_b_f"].rearrange("o a n -> o (a n)")).then_inc(lb_in, 16)
            sp.dma_start(lb, k.a["h_lb_raw"].rearrange("o a n -> o (a n)").to_broadcast([P, 2 * D])).then_inc(lb_in, 16)
            s.send(sp, u0 + units + RING)

        @block.tensor
        def _(pe):
            pe.wait_ge(lb_in, 32)
            for p in range(4 * units):
                u, q = p // 4, p % 4
                pe.wait_ge(w.low_done, p + 1)
                wh, wl = w.parts(p)
                chunks = range(2 * q, 2 * q + 2) if w.by_rows(p) else range(KD)
                for n in (jobs_of[u] if w.by_rows(p) else jobs_after(p)):
                    _, kind, i = jobs[n]
                    rows = kind in ("f_row", "v")
                    out = k.ps[:, n % BANKS, 0:HALF if rows else LAT]
                    if chunks[0] == 0 and n >= BANKS:
                        pe.wait_ge(*freed(n - BANKS))
                    for c in chunks:
                        if n == 0:
                            pe.wait_ge(w.u_low_done, c + 1)
                        m = c - chunks[0]
                        if rows:
                            (h1, l1), (h2, l2) = ([x[:, c, i * P:(i + 1) * P] for x in (k.u_high, k.u_low)],
                                                  (wh[:, m, :], wl[:, m, :]))
                        else:
                            (h1, l1), (h2, l2) = ([x[:, m, i * P:(i + 1) * P] if w.by_rows(p) else x[:, m, :] for x in (wh, wl)],
                                                  [x[:, c, CTX:T] for x in (k.u_high, k.u_low)])
                        nc.tensor.matmul(out, h1, h2, start=(c == 0), stop=False)
                        nc.tensor.matmul(out, h1, l2, start=False, stop=False)
                        if kind == "f_row" and c == KD - 1:
                            nc.tensor.matmul(out, k.ones[0:1, :], bias_row[0:1, u * HALF:(u + 1) * HALF], start=False, stop=False)
                        last = nc.tensor.matmul(out, l1, h2, start=False, stop=(c == KD - 1))
                    if n in jobs_after(p):
                        last.then_inc(ready, 1)
                if w.by_rows(p) and q < 3:
                    last.then_inc(w.rows_used, 1)

        @block.scalar
        def _(act):
            def take(n):
                u, kind, i = jobs[n]
                if not by_act[n]:
                    return
                act.wait_ge(ready, n + 1)
                if kind == "f_row":
                    dst = k.f_rows[:, i, u * HALF:(u + 1) * HALF]
                    nc.scalar.activation(dst, k.ps[:, n % BANKS, :], ACT.Sigmoid).then_inc(copied_a, 1)
                elif kind == "f_col":
                    c = (u % 2) * 4 + i
                    col = (u // 2) * KD + c
                    nc.scalar.activation(k.f_cols[:, u // 2, c, :], k.ps[:, n % BANKS, 0:LAT], ACT.Sigmoid,
                                         bias=k.vcol[:, 104 + col:105 + col]).then_inc(copied_a, 1)
                else:
                    c = (u - 8) * 4 + i
                    nc.scalar.activation(k.g_cols(c), k.ps[:, n % BANKS, 0:LAT], ACT.Sigmoid).then_inc(copied_a, 1)

            w.split_u_high(act)
            act.wait_ge(lb_row, 1)
            nc.scalar.activation(lb, lb, ACT.Exp).then_inc(lb_row, 1)
            for p in range(4 * units):
                for n in jobs_after(p):
                    take(n)
                w.split_high(act, p + 2)
            act.wait_ge(f_made, 16)
            for i in range(2):
                nc.scalar.activation(k.f_rows[:, i, :], k.f_rows[:, i, :], ACT.Ln)

        @block.gpsimd
        def _(pool):
            pool.wait_ge(lb_in, 32)
            pool.tensor_tensor(lb, lb, lb, ALU.subtract).then_inc(lb_row, 1)

        @block.vector
        def _(dve):
            chain = Chain(dve, own)

            def take(n):
                u, kind, i = jobs[n]
                if kind == "f_row":
                    dve.wait_ge(*freed(n))
                    f = k.f_rows[:, i, u * HALF:(u + 1) * HALF]
                    kk = k.k_rows[:, i, u * HALF:(u + 1) * HALF]
                    chain.link(nc.vector.scalar_tensor_tensor(out=kk, in0=f, scalar=-1.0, in1=lb[:, u * HALF:(u + 1) * HALF],
                                                              op0=ALU.add, op1=ALU.mult))
                    chain.link(nc.vector.tensor_tensor(f, f, kk, ALU.subtract))
                    chain.link(nc.vector.tensor_scalar(kk, f, -1.0, 1.0, ALU.mult, ALU.add))
                    nc.vector.tensor_scalar(f, f, 2.0 ** -63, None, ALU.max).then_inc(f_made, 2)
                elif kind == "f_col":
                    dve.wait_ge(*freed(n))
                    c = (u % 2) * 4 + i
                    col = (u // 2) * KD + c
                    f = k.f_cols[:, u // 2, c, :]
                    nc.vector.tensor_scalar(f, f, k.lb_rest[:, col:col + 1], k.lb_col[:, col:col + 1], ALU.mult, ALU.add)
                elif kind == "v":
                    dve.wait_ge(ready, n + 1)
                    nc.vector.tensor_copy(k.v_rows[:, i, (u - 4) * HALF:(u - 3) * HALF], k.ps[:, n % BANKS, :]).then_inc(copied_v, 1)
                elif kind == "q":
                    dve.wait_ge(ready, n + 1)
                    nc.vector.tensor_copy(k.q_cols[:, (u - 6) * 4 + i, :], k.ps[:, n % BANKS, 0:LAT]).then_inc(copied_v, 1)

            w.split_u_low(dve)
            dve.wait_ge(lb_row, 2)
            dve.wait_ge(w.u_low_done, KD)

            def lower_bound(u):
                b, inverse = (x[:, u * HALF:(u + 1) * HALF] for x in (lb, k.k_rows[:, 0, :]))
                chain.link(nc.vector.reciprocal(inverse, b))
                chain.link(nc.vector.tensor_tensor(inverse, b, inverse, ALU.mult))
                chain.link(nc.vector.tensor_tensor(b, inverse, inverse, ALU.subtract))

            for p in range(4 * units):
                banks_first = p // 4 >= 4
                if not banks_first:
                    w.split_low(dve, p + 2)
                    if p % 4 == 1:
                        lower_bound(p // 4)
                for n in jobs_after(p):
                    take(n)
                if banks_first:
                    w.split_low(dve, p + 2)



def hgrn_state(k):
    nc = k.nc
    summed, decayed, scaled, stated, copied = (k.sem("hs_" + n) for n in ("summed", "decayed", "scaled", "stated", "copied"))
    rest = k.sem("hs_rest")
    decay = k.junk.rearrange("p (b n) -> p b n", b=2)
    jobs = [(d, half, i) for d in range(2) for half in range(2) for i in range(2)]

    with nc.Block() as block:

        @block.tensor
        def _(pe):
            for n, (d, half, i) in enumerate(jobs):
                if n >= 4:
                    pe.wait_ge(decayed, n - 3)
                cols = slice(d * D + half * HALF, d * D + (half + 1) * HALF)
                own = (k.after, k.before)[d]
                other = (i == 0) if d == 0 else (i == 1)
                last = nc.tensor.matmul(k.ps[:, n % 4, :], own[:, :], k.f_rows[:, i, cols], start=True, stop=not other)
                if other:
                    last = nc.tensor.matmul(k.ps[:, n % 4, :], k.ones[:, :], k.f_rows[:, 1 - i, cols], start=False, stop=True)
                last.then_inc(summed, 1)
            for g in range(4):
                d, half = g // 2, g % 2
                pe.wait_ge(scaled, 2 * g + 2)
                for q in range(4):
                    h = half * 4 + q
                    for i in range(2):
                        last = nc.tensor.matmul(k.ps[:, 4 + g, q * P:(q + 1) * P],
                                                k.k_rows[:, i, d * D + h * P:d * D + (h + 1) * P],
                                                k.v_rows[:, i, h * P:(h + 1) * P], start=(i == 0), stop=(i == 1))
                last.then_inc(stated, 1)

        @block.scalar
        def _(act):
            for n in range(len(jobs)):
                act.wait_ge(summed, n + 1)
                if n >= 2:
                    act.wait_ge(scaled, n - 1)
                nc.scalar.activation(decay[:, n % 2, :], k.ps[:, n % 4, :], ACT.Exp).then_inc(decayed, 1)
            for g in range(4):
                act.wait_ge(stated, g + 1)
                nc.scalar.activation(k.state[:, 4 * g:4 * g + 4, :], k.ps[:, 4 + g, :].rearrange("p (h c) -> p h c", h=4), ACT.Copy)

        @block.vector
        def _(dve):
            for n, (d, half, i) in enumerate(jobs):
                cols = slice(d * D + half * HALF, d * D + (half + 1) * HALF)
                dve.wait_ge(decayed, n + 1)
                nc.vector.tensor_tensor(k.k_rows[:, i, cols], k.k_rows[:, i, cols], decay[:, n % 2, :], ALU.mult).then_inc(scaled, 1)



def hgrn_pairs(k):
    nc = k.nc
    q_made, k_made, q_grown, k_grown, ends_made = (k.sem("hp_" + n) for n in ("q_made", "k_made", "q_grown", "k_grown", "ends_made"))
    paired, taken, sum_made, joined = (k.sem("hp_" + n) for n in ("paired", "taken", "sum_made", "joined"))
    q_f, k_f, ends = k.q_fac, k.k_fac, k.f_cols
    G = 4

    def halves(x, d, g, size):
        v = x[:, d, G * g:G * g + G, :].rearrange("p h (b two l) -> p (h b) two l", two=2, l=size)
        return v[:, :, 0, :], v[:, :, 1, :]

    def end_of(d, g, size):
        v = ends[:, d, G * g:G * g + G, :].rearrange("p h (b two l) -> p (h b) two l", two=2, l=size)
        return v[:, :, 0, 0:1], v[:, :, 1, 0:1]

    def joined_half(which, g, size, side):
        return k.joined[:, which, G * g:G * g + G, :].rearrange("p h (b two l) -> p (h b) two l", two=2, l=size)[:, :, side, :]

    n_blocks = lambda size: G * LAT // (2 * size)

    with nc.Block() as block:

        @block.tensor
        def _(pe):
            for level in range(-1, LEVELS + 1):
                for g in range(2):
                    n = (level + 1) * 2 + g
                    if level < 0:
                        pe.wait_ge(sum_made, g + 1)
                    elif level < LEVELS:
                        pe.wait_ge(joined, n - 1)
                    else:
                        pe.wait_ge(q_grown, 2 * (n - 3))
                        pe.wait_ge(k_grown, 2 * (n - 3))
                    if n >= 4:
                        pe.wait_ge(taken, 2 * (n - 3))
                    for i in range(2):
                        bank = (n % 4) * 2 + i
                        for q in range(G):
                            h = G * g + q
                            out = k.ps[:, bank, q * P:(q + 1) * P]
                            t = slice(i * P, (i + 1) * P)
                            if level < 0:
                                last = nc.tensor.matmul(out, k.k_sum[:, h, t], k.q_cols[:, h, t], start=True, stop=True)
                            elif level < LEVELS:
                                last = nc.tensor.matmul(out, k.joined[:, 0, h, t], k.joined[:, 1, h, t], start=True, stop=True)
                            else:
                                last = nc.tensor.matmul(out, k_f[:, i, h, t], q_f[:, i, h, (1 - i) * P:(2 - i) * P],
                                                        start=True, stop=True)
                        last.then_inc(paired, 1)

        @block.vector
        def _(dve):
            for g in range(2):
                for d in range(2):
                    nc.vector.tensor_tensor(q_f[:, d, G * g:G * g + G, :], k.q_cols[:, G * g:G * g + G, :],
                                            ends[:, d, G * g:G * g + G, :], ALU.mult).then_inc(q_made, 1)

            def take(level, g):
                n = (level + 1) * 2 + g
                for i in range(2):
                    bank = (n % 4) * 2 + i
                    dve.wait_ge(paired, 2 * n + i + 1)
                    src = k.ps[:, bank, :].rearrange("p (h t) -> p h t", h=G)
                    near, cross = k.pair_near[:, g, i, :, :], k.pair_cross[:, g, i, :, :]
                    if level < 0:
                        nc.vector.tensor_tensor(near, src, k.ident[:, :].unsqueeze(1).to_broadcast([P, G, P]),
                                                ALU.mult).then_inc(taken, 1)
                    elif level < LEVELS:
                        dve.wait_ge(taken, 2 * (n - 2) + i + 1)
                        nc.vector.copy_predicated(near, k.level_mask[:, level, :].unsqueeze(1).to_broadcast([P, G, P]),
                                                  src).then_inc(taken, 1)
                    else:
                        nc.vector.tensor_copy(cross, src).then_inc(taken, 1)

            def grow(level, g):
                size, n = 2 ** level, (level + 1) * 2 + g
                if level < LEVELS:
                    dve.wait_ge(joined, n - 1)
                if level:
                    dve.wait_ge(q_grown, 2 * (n - 3))
                    dve.wait_ge(ends_made, 4 * (n - 3))
                else:
                    dve.wait_ge(q_made, 4)
                for d in range(2):
                    side = halves(q_f, d, g, size)[1 - d]
                    nc.vector.tensor_tensor(side, side, end_of(d, g, size)[d].to_broadcast([P, n_blocks(size), size]),
                                            ALU.mult).then_inc(q_grown, 1)

            turns = [(level, g) for level in range(-1, LEVELS) for g in range(2)]
            for n, (level, g) in enumerate(turns):
                if level >= 0:
                    grow(level, g)
                if n:
                    take(*turns[n - 1])
            take(*turns[-1])
            for g in range(2):
                take(LEVELS, g)
                grow(LEVELS, g)

        @block.scalar
        def _(act):
            for level in range(LEVELS):
                size = 2 ** level
                for g in range(2):
                    n = (level + 1) * 2 + g
                    if level:
                        act.wait_ge(q_grown, 2 * (n - 3))
                        act.wait_ge(k_grown, 2 * (n - 3))
                        act.wait_ge(paired, 2 * (n - 1))
                    else:
                        act.wait_ge(q_made, 2 * g + 2)
                        act.wait_ge(k_made, 2 * g + 2)
                    for d in range(2):
                        nc.scalar.activation(joined_half(0, g, size, d), halves(k_f, d, g, size)[d], ACT.Copy)
                        last = nc.scalar.activation(joined_half(1, g, size, 1 - d), halves(q_f, d, g, size)[1 - d], ACT.Copy)
                    last.then_inc(joined, 1)

        @block.gpsimd
        def _(pool):
            for g in range(2):
                for d in range(2):
                    pool.tensor_scalar(k_f[:, d, G * g:G * g + G, :], ends[:, d, G * g:G * g + G, :], -1.0, 1.0,
                                       ALU.mult, ALU.add).then_inc(k_made, 1)
                pool.wait_ge(k_made, 2 * g + 2)
                pool.tensor_tensor(k.k_sum[:, G * g:G * g + G, :], k_f[:, 0, G * g:G * g + G, :],
                                   k_f[:, 1, G * g:G * g + G, :], ALU.add).then_inc(sum_made, 1)
            for level in range(LEVELS):
                size = 2 ** level
                for g in range(2):
                    n = (level + 1) * 2 + g
                    turn = level * 2 + g
                    pool.wait_ge(joined, n - 1)
                    if level:
                        pool.wait_ge(k_grown, 2 * ((level - 1) * 2 + g + 1))
                        pool.wait_ge(ends_made, 4 * ((level - 1) * 2 + g + 1))
                    for d in range(2):
                        side = halves(k_f, d, g, size)[d]
                        end = end_of(d, g, size)[1 - d]
                        pool.tensor_tensor(side, side, end.to_broadcast([P, n_blocks(size), size]),
                                           ALU.mult).then_inc(k_grown, 1)
                    pool.wait_ge(q_grown, 2 * (turn + 1))
                    pool.wait_ge(k_grown, 2 * (turn + 1))
                    for d in range(2):
                        left, right = end_of(d, g, size)
                        pool.tensor_tensor(left, left, right, ALU.mult).then_inc(ends_made, 2)



def hgrn_values(k):
    nc = k.nc
    ready = k.sem("hv_ready")
    with nc.Block() as block:

        @block.tensor
        def _(pe):
            for i in range(2):
                for g in range(2):
                    for q in range(4):
                        h = 4 * g + q
                        out = k.ps[:, 2 * i + g, q * P:(q + 1) * P]
                        v = [k.v_rows[:, 2 + j, h * DV:(h + 1) * DV] for j in range(2)]
                        t = slice(i * P, (i + 1) * P)
                        nc.tensor.matmul(out, k.pair_near[:, g, i, q, :], v[i], start=True, stop=False)
                        nc.tensor.matmul(out, k.pair_cross[:, g, 1 - i, q, :], v[1 - i], start=False, stop=False)
                        nc.tensor.matmul(out, k.q_fac[:, 0, h, t], k.state[:, h, :], start=False, stop=False)
                        last = nc.tensor.matmul(out, k.q_fac[:, 1, h, t], k.state[:, 8 + h, :], start=False, stop=True)
                    last.then_inc(ready, 1)

        @block.vector
        def _(dve):
            for n in range(0, 4, 2):
                dve.wait_ge(ready, n + 1)
                nc.vector.tensor_copy(k.tok[:, 2 + n // 2, (n % 2) * HALF:(n % 2 + 1) * HALF], k.ps[:, n, :])

        @block.scalar
        def _(act):
            for n in range(1, 4, 2):
                act.wait_ge(ready, n + 1)
                nc.scalar.activation(k.tok[:, 2 + n // 2, (n % 2) * HALF:(n % 2 + 1) * HALF], k.ps[:, n, :], ACT.Copy)



def routing(k):
    nc = k.nc
    logits_ready, own, diff, expd, chosen, placed = (k.sem("r_" + n) for n in ("logits_ready", "own", "diff", "expd", "chosen", "placed"))
    r = k.route
    L, EQ, CAND, OH1, OH2, L2, COMB, SEL = (r[:, n, :, :] for n in range(8))
    V1, V2, IDX, W1, W2, EX = (r[:, 8 + n // 4, :, 2 * (n % 4):2 * (n % 4) + 1] for n in range(6))
    per = lambda v: v.to_broadcast([P, 2, EXPERTS])

    with nc.Block() as block:

        @block.tensor
        def _(pe):
            for i in range(2):
                for c in range(KD):
                    nc.tensor.matmul(k.ps[:, 0, i * 8:i * 8 + 8], k.u_cols[:, c, CTX + i * P:CTX + (i + 1) * P],
                                     k.w_router[:, c, :], start=(c == 0), stop=False)
                last = nc.tensor.matmul(k.ps[:, 0, i * 8:i * 8 + 8], k.ones[0:1, :], k.b_router[0:1, :], start=False, stop=True)
            last.then_inc(logits_ready, 1)
            pe.wait_ge(chosen, 1)
            nc.tensor.matmul(k.ps[:, 1, 0:8], k.before[:, :], SEL[:, 0, :], start=True, stop=True)
            nc.tensor.matmul(k.ps[:, 1, 8:16], k.ones[:, :], SEL[:, 0, :], start=True, stop=False)
            nc.tensor.matmul(k.ps[:, 1, 8:16], k.before[:, :], SEL[:, 1, :], start=False, stop=True)
            nc.tensor.matmul(k.ps[:, 1, 16:24], k.ones[:, :], SEL[:, 0, :], start=True, stop=False)
            nc.tensor.matmul(k.ps[:, 1, 16:24], k.ones[:, :], SEL[:, 1, :], start=False, stop=True).then_inc(placed, 1)

        @block.scalar
        def _(act):
            act.wait_ge(diff, 1)
            nc.scalar.activation(EX, EX, ACT.Exp).then_inc(expd, 1)

        @block.gpsimd
        def _(pool):
            pool.memset(k.acc[:, :, :], 0.0)

        @block.vector
        def _(dve):
            chain = Chain(dve, own)
            dve.wait_ge(logits_ready, 1)
            chain.link(nc.vector.tensor_copy(L, k.ps[:, 0, 0:16].rearrange("p (i e) -> p i e", i=2)))

            def pick(logits, value, onehot):
                chain.link(nc.vector.tensor_reduce(out=value, in_=logits, op=ALU.max, axis=AX.X))
                chain.link(nc.vector.tensor_tensor(EQ, logits, per(value), ALU.is_equal))
                chain.link(nc.vector.scalar_tensor_tensor(out=CAND, in0=EQ, scalar=-8.0, in1=k.expert_no[:, :, :],
                                                          op0=ALU.mult, op1=ALU.add))
                chain.link(nc.vector.tensor_reduce(out=IDX, in_=CAND, op=ALU.min, axis=AX.X))
                chain.link(nc.vector.tensor_tensor(onehot, CAND, per(IDX), ALU.is_equal))

            pick(L, V1, OH1)
            chain.link(nc.vector.scalar_tensor_tensor(out=L2, in0=OH1, scalar=-3.0e38, in1=L, op0=ALU.mult, op1=ALU.add))
            pick(L2, V2, OH2)
            chain.link(nc.vector.tensor_tensor(SEL, OH1, OH2, ALU.add))
            nc.vector.tensor_tensor(EX, V2, V1, ALU.subtract).then_inc(diff, 1)
            dve.nop().then_inc(chosen, 1)
            dve.wait_ge(expd, 1)
            chain.link(nc.vector.tensor_scalar(W2, EX, 1.0, None, ALU.add))
            chain.link(nc.vector.reciprocal(W1, W2))
            chain.link(nc.vector.tensor_tensor(W2, EX, W1, ALU.mult))
            chain.link(nc.vector.tensor_tensor(OH1, OH1, per(W1), ALU.mult))
            chain.link(nc.vector.tensor_tensor(OH2, OH2, per(W2), ALU.mult))
            nc.vector.memset(k.place[:, :, EXPERTS:EXPERTS + 1], -1.0)
            nc.vector.tensor_tensor(k.comb[:, :, :], OH1, OH2, ALU.add)
            dve.wait_ge(placed, 1)
            chain.link(nc.vector.scalar_tensor_tensor(out=EQ, in0=k.ps[:, 1, 0:16].rearrange("p (i e) -> p i e", i=2),
                                                      scalar=1.0, in1=SEL, op0=ALU.add, op1=ALU.mult))
            nc.vector.tensor_scalar(k.place[:, :, 0:EXPERTS], EQ, -1.0, None, ALU.add)
            chain.link(nc.vector.tensor_reduce(out=V1[:, 0, :], in_=k.ps[:, 1, 16:24], op=ALU.max, axis=AX.X))
            nc.vector.tensor_scalar(k.passes[:, 0:1], V1[:, 0, :], float(P), 1.0, ALU.is_gt, ALU.add)



def experts(k):
    nc, a = k.nc, k.a
    S = Names()
    S.used, S.high_done, S.low_done = k.sem("e_used"), k.sem("e_high_done"), k.sem("e_low_done")
    S.silu_ready, S.hid_done = k.sem("e_silu_ready"), k.sem("e_hid_done")
    S.places_ready, S.gathered = k.sem("e_places_ready"), k.sem("e_gathered")
    S.list_made, S.list_high, S.list_low = k.sem("e_list_made"), k.sem("e_list_high"), k.sem("e_list_low")
    S.pturned, S.pcopied, S.pcleared = (k.sem("e_" + n) for n in ("pturned", "pcopied", "pcleared"))
    S.hturned, S.hid_high, S.hid_low = k.sem("e_hturned"), k.sem("e_hid_high"), k.sem("e_hid_low")
    S.y_high, S.y_low, S.scattered, S.added = (k.sem("e_" + n) for n in ("y_high", "y_low", "scattered", "added"))
    loaded = [k.sem(f"e_loaded{i}") for i in range(E_RING)]
    HG = -(-FC // 4)
    per_slot = E_UNITS // E_RING
    Y0 = 2 * E_TILES
    PIECES = 2 * E_UNITS
    GS = KD // 2
    HIDDEN_TURNS = (15, 19, 23, 27, 33, 35)
    assert len(HIDDEN_TURNS) == HG

    down_units = [(0, 6), (6, 5), (11, 6), (17, 5)]
    down_pieces = [x for f, m in down_units for x in ((f, 3), (f + 3, m - 3))]

    def slot(j):
        return k.e_ring[:, (j % E_RING) * E_SLOT:(j % E_RING + 1) * E_SLOT]

    def piece_shape(p):
        if p < 2 * Y0:
            return GS, E_N, (p % 2) * GS * E_N
        m = down_pieces[(p - 2 * Y0) % len(down_pieces)][1]
        return m, HALF, (p % 2) * 3 * HALF

    def piece(buffer, p):
        m, n, _ = piece_shape(p)
        return buffer[:, (p % E_BUFS) * E_PIECE:(p % E_BUFS) * E_PIECE + m * n].rearrange("p (c n) -> p c n", c=m)

    def raw(p):
        m, n, first = piece_shape(p)
        return slot(p // 2)[:, first:first + m * n].rearrange("p (c n) -> p c n", c=m)

    def passes(engine):
        return engine.value_load(k.passes[0:1, 0:1], min_val=1, max_val=2)

    with nc.Block() as block:

        @block.sync
        def _(sp):
            n = passes(sp)
            with sp.Fori(0, n) as ps_:
                with sp.Fori(0, EXPERTS) as e:
                    it = sp.snap(ps_ * EXPERTS + e)
                    gu = a["e_w_gu"][0, e]
                    dn = a["e_w_down"][0, e]
                    for j in range(E_UNITS):
                        if j < Y0:
                            t, side = j // 2, j % 2
                            src = gu[:, side * FFN + t * E_N:side * FFN + (t + 1) * E_N].rearrange("(k p) n -> p k n", p=P)
                            dst = slot(j)[:, 0:KD * E_N].rearrange("p (k n) -> p k n", k=KD)
                        else:
                            half, (f, m) = (j - Y0) // 4, down_units[(j - Y0) % 4]
                            src = dn[f * P:(f + m) * P, half * HALF:(half + 1) * HALF].rearrange("(k p) n -> p k n", p=P)
                            dst = slot(j)[:, 0:m * HALF].rearrange("p (k n) -> p k n", k=m)
                        need = sp.snap(it * PIECES + (2 * j + 2))
                        sp.wait_ge(S.low_done, need)
                        sp.dma_start(dst, src).then_inc(loaded[j % E_RING], 16)

        @block.tensor
        def _(pe):
            n = passes(pe)
            pe.nop().then_inc(S.used, E_BUFS)

            def gather(m):
                pe.wait_ge(S.places_ready, m + 1)
                for c in range(KD):
                    for i in range(2):
                        last = nc.tensor.matmul(k.ps[:, 4 + c // 4, (c % 4) * P:(c % 4 + 1) * P],
                                                k.tok[:, 2 + i, c * P:(c + 1) * P], k.places[:, i, :],
                                                start=(i == 0), stop=(i == 1))
                last.then_inc(S.gathered, 1)

            def three_passes(it, p, out, high, low, first, chunks, total):
                pe.wait_ge(S.low_done, it * PIECES + (p + 1 + 2 * E_RING))
                w_high, w_low = piece(k.w_high, p), piece(k.w_low, p)
                for c in range(chunks):
                    f = first + c
                    nc.tensor.matmul(out, high[:, f, :], w_high[:, c, :], start=(f == 0), stop=False)
                    nc.tensor.matmul(out, high[:, f, :], w_low[:, c, :], start=False, stop=False)
                    last = nc.tensor.matmul(out, low[:, f, :], w_high[:, c, :], start=False, stop=(f == total - 1))
                last.then_inc(S.used, 1)

            def scatter(y_count, add_count, half):
                pe.wait_ge(S.y_low, y_count)
                pe.wait_ge(S.added, add_count + 1)
                for i in range(2):
                    for n, part in enumerate((k.ey_high, k.ey_low)):
                        last = nc.tensor.matmul(k.ps[:, 6 + i, :], k.place_cols[:, i * P:(i + 1) * P],
                                                part[:, half * HALF:(half + 1) * HALF], start=(n == 0), stop=(n == 1))
                    last.then_inc(S.scattered, 1)

            def turn_places(it, adds, e):
                pe.wait_ge(S.added, adds + 3)
                for i in range(2):
                    nc.tensor.transpose(k.ps[:, 6, i * P:(i + 1) * P], k.places[:, i, :], k.ident[:, :])
                for i in range(2):
                    last = nc.tensor.matmul(k.ps[:, 6, 256:257], k.places[:, i, :], k.comb[:, i, bass.ds(e, 1)],
                                            start=(i == 0), stop=(i == 1))
                last.then_inc(S.pturned, 1)

            def turn_hidden(it, g):
                m = min(4, FC - 4 * g)
                tiles = min(E_TILES, -(-(4 * g + m) * P // E_N))
                pe.wait_ge(S.hid_done, it * E_TILES + tiles + 2)
                if g == 1:
                    pe.wait_ge(S.pcopied, it + 1)
                elif g >= 2:
                    pe.wait_ge(S.hid_low, it * HG + g - 1)
                for q in range(m):
                    f = 4 * g + q
                    last = nc.tensor.transpose(k.ps[:, 7 - g % 2, q * P:(q + 1) * P], k.e_hid[:, f * P:(f + 1) * P],
                                               k.ident[:, :])
                last.then_inc(S.hturned, 1)

            with pe.Fori(0, n) as ps_:
                gather(ps_ * 9)
                with pe.Fori(0, EXPERTS) as e:
                    it = ps_ * EXPERTS + e
                    ys = ps_ * 17 + 2 * e
                    adds = ps_ * 34 + 4 * e
                    pe.wait_ge(S.list_low, ps_ * 9 + e + 1)

                    def after(p):
                        if p == 3:
                            scatter(ys + 1, adds, 1)
                        elif p == 11:
                            turn_places(it, adds, e)
                        elif p == 21:
                            gather(ps_ * 9 + e + 1)
                        elif p in HIDDEN_TURNS:
                            turn_hidden(it, HIDDEN_TURNS.index(p))
                        elif p == 42:
                            pe.wait_ge(S.hid_low, it * HG + HG)
                            scatter(ys + 2, adds + 2, 0)

                    for t in range(E_TILES):
                        pe.wait_ge(S.hid_done, it * E_TILES + t + 1)
                        for side in range(2):
                            for b in range(2):
                                p = 4 * t + 2 * side + b
                                three_passes(it, p, k.ps[:, 2 * (t % 2) + side, 0:E_N], k.list_h, k.list_l, b * GS, GS, KD)
                                after(p)
                    pe.wait_ge(S.list_made, ps_ * 9 + e + 2)
                    for half in range(2):
                        for b, (f, m) in enumerate(down_pieces):
                            if half == 0:
                                pe.wait_ge(S.hid_low, it * HG + ((f + m - 1) // 4 + 1))
                            p = 2 * Y0 + 8 * half + b
                            three_passes(it, p, k.ps[:, 4 + half, :], k.hid_h, k.hid_l, f, m, FC)
                            after(p)
                scatter(ps_ * 17 + 17, ps_ * 34 + 32, 1)

        @block.scalar
        def _(act):
            n = passes(act)

            def split(it, p):
                if p % 2 == 0:
                    j = p // 2
                    act.wait_ge(loaded[j % E_RING], it * (16 * per_slot) + 16 * (j // E_RING + 1))
                act.wait_ge(S.used, it * PIECES + (p + 1))
                nc.scalar.activation(piece(k.w_high, p), raw(p), ACT.Copy).then_inc(S.high_done, 1)

            def list_high(m):
                act.wait_ge(S.list_made, m + 1)
                nc.scalar.activation(k.list_h, k.list_raw, ACT.Copy).then_inc(S.list_high, 1)

            def silu(it, t):
                act.wait_ge(S.used, it * PIECES + (E_BUFS + 4 * t + 2))
                act.wait_ge(S.hid_done, it * E_TILES + (t + 1))
                nc.scalar.activation(k.e_silu[:, t % 2, :], k.ps[:, 2 * (t % 2), 0:E_N], ACT.Silu).then_inc(S.silu_ready, 1)

            def y_high(pieces, half):
                act.wait_ge(S.used, pieces + E_BUFS)
                nc.scalar.activation(k.ey_high[:, half * HALF:(half + 1) * HALF], k.ps[:, 4 + half, :], ACT.Copy,
                                     scale=k.list_weight[:, 0:1]).then_inc(S.y_high, 1)

            with act.Fori(0, n) as ps_:
                act.wait_ge(S.scattered, ps_ * 34 + 1)
                nc.scalar.activation(k.place_cols[:, :], k.slot_no[:, :], ACT.Copy, scale=0.0)
                nc.scalar.activation(k.list_weight[:, 0:1], k.slot_no[:, 0:1], ACT.Copy, scale=0.0).then_inc(S.pcleared, 1)
                list_high(ps_ * 9)
                act.wait_ge(S.pcleared, ps_ + 1)
                with act.Fori(0, EXPERTS) as e:
                    it = ps_ * EXPERTS + e
                    for p in range(E_BUFS):
                        split(it, p)
                    act.wait_ge(S.gathered, ps_ * 9 + e + 1)
                    y_high(it * PIECES, 1)
                    for p in range(PIECES):
                        if p + E_BUFS < PIECES:
                            split(it, p + E_BUFS)
                        if p < 2 * Y0 and p % 4 == 1:
                            silu(it, p // 4)
                        if p == 12:
                            act.wait_ge(S.pturned, it + 1)
                            nc.scalar.activation(k.place_cols[:, :], k.ps[:, 6, 0:256], ACT.Copy)
                            nc.scalar.activation(k.list_weight[:, 0:1], k.ps[:, 6, 256:257], ACT.Copy).then_inc(S.pcopied, 1)
                        if p - 1 in HIDDEN_TURNS:
                            g = HIDDEN_TURNS.index(p - 1)
                            m = min(4, FC - 4 * g)
                            act.wait_ge(S.hturned, it * HG + g + 1)
                            nc.scalar.activation(k.hid_h[:, 4 * g:4 * g + m, :],
                                                 k.ps[:, 7 - g % 2, 0:m * P].rearrange("p (f t) -> p f t", f=m), ACT.Copy).then_inc(S.hid_high, 1)
                        if p == 32:
                            list_high(ps_ * 9 + e + 1)
                        if p == 39:
                            act.wait_ge(S.pcopied, it + 1)
                            y_high(it * PIECES + 40, 0)
                y_high(ps_ * (EXPERTS * PIECES) + EXPERTS * PIECES, 1)

        @block.vector
        def _(dve):
            n = passes(dve)
            dve.nop().then_inc(S.hid_done, 2)
            dve.nop().then_inc(S.added, 1)
            dve.nop().then_inc(S.scattered, 1)
            dve.nop().then_inc(S.low_done, 2 * E_RING)

            def split(it, p):
                dve.wait_ge(S.high_done, it * PIECES + (p + 1))
                nc.vector.tensor_tensor(piece(k.w_low, p), raw(p), piece(k.w_high, p).bitcast(F32), ALU.subtract).then_inc(S.low_done, 1)

            def find(ps_, e):
                for i in range(2):
                    last = nc.vector.tensor_scalar(k.places[:, i, :], k.slot_no[:, bass.ds(ps_ * P, P)],
                                                   k.place[:, i, bass.ds(e, 1)], None, ALU.is_equal)
                last.then_inc(S.places_ready, 1)

            def take(m):
                dve.wait_ge(S.gathered, m + 1)
                for c in range(KD):
                    last = nc.vector.tensor_scalar(k.list_raw[:, c, :], k.ps[:, 4 + c // 4, (c % 4) * P:(c % 4 + 1) * P],
                                                   k.mod_scale[:, 1, c, 1:2], k.mod_cols[:, 3, c, 1:2], ALU.mult, ALU.add)
                last.then_inc(S.list_made, 1)

            def list_low(m):
                dve.wait_ge(S.list_high, m + 1)
                nc.vector.tensor_tensor(k.list_l, k.list_raw, k.list_h.bitcast(F32), ALU.subtract).then_inc(S.list_low, 1)

            def hidden(it, t):
                dve.wait_ge(S.used, it * PIECES + (E_BUFS + 4 * t + 4))
                dve.wait_ge(S.silu_ready, it * E_TILES + (t + 1))
                nc.vector.tensor_tensor(k.e_hid[:, t * E_N:(t + 1) * E_N], k.e_silu[:, t % 2, :],
                                        k.ps[:, 2 * (t % 2) + 1, 0:E_N], ALU.mult).then_inc(S.hid_done, 1)

            def y_low(count, half):
                dve.wait_ge(S.y_high, count)
                cols = slice(half * HALF, (half + 1) * HALF)
                nc.vector.scalar_tensor_tensor(out=k.ey_low[:, cols], in0=k.ps[:, 4 + half, :], scalar=k.list_weight[:, 0:1],
                                               in1=k.ey_high[:, cols].bitcast(F32), op0=ALU.mult, op1=ALU.subtract).then_inc(S.y_low, 1)

            def add(count, half):
                for i in range(2):
                    dve.wait_ge(S.scattered, count + i + 2)
                    part = k.acc[:, i, half * HALF:(half + 1) * HALF]
                    nc.vector.tensor_tensor(part, part, k.ps[:, 6 + i, :], ALU.add).then_inc(S.added, 1)

            with dve.Fori(0, n) as ps_:
                find(ps_, 0)
                take(ps_ * 9)
                list_low(ps_ * 9)
                with dve.Fori(0, EXPERTS) as e:
                    it = ps_ * EXPERTS + e
                    ys, adds = ps_ * 17 + 2 * e, ps_ * 34 + 4 * e
                    for p in range(E_BUFS):
                        split(it, p)
                    y_low(ys + 1, 1)
                    for p in range(PIECES):
                        if p + E_BUFS < PIECES:
                            split(it, p + E_BUFS)
                        if p < 2 * Y0 and p % 4 == 3:
                            hidden(it, p // 4)
                        if p == 4:
                            add(adds, 1)
                        if p == 13:
                            dve.wait_ge(S.pturned, it + 1)
                            find(ps_, e + 1)
                        if p == 22:
                            take(ps_ * 9 + e + 1)
                        if p - 1 in HIDDEN_TURNS:
                            g = HIDDEN_TURNS.index(p - 1)
                            m = min(4, FC - 4 * g)
                            dve.wait_ge(S.hid_high, it * HG + g + 1)
                            nc.vector.tensor_tensor(k.hid_l[:, 4 * g:4 * g + m, :],
                                                    k.ps[:, 7 - g % 2, 0:m * P].rearrange("p (f t) -> p f t", f=m),
                                                    k.hid_h[:, 4 * g:4 * g + m, :].bitcast(F32), ALU.subtract).then_inc(S.hid_low, 1)
                        if p == 33:
                            list_low(ps_ * 9 + e + 1)
                        if p == 40:
                            y_low(ys + 2, 0)
                        if p == 43:
                            add(adds + 2, 0)
                y_low(ps_ * 17 + 17, 1)
                add(ps_ * 34 + 32, 1)


def finish(k):
    nc = k.nc
    r = residual_sems(k, "out_res", None, None)
    stored = k.sem("stored")
    with nc.Block() as block:

        @block.gpsimd
        def _(pool):
            for i in range(2):
                pool.tensor_copy(k.tok[:, 2 + i, :], k.acc[:, i, :]).then_inc(r.copied_a, 1)

        @block.scalar
        def _(act):
            act.wait_ge(r.copied_a, 2)
            residual_scalar(k, act, r, (2, 3), False)

        @block.vector
        def _(dve):
            dve.wait_ge(r.copied_a, 2)
            residual_vector(k, dve, r, (2, 3), 1, False)

        @block.sync
        def _(sp):
            for i in range(2):
                sp.wait_ge(r.added, i + 1)
                sp.dma_start(k.out[0, i * P:(i + 1) * P, :], k.resid[:, 2 + i, :]).then_inc(stored, 16)
            sp.wait_ge(stored, 32)



def hybrid_mlstm_hgrn2_moe(nc, a, out, stages=99):
    with ExitStack() as stack:
        def sb(name, shape, dtype=F32):
            return stack.enter_context(nc.sbuf_tensor(name, shape, dtype))

        stage_sems = []

        def sem(name):
            stage_sems.append(nc.alloc_semaphore(name))
            return stage_sems[-1]

        k = Names()
        k.nc, k.a, k.out, k.sem = nc, a, out, sem
        resid_at = -(-nc.sbuf_base // 32) * 32
        k.resid = sb("resid", [P, NT, D])
        k.tok = sb("tok", [P, NT, D])
        k.gate = sb("gate", [P, 2, 2, D])
        k.ex = sb("ex", [P, 4096])[:, :]
        k.junk = sb("junk", [P, D])[:, :]
        k.passes = sb("passes", [P, 1], I32)
        k.ones, k.ident, k.before, k.after = (sb(n, [P, P]) for n in ("ones", "ident", "before", "after"))
        k.level_mask = sb("level_mask", [P, LEVELS, P], U8)
        k.gate_sel = sb("gate_sel", [32, 4, 16])
        k.slot_no = sb("slot_no", [P, 256])
        k.expert_no = sb("expert_no", [P, 2, EXPERTS])
        k.crows = k.junk[:, 0:P]
        k.vrows = k.junk[:, P:2 * P]
        k.vcol = sb("vcol", [P, 120])
        k.c_parts = sb("c_parts", [P, KD, 4], F32R)
        k.first_rows, k.pair_sum = sb("first_rows", [1, 4]), sb("pair_sum", [4, 2])
        k.lb_raw, k.lb_exp, k.lb_col, k.lb_rest = (sb(n, [P, 16]) for n in ("lb_raw", "lb_exp", "lb_col", "lb_rest"))
        k.gate_bias = sb("gate_bias", [16, 2])
        k.w_router = sb("w_router", [P, KD, EXPERTS])
        k.b_router = sb("b_router", [1, EXPERTS])
        k.mod_cols = sb("mod_cols", [P, N_MOD, KD, 2])
        k.mod_scale = sb("mod_scale", [P, 2, KD, 2])
        k.ssq, k.rms, k.rstd = (sb(n, [P, NT]) for n in ("ssq", "rms", "rstd"))
        k.eps = sb("eps", [P, 1])
        k.a_cols = sb("a_cols", [P, NT, 16])
        k.e_cols = sb("e_cols", [P, NT, 16])
        k.den = sb("den", [P, 2, NT])
        k.head_sum = sb("head_sum", [P, NT * HEADS])
        base = -(-nc.sbuf_base // 64) * 64

        def at(name, words, first, dtype=F32):
            return nc.alloc_sbuf_tensor_at(name, [P, words], dtype, offset=base + 4 * first)[:, :]

        chunked = lambda area: area.rearrange("p (c t) -> p c t", c=KD)
        k.u_area = at("u_area", KD * T, 0)
        k.u_cols = k.u_area.rearrange("p (c t) -> p c t", c=KD)
        k.u_high, k.u_low = chunked(at("u_high", KD * T, 0, F32R)), chunked(at("u_low", KD * T, KD * T, F32R))
        k.ring = at("ring", RING * SLOT, 2 * KD * T)
        big_words = 2 * KD * T + NT * HEADS * VST
        big_at = 2 * KD * T + RING * SLOT
        k.big = at("big", big_words, big_at)
        k.u_raw = chunked(k.big[:, KD * T:2 * KD * T])
        parts = W_BUFS * W_PIECE
        k.fh_high, k.fh_low = (at(n, F_GROUP * T, big_at + m * F_GROUP * T, F32R).rearrange("p (f t) -> p f t", f=F_GROUP)
                               for m, n in enumerate(("fh_high", "fh_low")))
        k.fw_high = at("fw_high", parts, big_at + 2 * F_GROUP * T, F32R)
        k.fw_low = at("fw_low", parts, big_at + 2 * F_GROUP * T + parts, F32R)
        k.qk = k.big[:, 0:KD * T].rearrange("p (c t) -> p c t", c=KD)
        k.o_cols = k.big[:, KD * T:2 * KD * T].rearrange("p (c t) -> p c t", c=KD)
        k.vaug = k.big[:, 2 * KD * T:big_words].rearrange("p (i h c) -> p i h c", i=NT, h=HEADS)
        k.sq = k.big[:, 2 * KD * T:2 * KD * T + NT * D].rearrange("p (i n) -> p i n", i=NT)
        k.f_rows = k.big[:, 0:4 * D].rearrange("p (i n) -> p i n", i=2)
        k.k_rows = k.big[:, 4 * D:8 * D].rearrange("p (i n) -> p i n", i=2)
        k.v_rows = k.big[:, 8 * D:12 * D].rearrange("p (i n) -> p i n", i=NT)
        k.f_cols = k.ex.rearrange("p (d c t) -> p d c t", d=2, c=KD)
        k.q_cols = k.tok[:, 0:2, :].rearrange("p a (c t) -> p (a c) t", t=LAT)
        k.g_cols = lambda c: k.gate[:, c // 4, 0, (c % 4) * LAT:(c % 4 + 1) * LAT]
        k.state = k.resid[:, 0:2, :].rearrange("p a (h c) -> p (a h) c", c=DV)
        k.q_fac = k.big[:, 0:4 * D].rearrange("p (d c t) -> p d c t", d=2, c=KD)
        k.k_fac = k.u_area.rearrange("p (d c t) -> p d c t", d=2, c=KD)
        k.joined = at("joined", KD * T, KD * T).rearrange("p (w c t) -> p w c t", w=2, c=KD)
        k.k_sum = k.tok[:, 2:4, :].rearrange("p a (c t) -> p (a c) t", t=LAT)
        k.pair_near = k.big[:, 4 * D:6 * D].rearrange("p (g i h t) -> p g i h t", g=2, i=2, h=4)
        k.pair_cross = k.big[:, 6 * D:8 * D].rearrange("p (g i h t) -> p g i h t", g=2, i=2, h=4)
        k.acc = k.tok[:, 0:2, :]
        k.e_silu = k.resid[:, 1, 0:2 * E_N].rearrange("p (b n) -> p b n", b=2)
        k.list_raw = k.ex[:, 2048:2048 + KD * P].rearrange("p (c t) -> p c t", c=KD)
        k.places = k.ex[:, 0:256].rearrange("p (i n) -> p i n", i=2)
        k.list_weight = k.ex[:, 512:513]
        k.route = k.ex[:, 1024:1024 + 16 * 16].rearrange("p (f i e) -> p f i e", f=16, i=2)
        k.comb = k.ex[:, 1536:1552].rearrange("p (i e) -> p i e", i=2)
        k.place = k.ex[:, 1552:1570].rearrange("p (i e) -> p i e", i=2)
        scan = k.tok[:, :, :].rearrange("p a n -> p (a n)")
        k.zeros = scan[:, 0:HALF]
        k.gates_f, k.gates_b = (k.ex[:, n * HALF:(n + 1) * HALF] for n in (6, 7))
        (k.scan_t, k.scan_z, k.scan_a, k.scan_a_rev, k.scan_e, k.scan_e_rev, k.scan_m,
         k.scan_m_rev) = (k.ex[:, n * HALF:(n + 1) * HALF] for n in range(8))
        k.ps = stack.enter_context(nc.psum_tensor("ps", [P, 8, HALF], F32))
        k.x_in = stack.enter_context(nc.semaphore("x_in"))
        k.stream = WeightStream(k.ring, k.ex[:, 4 * HALF:8 * HALF], [stack.enter_context(nc.semaphore(f"loaded{i}")) for i in range(RING)])
        plan_stream(k)

        words = 4 * NT * D
        resid_first, tok_first, junk_first = ((resid_at - base + n * words) // 4 for n in (0, 1, 4))
        spare = big_at + big_words
        m_parts = [at(f"m_part{n}", W_PIECE, first, F32R) for n, first in
                   enumerate((tok_first + HALF, tok_first + HALF + D, tok_first + HALF + 2 * D, spare))]
        h_parts = [at(f"h_part{n}", W_PIECE, first, F32R) for n, first in
                   enumerate((resid_first, resid_first + D, junk_first, spare))]
        k.out_parts = [at(f"out_part{n}", W_PIECE, (resid_at - base + 3 * words) // 4 + n * W_PIECE, F32R) for n in range(4)]
        k.m_high, k.m_low, k.h_high, k.h_low = m_parts[:2], m_parts[2:], h_parts[:2], h_parts[2:]
        area = {}

        def place_experts():
            first = 0
            for name, words, dtype in (("e_ring", E_RING * E_SLOT, F32), ("e_hid", FFN, F32),
                                       ("w_high", E_BUFS * E_PIECE, F32R), ("w_low", E_BUFS * E_PIECE, F32R),
                                       ("list_h", KD * P, F32R), ("list_l", KD * P, F32R),
                                       ("hid_h", FC * P, F32R), ("hid_l", FC * P, F32R),
                                       ("ey_high", D, F32R), ("ey_low", D, F32R)):
                area[name] = at(name, words, first, dtype)
                first += words
            k.ey_high, k.ey_low = area["ey_high"], area["ey_low"]
            k.place_cols = nc.alloc_sbuf_tensor_at("place_cols", [P, 2 * P], F32R, offset=resid_at)[:, :]
            k.e_ring, k.e_hid, k.w_high, k.w_low = (area[n] for n in ("e_ring", "e_hid", "w_high", "w_low"))
            k.list_h, k.list_l, k.hid_h, k.hid_l = (area[n].rearrange("p (c t) -> p c t", t=P) for n in ("list_h", "list_l", "hid_h", "hid_l"))

        order = [
            lambda: setup(k),
            lambda: modulation(k, 0),
            lambda: norm_in(k, "n0", 0, range(NT), u_cols=k.u_raw, arrived=(k.x_in, 32)),
            lambda: mlstm_in(k),
            lambda: mlstm_heads(k),
            lambda: mixer_out(k, "mo", "m_out", range(NT), 88, lambda h: k.o_cols[:, h, :], False),
            lambda: norm_in(k, "n1", 1, range(NT), u_cols=k.u_raw),
            lambda: feed_forward(k),
            lambda: modulation(k, 1),
            lambda: norm_in(k, "n2", 0, range(NT), True, u_cols=k.u_raw),
            lambda: hgrn_in(k),
            lambda: hgrn_state(k),
            lambda: hgrn_pairs(k),
            lambda: hgrn_values(k),
            lambda: mixer_out(k, "ho", "h_out", (2, 3), 96, k.g_cols, True),
            lambda: norm_in(k, "n3", 1, (2, 3)),
            lambda: routing(k),
            lambda: (place_experts(), experts(k)),
            lambda: finish(k),
        ]
        for n, stage in enumerate(order[:stages]):
            stage()
            if n == len(order) // 2:
                nc.clear_and_free_semaphores(list(stage_sems))
                stage_sems.clear()
                k.stream.release = {}
                nc.all_engine_barrier()


_INS = ['x', 'c', 'ctx', 'c_ctx', 'mod_w', 'mod_b', 'norm_g', 'm_w_in', 'm_b_gate', 'm_w_conv', 'm_g_head', 'm_w_out',
        'h_w_in', 'h_b_f', 'h_lb_raw', 'h_g_head', 'h_w_out', 'f_w_gu', 'f_w_down',
        'e_w_router', 'e_b_router', 'e_w_gu', 'e_w_down']


def kernel(**inputs):
    import numpy as _np
    import concourse.bacc as _bacc
    from concourse.bass_utils import run_bass_kernel_spmd as _run

    nc = _bacc.Bacc("TRN2", target_bir_lowering=False, num_devices=1)
    arrays, args = {}, {}
    for name in _INS:
        array = _np.ascontiguousarray(inputs[name])
        arrays[f"in_{name}_dram"] = array
        args[name] = nc.dram_tensor(f"in_{name}_dram", array.shape, mybir.dt.from_np(array.dtype), kind="ExternalInput").ap()
    out = nc.dram_tensor("out_0_dram", inputs["x"].shape, F32, kind="ExternalOutput").ap()
    hybrid_mlstm_hgrn2_moe(nc, args, out)
    r = _run(nc, [arrays], core_ids=[0])
    return r.results[0]["out_0_dram"]
```
